# Optimizing a Trainium2 kernel written in Bass

```python
import jax, jax.numpy as jnp
from jax import lax
import numpy as np
import math

D_MODEL = 1024
BATCH = 1
SEQ = 512
DEPTH = 2

HEAD_DIM = 64
N_TOK_HEADS = 12
N_KV_HEADS = 3
GQA_GROUP = N_TOK_HEADS // N_KV_HEADS
N_MEM_HEADS = 4
N_MEM = 256
Q_W = N_TOK_HEADS * HEAD_DIM
KV_W = N_KV_HEADS * HEAD_DIM
QM_W = N_MEM_HEADS * HEAD_DIM
IN_W = Q_W + 2 * KV_W + QM_W
MIX_WIDTH = Q_W + QM_W
D_FF = -(-8 * D_MODEL // (3 * 256)) * 256
N_MIXERS = 3
BLOCK = 128
A_RADIUS = 128
C_GROUPS = ((128, 1), (512, 4), (2048, 16))
ROPE_THETA = 500000.0
ROPE_DIMS = HEAD_DIM // 4
AXIAL_THETA = 10000.0
GRID_W = 64
EPS = 1e-6
N_A = (DEPTH + 2) // N_MIXERS
N_B = (DEPTH + 1) // N_MIXERS
ATTN_SCALE = HEAD_DIM ** -0.5


def rms_norm(x, g):
    xf = x.astype(jnp.float32)
    y = xf * lax.rsqrt(jnp.mean(xf * xf, axis=-1, keepdims=True) + EPS)
    return (y * g.astype(jnp.float32)).astype(x.dtype)

def rope_table(pos, n_dims, theta):
    inv = theta ** (-(jnp.arange(0, n_dims, 2, dtype=jnp.float32) / n_dims))
    ang = pos.astype(jnp.float32)[:, None] * inv[None, :]
    return jnp.cos(ang), jnp.sin(ang)

def apply_rotary(x, cos, sin):
    half = x.shape[-1] // 2
    xf = x.astype(jnp.float32)
    x1, x2 = xf[..., :half], xf[..., half:]
    c, s = cos[:, None, :], sin[:, None, :]
    return jnp.concatenate([x1 * c - x2 * s, x2 * c + x1 * s], axis=-1).astype(x.dtype)

def partial_rope(x, cos, sin):
    return jnp.concatenate([apply_rotary(x[..., :ROPE_DIMS], cos, sin), x[..., ROPE_DIMS:]], axis=-1)

def axial_rope(x, cos_r, sin_r, cos_c, sin_c):
    half = HEAD_DIM // 2
    return jnp.concatenate([apply_rotary(x[..., :half], cos_r, sin_r),
                            apply_rotary(x[..., half:], cos_c, sin_c)], axis=-1)

def banded_attention(q, k, v, radius, sink=None):
    B, L, KVH, G, HD = q.shape
    blk = radius
    nb = -(-L // blk)
    Lp = nb * blk
    pad = Lp - L
    qb = jnp.pad(q, [(0, 0), (0, pad), (0, 0), (0, 0), (0, 0)]).reshape(B, nb, blk, KVH, G, HD)

    def windows(t):
        tp = jnp.pad(t, [(0, 0), (blk, blk + pad), (0, 0), (0, 0)]).reshape(B, nb + 2, blk, KVH, HD)
        return jnp.concatenate([tp[:, :-2], tp[:, 1:-1], tp[:, 2:]], axis=2)

    kw, vw = windows(k), windows(v)
    qpos = jnp.arange(Lp).reshape(nb, blk)
    kpos = (jnp.arange(nb)[:, None] - 1) * blk + jnp.arange(3 * blk)[None, :]
    mask = ((jnp.abs(qpos[:, :, None] - kpos[:, None, :]) <= radius)
            & (kpos >= 0)[:, None, :] & (kpos < L)[:, None, :])
    s = jnp.einsum('bnqhgd,bnkhd->bnhgqk', qb, kw, preferred_element_type=jnp.float32) * ATTN_SCALE
    s = jnp.where(mask[None, :, None, None], s, -jnp.inf)
    m = jnp.max(s, axis=-1, keepdims=True)
    if sink is not None:
        sk = sink.astype(jnp.float32)[None, None, :, :, None, None]
        m = jnp.maximum(m, sk)
    p = jnp.exp(s - m)
    denom = jnp.sum(p, axis=-1)
    if sink is not None:
        denom = denom + jnp.exp(sk - m)[..., 0]
    o = jnp.einsum('bnhgqk,bnkhd->bnqhgd', p.astype(v.dtype), vw)
    den_t = jnp.transpose(denom, (0, 1, 4, 2, 3))
    o = (o / den_t[..., None]).astype(q.dtype).reshape(B, Lp, KVH, G, HD)[:, :L]
    lse = jnp.transpose(m[..., 0] + jnp.log(denom), (0, 1, 4, 2, 3)).reshape(B, Lp, KVH, G)[:, :L]
    return o, lse

def full_attention_blocks(q, k, v):
    B, S, KVH, G, HD = q.shape
    nb = S // BLOCK
    qb = jnp.moveaxis(q.reshape(B, nb, BLOCK, KVH, G, HD), 1, 0)

    def one_block(qblk):
        s = jnp.einsum('bqhgd,bkhd->bhgqk', qblk, k, preferred_element_type=jnp.float32) * ATTN_SCALE
        p = jax.nn.softmax(s, axis=-1)
        return jnp.einsum('bhgqk,bkhd->bqhgd', p.astype(v.dtype), v)

    o = lax.map(one_block, qb)
    return jnp.moveaxis(o, 0, 1).reshape(B, S, KVH, G, HD)

def mixer_a(q, k, v, sink, cos_p, sin_p):
    B, S = q.shape[:2]
    q = partial_rope(q, cos_p, sin_p).reshape(B, S, N_KV_HEADS, GQA_GROUP, HEAD_DIM)
    k = partial_rope(k, cos_p, sin_p)
    o, _ = banded_attention(q, k, v, A_RADIUS, sink.reshape(N_KV_HEADS, GQA_GROUP))
    return o.reshape(B, S, Q_W)

def mixer_b(q, k, v, qk_g, cos_r, sin_r, cos_c, sin_c):
    B, S = q.shape[:2]
    q = axial_rope(rms_norm(q, qk_g[0]), cos_r, sin_r, cos_c, sin_c)
    k = axial_rope(rms_norm(k, qk_g[1]), cos_r, sin_r, cos_c, sin_c)
    o = full_attention_blocks(q.reshape(B, S, N_KV_HEADS, GQA_GROUP, HEAD_DIM), k, v)
    return o.reshape(B, S, Q_W)

def dilated_group(q, k, v, dil, radius):
    B, S = q.shape[:2]
    L = S // dil

    def split(t):
        t = jnp.moveaxis(t.reshape((B, L, dil) + t.shape[2:]), 2, 1)
        return t.reshape((B * dil, L) + t.shape[3:])

    def merge(t):
        t = jnp.moveaxis(t.reshape((B, dil, L) + t.shape[2:]), 1, 2)
        return t.reshape((B, S) + t.shape[3:])

    o, lse = banded_attention(split(q)[:, :, None], split(k)[:, :, None], split(v)[:, :, None], radius)
    return merge(o[:, :, 0]), merge(lse[:, :, 0])

def mixer_c(q, k, v, cos_p, sin_p):
    B, S = q.shape[:2]
    q = partial_rope(q, cos_p, sin_p)
    k = partial_rope(k, cos_p, sin_p)
    outs, lses = [], []
    for g, (window, dil) in enumerate(C_GROUPS):
        o, l = dilated_group(q[:, :, g * GQA_GROUP:(g + 1) * GQA_GROUP], k[:, :, g], v[:, :, g],
                             dil, window // (2 * dil))
        outs.append(o)
        lses.append(l)
    alpha = jax.nn.softmax(jnp.stack(lses, axis=2), axis=2)
    o = jnp.stack(outs, axis=2) * alpha[..., None].astype(q.dtype)
    return o.reshape(B, S, Q_W)

def memory_attention(qm, km, vm):
    s = jnp.einsum('bshd,bmhd->bhsm', qm, km, preferred_element_type=jnp.float32) * ATTN_SCALE
    p = jax.nn.softmax(s, axis=-1)
    o = jnp.einsum('bhsm,bmhd->bshd', p.astype(vm.dtype), vm)
    return o.reshape(qm.shape[0], qm.shape[1], QM_W)

def first_inputs(seed: int = 0) -> dict:
    key = jax.random.key(seed)
    ks = jax.random.split(key, 14)
    nrm = jax.random.normal
    f32 = jnp.float32
    return {
        'x': nrm(ks[0], (BATCH, SEQ, D_MODEL), f32),
        'mem': nrm(ks[1], (BATCH, N_MEM, D_MODEL), f32),
        'mem_norm_g': 1.0 + 0.02 * nrm(ks[2], (D_MODEL,), f32),
        'w_in': nrm(ks[3], (DEPTH, D_MODEL, IN_W), f32) * D_MODEL ** -0.5,
        'w_mem_kv': nrm(ks[4], (DEPTH, D_MODEL, 2 * QM_W), f32) * D_MODEL ** -0.5,
        'w_o': nrm(ks[5], (DEPTH, MIX_WIDTH, D_MODEL), f32) * MIX_WIDTH ** -0.5,
        'g_mix_pre': 1.0 + 0.02 * nrm(ks[6], (DEPTH, D_MODEL), f32),
        'g_mix_post': 1.0 + 0.02 * nrm(ks[7], (DEPTH, D_MODEL), f32),
        'attn_sink': 0.5 * nrm(ks[8], (N_A, N_TOK_HEADS), f32),
        'qk_norm_g': 1.0 + 0.02 * nrm(ks[9], (N_B, 2, HEAD_DIM), f32),
        'w_gate_up': nrm(ks[10], (DEPTH, D_MODEL, 2 * D_FF), f32) * D_MODEL ** -0.5,
        'w_down': nrm(ks[11], (DEPTH, D_FF, D_MODEL), f32) * D_FF ** -0.5,
        'g_ffn_pre': 1.0 + 0.02 * nrm(ks[12], (DEPTH, D_MODEL), f32),
        'g_ffn_post': 1.0 + 0.02 * nrm(ks[13], (DEPTH, D_MODEL), f32),
    }

def first_block(x, mem, mem_norm_g, w_in, w_mem_kv, w_o, g_mix_pre, g_mix_post, attn_sink,
              qk_norm_g, w_gate_up, w_down, g_ffn_pre, g_ffn_post):
    B, S, _ = x.shape
    rows = S // GRID_W
    pos = jnp.arange(S, dtype=jnp.int32)
    row_ids = jnp.repeat(jnp.arange(rows, dtype=jnp.int32), GRID_W)
    col_ids = jnp.tile(jnp.arange(GRID_W, dtype=jnp.int32), rows)
    cos_p, sin_p = rope_table(pos, ROPE_DIMS, ROPE_THETA)
    cos_r, sin_r = rope_table(row_ids, HEAD_DIM // 2, AXIAL_THETA)
    cos_c, sin_c = rope_table(col_ids, HEAD_DIM // 2, AXIAL_THETA)
    mem_n = rms_norm(mem, mem_norm_g)

    for i in range(DEPTH):
        h = rms_norm(x, g_mix_pre[i])
        proj = h @ w_in[i]
        q = proj[..., :Q_W].reshape(B, S, N_TOK_HEADS, HEAD_DIM)
        k = proj[..., Q_W:Q_W + KV_W].reshape(B, S, N_KV_HEADS, HEAD_DIM)
        v = proj[..., Q_W + KV_W:Q_W + 2 * KV_W].reshape(B, S, N_KV_HEADS, HEAD_DIM)
        qm = proj[..., Q_W + 2 * KV_W:].reshape(B, S, N_MEM_HEADS, HEAD_DIM)
        kind = i % N_MIXERS
        if kind == 0:
            tok = mixer_a(q, k, v, attn_sink[i // N_MIXERS], cos_p, sin_p)
        elif kind == 1:
            tok = mixer_b(q, k, v, qk_norm_g[i // N_MIXERS], cos_r, sin_r, cos_c, sin_c)
        else:
            tok = mixer_c(q, k, v, cos_p, sin_p)
        mkv = mem_n @ w_mem_kv[i]
        km = mkv[..., :QM_W].reshape(B, N_MEM, N_MEM_HEADS, HEAD_DIM)
        vm = mkv[..., QM_W:].reshape(B, N_MEM, N_MEM_HEADS, HEAD_DIM)
        mo = memory_attention(qm, km, vm)
        o = jnp.concatenate([tok, mo], axis=-1) @ w_o[i]
        x = x + rms_norm(o, g_mix_post[i])

        h = rms_norm(x, g_ffn_pre[i])
        gu = h @ w_gate_up[i]
        f = (jax.nn.silu(gu[..., :D_FF]) * gu[..., D_FF:]) @ w_down[i]
        x = x + rms_norm(f, g_ffn_post[i])
    return x


DEPTH_2 = 1

RW_HEADS = 8
RW_HEAD_DIM = 64
RW_DIM = RW_HEADS * RW_HEAD_DIM
W_LORA = 64
A_LORA = 64
G_LORA = 128
GN_EPS = 64e-5
MLA_HEADS = 8
QK_NOPE = 64
QK_ROPE = 32
V_HEAD = 64
Q_LORA = 384
KV_LORA = 256
ROPE_THETA_2 = 10000.0
Q_BLOCK = 128
N_GROUPS = 4
EXPERTS_PER_GROUP = 8
N_EXPERTS = N_GROUPS * EXPERTS_PER_GROUP
TOP_K = 2
D_EXPERT = 256
EXPERT_BLOCK = 256
NORM_EPS = 1e-6

RW_COLS = 3 * RW_DIM + W_LORA + A_LORA + G_LORA
MLA_COLS = Q_LORA + KV_LORA + QK_ROPE
GATE_COLS = 2 * D_MODEL
IN_COLS = RW_COLS + MLA_COLS + GATE_COLS


def rmsnorm(x, g):
    xf = x.astype(jnp.float32)
    y = xf * lax.rsqrt(jnp.mean(xf * xf, axis=-1, keepdims=True) + NORM_EPS)
    return (y * g.astype(jnp.float32)).astype(x.dtype)

def rope(t, cos, sin):
    t1, t2 = jnp.split(t, 2, axis=-1)
    return jnp.concatenate([t1 * cos - t2 * sin, t2 * cos + t1 * sin], axis=-1)

def rwkv7_mix(z_in, mu, w0, w_up, a0, a_up, g_up, k_k, k_a, r_k, gn_w, gn_b):
    B, S, _ = z_in.shape
    dt = z_in.dtype
    prev = jnp.pad(z_in, ((0, 0), (1, 0), (0, 0)))[:, :-1]
    z = z_in + (prev - z_in) * mu
    r, k, v, wd, ad, gd = jnp.split(
        z, [RW_DIM, 2 * RW_DIM, 3 * RW_DIM, 3 * RW_DIM + W_LORA, 3 * RW_DIM + W_LORA + A_LORA], axis=-1)
    w_log = -jax.nn.softplus(-(w0 + jnp.tanh(wd) @ w_up).astype(jnp.float32)) - 0.5
    decay = jnp.exp(-jnp.exp(w_log))
    a = jax.nn.sigmoid(a0 + ad @ a_up)
    g = jax.nn.sigmoid(gd) @ g_up

    def heads(t):
        return t.reshape(B, S, RW_HEADS, RW_HEAD_DIM).astype(jnp.float32)

    kk = heads(k * k_k)
    kk = kk / jnp.maximum(jnp.sqrt(jnp.sum(kk * kk, axis=-1, keepdims=True)), 1e-12)
    k = k * (1.0 + (a - 1.0) * k_a)
    r_h, k_h, v_h, a_h, w_h = heads(r), heads(k), heads(v), heads(a), heads(decay)

    def step(state, inp):
        r_t, w_t, k_t, v_t, kk_t, a_t = inp
        sa = jnp.einsum('bhvk,bhk->bhv', state, -kk_t)
        state = (state * w_t[:, :, None, :]
                 + sa[..., None] * (kk_t * a_t)[:, :, None, :]
                 + v_t[..., None] * k_t[:, :, None, :])
        return state, jnp.einsum('bhvk,bhk->bhv', state, r_t)

    xs = tuple(jnp.moveaxis(t, 1, 0) for t in (r_h, w_h, k_h, v_h, kk, a_h))
    s0 = jnp.zeros((B, RW_HEADS, RW_HEAD_DIM, RW_HEAD_DIM), jnp.float32)
    _, ys = lax.scan(step, s0, xs)
    y = jnp.moveaxis(ys, 0, 1)
    mean = jnp.mean(y, axis=-1, keepdims=True)
    var = jnp.mean(jnp.square(y - mean), axis=-1, keepdims=True)
    y = ((y - mean) * lax.rsqrt(var + GN_EPS)).reshape(B, S, RW_DIM)
    y = y * gn_w.astype(jnp.float32) + gn_b.astype(jnp.float32)
    bonus = jnp.sum(r_h * k_h * r_k.astype(jnp.float32), axis=-1, keepdims=True) * v_h
    y = y + bonus.reshape(B, S, RW_DIM)
    return (y * g.astype(jnp.float32)).astype(dt)

def mla_mix(q_d, kv_d, kr_raw, cos, sin, g_qa, w_q_up, g_kva, w_kv_up):
    B, S, _ = q_d.shape
    q = (rmsnorm(q_d, g_qa) @ w_q_up).reshape(B, S, MLA_HEADS, QK_NOPE + QK_ROPE)
    q_nope, q_rope = q[..., :QK_NOPE], q[..., QK_NOPE:]
    kv = (rmsnorm(kv_d, g_kva) @ w_kv_up).reshape(B, S, MLA_HEADS, QK_NOPE + V_HEAD)
    k_nope, v = kv[..., :QK_NOPE], kv[..., QK_NOPE:]
    q_rope = rope(q_rope, cos[:, :, None, :], sin[:, :, None, :])
    k_rope = rope(kr_raw, cos, sin)
    scale = 1.0 / math.sqrt(QK_NOPE + QK_ROPE)
    outs = []
    for start in range(0, S, Q_BLOCK):
        end = min(start + Q_BLOCK, S)
        s = (jnp.einsum('bqhd,bkhd->bhqk', q_nope[:, start:end], k_nope[:, :end])
             + jnp.einsum('bqhr,bkr->bhqk', q_rope[:, start:end], k_rope[:, :end]))
        s = s.astype(jnp.float32) * scale
        causal = jnp.arange(end)[None, :] <= jnp.arange(start, end)[:, None]
        p = jax.nn.softmax(jnp.where(causal, s, -jnp.inf), axis=-1).astype(v.dtype)
        outs.append(jnp.einsum('bhqk,bkhd->bqhd', p, v[:, :end]))
    return jnp.concatenate(outs, axis=1).reshape(B, S, MLA_HEADS * V_HEAD)

def hier_moe(h, w_group, b_group, w_router, b_router, w_gu, w_down):
    B, S, D = h.shape
    N = B * S
    hf = h.reshape(N, D)
    p_group = jax.nn.softmax((hf @ w_group).astype(jnp.float32) + b_group.astype(jnp.float32), axis=-1)
    g_sel = jnp.argmax(p_group, axis=-1)
    gate_g = jnp.take_along_axis(p_group, g_sel[:, None], axis=-1)
    fine = ((hf @ w_router).astype(jnp.float32) + b_router.astype(jnp.float32)
            ).reshape(N, N_GROUPS, EXPERTS_PER_GROUP)
    fine_sel = jnp.take_along_axis(fine, g_sel[:, None, None], axis=1)[:, 0]
    top_v, top_i = lax.top_k(fine_sel, TOP_K)
    gate = jax.nn.softmax(top_v, axis=-1) * gate_g
    expert = g_sel[:, None] * EXPERTS_PER_GROUP + top_i

    A = N * TOP_K
    e_flat = expert.reshape(A)
    t_flat = jnp.arange(A) // TOP_K
    w_flat = gate.reshape(A)
    order = jnp.argsort(e_flat)
    e_s, t_s, w_s = e_flat[order], t_flat[order], w_flat[order]
    counts = jnp.bincount(e_flat, length=N_EXPERTS)
    starts = jnp.cumsum(counts) - counts
    padded = (counts + EXPERT_BLOCK - 1) // EXPERT_BLOCK * EXPERT_BLOCK
    pad_end = jnp.cumsum(padded)
    pad_start = pad_end - padded
    dest = pad_start[e_s] + (jnp.arange(A) - starts[e_s])
    n_blocks = -(-A // EXPERT_BLOCK) + N_EXPERTS
    P = n_blocks * EXPERT_BLOCK
    tok_buf = jnp.full((P,), N, jnp.int32).at[dest].set(t_s.astype(jnp.int32))
    w_buf = jnp.zeros((P,), jnp.float32).at[dest].set(w_s)
    blk_expert = jnp.minimum(
        jnp.searchsorted(pad_end, jnp.arange(n_blocks) * EXPERT_BLOCK, side='right'), N_EXPERTS - 1)
    x_pad = jnp.concatenate([hf, jnp.zeros((1, D), hf.dtype)], axis=0)
    xb = x_pad[tok_buf].reshape(n_blocks, EXPERT_BLOCK, D)

    def expert_block(args):
        xblk, e = args
        gt, up = jnp.split(xblk @ w_gu[e], 2, axis=-1)
        return (jax.nn.silu(gt) * up) @ w_down[e]

    yb = lax.map(expert_block, (xb, blk_expert)).reshape(P, D)
    out = jnp.zeros((N + 1, D), h.dtype).at[tok_buf].add(yb * w_buf[:, None].astype(h.dtype))
    return out[:N].reshape(B, S, D)

def second_inputs(seed: int = 0) -> dict:
    key = jax.random.key(seed)
    ks = jax.random.split(key, 32)
    f32 = jnp.float32

    def nrm(k, shape, scale):
        return jax.random.normal(k, shape, f32) * scale

    L, D = DEPTH_2, D_MODEL
    x = jax.random.normal(ks[0], (BATCH, SEQ, D), f32)
    offsets = jax.random.randint(ks[1], (BATCH, 1), 0, 1024, dtype=jnp.int32)
    positions = offsets + jnp.arange(SEQ, dtype=jnp.int32)[None, :]
    return {
        "x": x,
        "positions": positions,
        "mix_norm_g": 1.0 + nrm(ks[2], (L, D), 0.02),
        "w_in": nrm(ks[3], (L, D, IN_COLS), D ** -0.5),
        "rw_mu": jax.random.uniform(ks[4], (L, RW_COLS), f32),
        "rw_w0": jax.random.uniform(ks[5], (L, RW_DIM), f32, -6.0, -1.0),
        "rw_w_up": nrm(ks[6], (L, W_LORA, RW_DIM), 0.1 * W_LORA ** -0.5),
        "rw_a0": nrm(ks[7], (L, RW_DIM), 0.1),
        "rw_a_up": nrm(ks[8], (L, A_LORA, RW_DIM), 0.5 * A_LORA ** -0.5),
        "rw_g_up": nrm(ks[9], (L, G_LORA, RW_DIM), G_LORA ** -0.5),
        "rw_k_k": 0.85 + nrm(ks[10], (L, RW_DIM), 0.02),
        "rw_k_a": 1.0 + nrm(ks[11], (L, RW_DIM), 0.02),
        "rw_r_k": nrm(ks[12], (L, RW_HEADS, RW_HEAD_DIM), 0.1),
        "rw_gn_w": 1.0 + nrm(ks[13], (L, RW_DIM), 0.02),
        "rw_gn_b": nrm(ks[14], (L, RW_DIM), 0.02),
        "mla_g_qa": 1.0 + nrm(ks[15], (L, Q_LORA), 0.02),
        "mla_w_q_up": nrm(ks[16], (L, Q_LORA, MLA_HEADS * (QK_NOPE + QK_ROPE)), Q_LORA ** -0.5),
        "mla_g_kva": 1.0 + nrm(ks[17], (L, KV_LORA), 0.02),
        "mla_w_kv_up": nrm(ks[18], (L, KV_LORA, MLA_HEADS * (QK_NOPE + V_HEAD)), KV_LORA ** -0.5),
        "w_branch_rw": nrm(ks[19], (L, RW_DIM, D), RW_DIM ** -0.5),
        "w_branch_mla": nrm(ks[20], (L, MLA_HEADS * V_HEAD, D), (MLA_HEADS * V_HEAD) ** -0.5),
        "w_out": nrm(ks[21], (L, D, D), D ** -0.5),
        "ffn_norm_g": 1.0 + nrm(ks[22], (L, D), 0.02),
        "moe_w_group": nrm(ks[23], (L, D, N_GROUPS), D ** -0.5),
        "moe_b_group": nrm(ks[24], (L, N_GROUPS), 0.01),
        "moe_w_router": nrm(ks[25], (L, D, N_EXPERTS), D ** -0.5),
        "moe_b_router": nrm(ks[26], (L, N_EXPERTS), 0.01),
        "moe_w_gu": nrm(ks[27], (L, N_EXPERTS, D, 2 * D_EXPERT), D ** -0.5),
        "moe_w_down": nrm(ks[28], (L, N_EXPERTS, D_EXPERT, D), D_EXPERT ** -0.5),
        "final_norm_g": 1.0 + nrm(ks[29], (D,), 0.02),
    }

def second_block(x, positions, mix_norm_g, w_in, rw_mu, rw_w0, rw_w_up, rw_a0, rw_a_up, rw_g_up,
              rw_k_k, rw_k_a, rw_r_k, rw_gn_w, rw_gn_b, mla_g_qa, mla_w_q_up, mla_g_kva, mla_w_kv_up,
              w_branch_rw, w_branch_mla, w_out, ffn_norm_g, moe_w_group, moe_b_group, moe_w_router,
              moe_b_router, moe_w_gu, moe_w_down, final_norm_g):
    inv_freq = ROPE_THETA_2 ** (-jnp.arange(0, QK_ROPE, 2, dtype=jnp.float32) / QK_ROPE)
    ang = positions.astype(jnp.float32)[..., None] * inv_freq
    cos, sin = jnp.cos(ang).astype(x.dtype), jnp.sin(ang).astype(x.dtype)

    for l in range(DEPTH_2):
        h = rmsnorm(x, mix_norm_g[l])
        cols = h @ w_in[l]
        c_rw = cols[..., :RW_COLS]
        c_q = cols[..., RW_COLS:RW_COLS + Q_LORA]
        c_kv = cols[..., RW_COLS + Q_LORA:RW_COLS + Q_LORA + KV_LORA]
        c_kr = cols[..., RW_COLS + Q_LORA + KV_LORA:RW_COLS + MLA_COLS]
        gate_rw = jax.nn.sigmoid(cols[..., RW_COLS + MLA_COLS:RW_COLS + MLA_COLS + D_MODEL])
        gate_mla = jax.nn.sigmoid(cols[..., RW_COLS + MLA_COLS + D_MODEL:])

        y_rw = rwkv7_mix(c_rw, rw_mu[l], rw_w0[l], rw_w_up[l], rw_a0[l], rw_a_up[l], rw_g_up[l],
                         rw_k_k[l], rw_k_a[l], rw_r_k[l], rw_gn_w[l], rw_gn_b[l])
        y_mla = mla_mix(c_q, c_kv, c_kr, cos, sin, mla_g_qa[l], mla_w_q_up[l], mla_g_kva[l], mla_w_kv_up[l])
        merged = gate_rw * (y_rw @ w_branch_rw[l]) + gate_mla * (y_mla @ w_branch_mla[l])
        x = x + merged @ w_out[l]

        h2 = rmsnorm(x, ffn_norm_g[l])
        x = x + hier_moe(h2, moe_w_group[l], moe_b_group[l], moe_w_router[l], moe_b_router[l],
                         moe_w_gu[l], moe_w_down[l])

    return rmsnorm(x, final_norm_g)


def setup_inputs(seed=0):
    out = dict(first_inputs(seed))
    for name, value in second_inputs(seed + 1).items():
        if name != "x":
            out[name + "_2"] = value
    return out


def reference(
    x, mem, mem_norm_g, w_in, w_mem_kv, w_o, g_mix_pre, g_mix_post, attn_sink, qk_norm_g,
    w_gate_up, w_down, g_ffn_pre, g_ffn_post, positions_2, mix_norm_g_2, w_in_2, rw_mu_2,
    rw_w0_2, rw_w_up_2, rw_a0_2, rw_a_up_2, rw_g_up_2, rw_k_k_2, rw_k_a_2, rw_r_k_2, rw_gn_w_2,
    rw_gn_b_2, mla_g_qa_2, mla_w_q_up_2, mla_g_kva_2, mla_w_kv_up_2, w_branch_rw_2,
    w_branch_mla_2, w_out_2, ffn_norm_g_2, moe_w_group_2, moe_b_group_2, moe_w_router_2,
    moe_b_router_2, moe_w_gu_2, moe_w_down_2, final_norm_g_2,
):
    x = first_block(
        x, mem, mem_norm_g, w_in, w_mem_kv, w_o, g_mix_pre, g_mix_post, attn_sink, qk_norm_g,
        w_gate_up, w_down, g_ffn_pre, g_ffn_post,
    )
    return second_block(
        x, positions_2, mix_norm_g_2, w_in_2, rw_mu_2, rw_w0_2, rw_w_up_2, rw_a0_2, rw_a_up_2,
        rw_g_up_2, rw_k_k_2, rw_k_a_2, rw_r_k_2, rw_gn_w_2, rw_gn_b_2, mla_g_qa_2, mla_w_q_up_2,
        mla_g_kva_2, mla_w_kv_up_2, w_branch_rw_2, w_branch_mla_2, w_out_2, ffn_norm_g_2,
        moe_w_group_2, moe_b_group_2, moe_w_router_2, moe_b_router_2, moe_w_gu_2, moe_w_down_2,
        final_norm_g_2,
    )


_drawn_inputs = setup_inputs


def setup_inputs(seed=0):
    import zlib

    import numpy as np

    out = dict(_drawn_inputs(seed))
    spreads = {}
    factors = {'mem_norm_g': 2.865,
     'attn_sink': 8.0,
     'qk_norm_g': 7.762,
     'g_ffn_post': 2.87,
     'mix_norm_g_2': 5.446,
     'rw_w_up_2': 27.824,
     'rw_a0_2': 5.454,
     'rw_k_k_2': 24.824,
     'rw_k_a_2': 3.383,
     'rw_gn_w_2': 46.59,
     'rw_gn_b_2': 55.077,
     'mla_g_qa_2': 8.0,
     'mla_g_kva_2': 7.623,
     'ffn_norm_g_2': 14.521,
     'moe_b_group_2': 38.606,
     'moe_b_router_2': 44.701,
     'final_norm_g_2': 7.788}
    for name, (base, spread) in spreads.items():
        noise = np.random.default_rng([zlib.crc32(name.encode()), seed]).standard_normal(out[name].shape)
        drawn = base * np.exp(spread * noise) if base else spread * noise
        out[name] = __import__('jax').numpy.asarray(drawn.astype(out[name].dtype))
    for name, factor in factors.items():
        out[name] = (out[name] * factor).astype(out[name].dtype)
    return out
```

```python
from contextlib import ExitStack

import numpy as np
import concourse.bass as bass
from concourse import mybir

F32 = mybir.dt.float32
I32 = mybir.dt.int32
U32 = mybir.dt.uint32
ALU = mybir.AluOpType
ACT = mybir.ActivationFunctionType
AX = mybir.AxisListType.X

P = 128
NT = 4
S = 512
D = 1024
NB = 39
SLOT = 4096
NEG = -1.0e30
SCALE = 64 ** -0.5
MSCALE = 1.0 / np.sqrt(96.0)

CONST = {}


def const_table():
    parts, at = [], [0]

    def put(name, a):
        a = np.asarray(a, np.float32)
        if a.ndim == 1:
            a = np.broadcast_to(a[None, :], (P, a.shape[0]))
        a = a.reshape(P, -1)
        CONST[name] = (at[0], at[0] + a.shape[1])
        at[0] += a.shape[1]
        parts.append(a)

    p = np.arange(P)
    s, t = p[:, None], p[None, :]
    put("ident", np.eye(P))
    put("bones", (s // 64 == t // 64))
    put("bmean", (s // 64 == t // 64) / 64.0)
    put("ident64", (s % 64 == np.arange(64)[None, :]))
    put("ones", np.ones((P, P)))
    put("triu", s < t)
    band = np.zeros((P, 384), np.float32)
    band[:, 0:128] = np.where(t >= s, 0.0, NEG)
    band[:, 256:384] = np.where(t <= s, 0.0, NEG)
    put("band", band)
    causal = np.zeros((P, 512), np.float32)
    causal[:, 384:] = np.where(t <= s, 0.0, NEG)
    put("causal", causal)
    same = s // 64 == t // 64
    strict, incl = same & (t > s), same & (t >= s)
    put("mgram", np.concatenate([strict, incl, strict, incl], 1))
    up = lambda n: (s // (2 * n) == t // (2 * n)) & (s % (2 * n) < n) & (t % (2 * n) >= n)
    put("low1", up(1).T)
    for n in (1, 2, 4, 8, 16, 32):
        put(f"up{n}", up(n))
    tok = np.arange(S).reshape(NT, P).T

    def angles(pos, dims, theta):
        inv = (theta ** (-(np.arange(0, dims, 2, dtype=np.float32) / np.float32(dims)))).astype(np.float32)
        return pos.astype(np.float32)[..., None] * inv

    a = angles(tok, 16, 500000.0)
    put("cosp", np.cos(a))
    put("sinp", np.sin(a))
    a = np.stack([angles(tok // 64, 32, 10000.0), angles(tok % 64, 32, 10000.0)], 2)
    put("cosx", np.cos(a))
    put("sinx", np.sin(a))
    put("invf", (np.float32(10000.0) ** (-np.arange(0, 32, 2, dtype=np.float32) / np.float32(32))).astype(np.float32))
    put("iota", np.arange(128))
    put("tokid", tok)
    put("keep", np.arange(S) % 64 != 0)
    return np.concatenate(parts, 1)


const_table()
NCONST = max(b for _, b in CONST.values())

GROWS = [("mem_norm_g", 0, 8), ("g_mix_pre", 0, 8), ("g_mix_pre", 1, 8), ("g_ffn_pre", 0, 8), ("g_ffn_pre", 1, 8),
         ("mix_norm_g_2", 0, 8), ("ffn_norm_g_2", 0, 8), ("rw_mu_2", 0, 14), ("rw_w0_2", 0, 4), ("rw_a0_2", 0, 4),
         ("rw_k_k_2", 0, 4), ("rw_k_a_2", 0, 4), ("rw_r_k_2", 0, 4), ("rw_gn_w_2", 0, 4), ("rw_gn_b_2", 0, 4),
         ("mla_g_qa_2", 0, 3), ("mla_g_kva_2", 0, 2)]


class Lane:

    def __init__(self, sem, chain):
        self.sem, self.chain, self.n, self.items, self.seen = sem, chain, 0, [], {}

    def wait(self, *toks):
        for t in toks:
            if t is None:
                continue
            if isinstance(t, list):
                self.wait(*t)
                continue
            sem, val = t
            if self.seen.get(sem.num, 0) < val:
                self.seen[sem.num] = val
                self.items.append(lambda e, sem=sem, val=val: e.wait_ge(sem, val))

    def do(self, fn, *toks):
        self.wait(*toks)
        if self.chain and self.n:
            self.wait((self.sem, self.n))
        self.n += 1
        self.items.append(lambda e: fn(e).then_inc(self.sem, 1))
        return (self.sem, self.n)

    def free(self, fn, *toks):
        self.wait(*toks)
        self.n += 1
        self.items.append(lambda e: fn(e).then_inc(self.sem, 1))
        return (self.sem, self.n)

    def quiet(self, fn, *toks):
        self.wait(*toks)
        self.items.append(lambda e: fn(e))

    def last(self):
        return (self.sem, self.n) if self.n else None

    def play(self, e):
        for f in self.items:
            f(e)


def build(nc, I, out, hn_scr, y_scr, consts, dbg=None, stop=None):
    with ExitStack() as ctx:
        sem = lambda n: ctx.enter_context(nc.semaphore(n))
        pe = Lane(sem("s_pe"), False)
        V = Lane(sem("s_dve"), True)
        A = Lane(sem("s_act"), True)
        G = Lane(sem("s_pool"), True)
        SP = Lane(sem("s_sp"), False)
        stores = []

        class Dma:

            def __init__(self, name):
                self.sem, self.n = sem(name), 0

            def start(self, lane, out_, in_, *toks, **kw):
                self.n += 16
                lane.wait(*toks)
                lane.items.append(lambda e: e.dma_start(out_, in_, **kw).then_inc(self.sem, 16))
                return (self.sem, self.n)

        AR_N = 53200
        arena = ctx.enter_context(nc.sbuf_tensor("arena", [P, AR_N], F32))
        banks = [ctx.enter_context(nc.psum_tensor(f"ps{i}", [P, 512], F32)) for i in range(8)]
        top = [0]

        def col(n):
            a = top[0]
            top[0] += n
            assert top[0] <= AR_N, top[0]
            return arena[:, a:a + n]

        X = col(4096).rearrange("p (i d) -> p i d", i=NT)
        HT = col(4096).rearrange("p (k t) -> p k t", k=8)
        RINGC = col(3 * SLOT)
        C = col(NCONST)
        k_ = lambda n: C[:, CONST[n][0]:CONST[n][1]]
        GC = col(103)
        goff, o_ = {}, 0
        for name, l, n in GROWS:
            goff[(name, l)] = o_
            o_ += n
        gcol = lambda name, l=0: GC[:, goff[(name, l)]:]
        st = col(900)
        stp = [0]

        def small(n):
            a = stp[0]
            stp[0] += n
            assert stp[0] <= 900
            return st[:, a:a + n]

        base = top[0]
        ident = k_("ident")

        class Banks:

            free_after = [None] * 8

            def __init__(self, ids):
                self.ids, self.at = list(ids), 0

            def take(self):
                b = self.ids[self.at % len(self.ids)]
                self.at += 1
                w = Banks.free_after[b]
                assert w != "held", b
                Banks.free_after[b] = "held"
                return b, banks[b], w

        def give(b, *toks):
            Banks.free_after[b] = list(toks)

        allb = Banks(range(8))

        def mm(o, l, r, start, stop_, *toks, inc=None):
            f = lambda e: e.matmul(o, l, r, start=start, stop=stop_, skip_group_check=True)
            return (pe.do if (stop_ if inc is None else inc) else pe.quiet)(f, *toks)

        def tr(o, i, *toks, inc=True):
            n = i.shape[0]
            f = lambda e: e.transpose(o, i, ident[0:n, 0:n])
            return (pe.do if inc else pe.quiet)(f, *toks)

        ring_sem = [Dma(f"s_ring{i}") for i in range(3)]
        jobs = []

        def job(*parts):
            jobs.append(parts)

        def w3(ap, k0, k1, c0, c1):
            return ap[k0 * P:k1 * P, c0:c1].rearrange("(k p) n -> p k n", p=P)

        def slot_w(n, off=0, k=8):
            return lambda s: s[:, off:off + k * n].rearrange("p (k n) -> p k n", n=n)

        for l in range(2):
            job((slot_w(512), w3(I["w_mem_kv"][l], 0, 8, 0, 512)))
            for c0, n in ((0, 512), (512, 512), (1024, 384)):
                job((slot_w(n), w3(I["w_in"][l], 0, 8, c0, c0 + n)))
            for h in range(2):
                job((slot_w(512), w3(I["w_o"][l], 0, 8, 512 * h, 512 * h + 512)))
            for c in range(11):
                job((slot_w(256), w3(I["w_gate_up"][l], 0, 8, 256 * c, 256 * c + 256)),
                    (slot_w(256, 2048), w3(I["w_gate_up"][l], 0, 8, 2816 + 256 * c, 3072 + 256 * c)))
            for h in range(2):
                for k0, k1 in ((0, 8), (8, 16), (16, 22)):
                    job((slot_w(512, 0, k1 - k0), w3(I["w_down"][l], k0, k1, 512 * h, 512 * h + 512)))
        W2 = I["w_in_2"][0]
        for c0, n in ((0, 512), (512, 512), (1024, 512), (1536, 256)):
            job((slot_w(n), w3(W2, 0, 8, c0, c0 + n)))
        job((lambda s: s[0:64, 0:512], I["rw_w_up_2"][0]), (lambda s: s[64:128, 0:512], I["rw_a_up_2"][0]),
            (lambda s: s[:, 512:1024], I["rw_g_up_2"][0]))
        job((slot_w(384), w3(W2, 0, 8, 1792, 2176)))
        job((slot_w(288), w3(W2, 0, 8, 2176, 2464)))
        job((slot_w(768, 0, 3), w3(I["mla_w_q_up_2"][0], 0, 3, 0, 768)))
        job((slot_w(1024, 0, 2), w3(I["mla_w_kv_up_2"][0], 0, 2, 0, 1024)))
        for h in range(2):
            job((slot_w(512, 0, 4), w3(I["w_branch_rw_2"][0], 0, 4, 512 * h, 512 * h + 512)),
                (slot_w(512, 2048, 4), w3(I["w_branch_mla_2"][0], 0, 4, 512 * h, 512 * h + 512)))
            for q in range(2):
                c0 = 512 * h + 256 * q
                job((slot_w(256), w3(W2, 0, 8, 2464 + c0, 2720 + c0)),
                    (slot_w(256, 2048), w3(W2, 0, 8, 3488 + c0, 3744 + c0)))
        for h in range(2):
            job((slot_w(512), w3(I["w_out_2"][0], 0, 8, 512 * h, 512 * h + 512)))

        class Ring:
            def __init__(self):
                self.loaded, self.taken, self.landed = 0, 0, []
                self.after = {}

            def pump(self):
                while self.loaded < len(jobs) and (self.loaded < 3 or (self.loaded - 3) in self.after):
                    n = self.loaded
                    s = RINGC[:, (n % 3) * SLOT:(n % 3 + 1) * SLOT]
                    tok = None
                    for view, src in jobs[n]:
                        tok = ring_sem[n % 3].start(SP, view(s), src, self.after.get(n - 3))
                    self.landed.append(tok)
                    self.loaded += 1

            def take(self):
                n = self.taken
                self.taken += 1
                self.pump()
                return n, RINGC[:, (n % 3) * SLOT:(n % 3 + 1) * SLOT], self.landed[n]

            def done(self, n, tok):
                self.after[n] = tok
                self.pump()

        ring = Ring()

        dc, dx, dg, dr, drow = Dma("s_const"), Dma("s_x"), Dma("s_g"), Dma("s_small"), Dma("s_rows")
        t_c = dc.start(SP, C, consts)
        U0 = top[0]
        T16 = col(4096).rearrange("p (i d) -> p i d", i=NT)
        U = col(12288)
        PB = col(2 * 2048).rearrange("p (b h n) -> p b h n", b=2, h=4)
        PT = col(3 * 512).rearrange("p (b n) -> p b n", b=3)
        MEMT = col(2048).rearrange("p (k m) -> p k m", k=8)
        KMT = col(512).rearrange("p (k m) -> p k m", k=2)
        VM = col(512).rearrange("p (k m) -> p k m", k=2)
        ROW = col(2048).rearrange("p (b n) -> p b n", b=2)
        GR = PT[0:103, 0, 0:128]

        memv = I["mem"][0].rearrange("(i p) d -> p i d", p=P)
        t_mem = dx.start(SP, T16[:, 0:2, :], memv)
        r0 = 0
        t_gr = None
        for name, l, n in GROWS:
            v = I[name]
            v = v.rearrange("(c q) -> c q", q=P) if name == "mem_norm_g" else (
                v[0].rearrange("h d -> (h d)").rearrange("(c q) -> c q", q=P) if name == "rw_r_k_2"
                else v[l].rearrange("(c q) -> c q", q=P))
            t_gr = dg.start(SP, GR[r0:r0 + n, :], v)
            r0 += n
        dxx = Dma("s_xx")
        t_x = dxx.start(SP, X, I["x"][0].rearrange("(i p) d -> p i d", p=P))
        ring.pump()
        sink = small(12)
        qkg = small(128)
        rb = small(36)
        rw = small(288).rearrange("p (k n) -> p k n", n=36)
        posi = small(4)
        dr.start(SP, sink, I["attn_sink"][0].partition_broadcast(P))
        dr.start(SP, qkg, I["qk_norm_g"][0].rearrange("a d -> (a d)").partition_broadcast(P))
        dr.start(SP, rb[:, 0:4], I["moe_b_group_2"][0].partition_broadcast(P))
        dr.start(SP, rb[:, 4:36], I["moe_b_router_2"][0].partition_broadcast(P))
        dr.start(SP, rw[:, :, 0:4], w3(I["moe_w_group_2"][0], 0, 8, 0, 4), allow_slow_non_contiguous=True)
        dr.start(SP, rw[:, :, 4:36], w3(I["moe_w_router_2"][0], 0, 8, 0, 32))
        t_small = dr.start(SP, posi.bitcast(I32), I["positions_2"][0].rearrange("(i p) -> p i", p=P),
                           allow_slow_non_contiguous=True)

        rowd = [Dma("s_row0"), Dma("s_row1")]
        row_n = [0]
        row_used = [None, None]

        def load_row(src):
            b = row_n[0] % 2
            row_n[0] += 1
            return b, rowd[b].start(SP, ROW[:, b, :], src.partition_broadcast(P), row_used[b])

        nhalf = small(8)
        eps6 = 1e-6
        t_nh = G.do(lambda e: e.memset(nhalf, -0.5))
        nsink = small(12)
        V.do(lambda e: e.tensor_scalar(nsink, sink, -1.0, None, ALU.mult), t_small)

        b, bk, w = allb.take()
        t = tr(bk[:, 0:103], GR, t_c, t_gr, w)
        t_gc = V.do(lambda e, bk=bk: e.tensor_copy(GC, bk[:, 0:103]), t)
        give(b, t_gc)

        junk = small(4)

        def rsqrt4(o, ms, n, eps, *toks):
            t1 = V.do(lambda e: e.tensor_scalar(ms, ms, eps, None, ALU.add), *toks)
            return G.do(lambda e: e.tensor_tensor(o, ms, nhalf[:, 0:n], ALU.pow), t1, t_nh)

        nst = [0]
        NST = [(small(4), small(4)) for _ in range(2)]

        def norm_T(src, ntile, D_, scr, g, dst, src_tok, dst_tok, keep=False):
            ms, rs = NST[nst[0] % 2]
            nst[0] += 1
            nk = D_ // P
            toks, hn = [], []
            for i in range(ntile):
                t1 = A.do(lambda e, i=i: e.activation(scr(i), src(i), ACT.Square, scale=float(D_ ** -0.5),
                                                      accum_out=ms[:, i:i + 1]), src_tok(i), dst_tok if i == 0 else None)
                t2 = rsqrt4(rs[:, i:i + 1], ms[:, i:i + 1], 1, eps6, t1)
                t3 = V.do(lambda e, i=i: e.tensor_scalar(scr(i), src(i), rs[:, i:i + 1], None, ALU.mult), t2)
                hn.append(t3)
                for k0 in range(0, nk, 4):
                    n = min(4, nk - k0)
                    b, bk, w = allb.take()
                    for k in range(n):
                        t4 = tr(bk[:, k * P:k * P + P], scr(i)[:, (k0 + k) * P:(k0 + k + 1) * P], t3, w, t_c)
                    o = dst[:, k0:k0 + n, i * P:(i + 1) * P]
                    iv = bk[:, 0:n * P].rearrange("p (k t) -> p k t", k=n)
                    gb = g[:, k0:k0 + n].unsqueeze(2).broadcast_to((P, n, P))
                    t5 = V.do(lambda e, o=o, iv=iv, gb=gb: e.tensor_tensor(o, iv, gb, ALU.mult), t4, t_gc, dst_tok)
                    give(b, t5)
                    toks.append(t5)
            return toks[-1], hn

        AST = [[small(4) for _ in range(5)] for _ in range(2)]
        un = [0]
        pv_done = [None, None]
        pt_n = [0]
        pt_used = [None] * 3

        def scores(u, bp):
            i = un[0] % 2
            un[0] += 1
            u["b"] = i
            mS, ngm, den, rden, ske = AST[i]
            n = u["n"]
            tv = []
            for h in range(4):
                b, bk, w = bp.take()
                t1 = mm(bk[:, 0:n], u["q"][h], u["k"][h], True, True, w, u["tok"])
                if u.get("mask") is not None:
                    t2 = V.free(lambda e, h=h, bk=bk: e.tensor_tensor_reduce(
                        PB[:, i, h, 0:n], bk[:, 0:n], u["mask"], 1.0, -3.0e38, ALU.add, ALU.max, mS[:, h:h + 1]),
                        t1, pv_done[i], t_c, A.last())
                    give(b, t2)
                    tv.append((None, None, t2))
                else:
                    t2 = V.free(lambda e, h=h, bk=bk: e.tensor_reduce(mS[:, h:h + 1], bk[:, 0:n], AX, ALU.max),
                                t1, pv_done[i])
                    tv.append((b, bk, t2))
            if u.get("sink") is not None:
                sl = slice(4 * u["sink"], 4 * u["sink"] + 4)
                t3 = V.do(lambda e: e.scalar_tensor_tensor(ngm, mS, -u["scale"], nsink[:, sl], ALU.mult, ALU.min))
                t3 = V.do(lambda e: e.tensor_tensor(ske, ngm, sink[:, sl], ALU.add))
            else:
                t3 = V.do(lambda e: e.tensor_scalar(ngm, mS, -u["scale"], None, ALU.mult))
            for h in range(4):
                b, bk, t2 = tv[h]
                src = PB[:, i, h, 0:n] if b is None else bk[:, 0:n]
                t4 = A.free(lambda e, h=h, src=src: e.activation(PB[:, i, h, 0:n], src, ACT.Exp, bias=ngm[:, h:h + 1],
                                                                 scale=u["scale"], accum_out=den[:, h:h + 1]),
                            t3, pv_done[i])
                if b is not None:
                    give(b, t4)
                u.setdefault("e", []).append(t4)
            if u.get("sink") is not None:
                t5 = A.free(lambda e: e.activation(ske, ske, ACT.Exp), t3)
                V.do(lambda e: e.tensor_tensor(den, den, ske, ALU.add), t5, t4)
            u["rd"] = V.do(lambda e: e.reciprocal(rden, den), t4)

        def attend(u, bp):
            i, n = u["b"], u["n"]
            nk = n // P
            rden = AST[i][3]
            ob, obk, ow = bp.take()
            for h in range(4):
                b, bk, w = bp.take()
                for k in range(nk):
                    t1 = tr(bk[:, k * P:(k + 1) * P], PB[:, i, h, k * P:(k + 1) * P], u["e"][h], w, inc=(k == nk - 1))
                x = pt_n[0] % 3
                pt_n[0] += 1
                if h % 2 == 0:
                    t2 = A.free(lambda e, x=x, bk=bk: e.activation(PT[:, x, 0:n], bk[:, 0:n], ACT.Copy), t1, pt_used[x])
                else:
                    t2 = V.free(lambda e, x=x, bk=bk: e.tensor_copy(PT[:, x, 0:n], bk[:, 0:n]), t1, pt_used[x])
                give(b, t2)
                for k in range(nk):
                    t3 = mm(obk[:, h * 64:h * 64 + 64], PT[:, x, k * P:(k + 1) * P], u["v"][h][k], k == 0, k == nk - 1,
                            t2, ow)
                pt_used[x] = t3
            pv_done[i] = t1
            o3 = obk[:, 0:256].rearrange("p (h d) -> p h d", h=4)
            t4 = V.free(lambda e: e.tensor_tensor(u["o"], o3, rden.unsqueeze(2).broadcast_to((P, 4, 64)), ALU.mult),
                        t3, u["rd"], u.get("otok"))
            give(ob, t4)
            return t4

        def attention(units, bp):
            scores(units[0], bp)
            for n, u in enumerate(units):
                if n + 1 < len(units):
                    scores(units[n + 1], bp)
                t = attend(u, bp)
            return t

        def rotate(dst1, dst2, x1, x2, c, s, t1, t2, *toks):
            V.do(lambda e: e.tensor_tensor(t1, x1, s, ALU.mult), *toks)
            V.do(lambda e: e.tensor_tensor(t2, x2, s, ALU.mult))
            V.do(lambda e: e.tensor_tensor(dst1, x1, c, ALU.mult))
            V.do(lambda e: e.tensor_tensor(dst2, x2, c, ALU.mult))
            V.do(lambda e: e.tensor_tensor(dst1, dst1, t2, ALU.subtract))
            return V.do(lambda e: e.tensor_tensor(dst2, dst2, t1, ALU.add))

        evn = [0]

        def evac(o, i, *toks):
            evn[0] += 1
            if evn[0] % 2:
                return A.free(lambda e: e.activation(o, i, ACT.Copy), *toks)
            return V.free(lambda e: e.tensor_copy(o, i), *toks)

        def gemm_tok(xT, nk, n, ev, *toks):
            s, slot, t_w = ring.take()
            w = slot_w(n, 0, nk)(slot)
            for i in range(NT):
                b, bk, fr = allb.take()
                for k in range(nk):
                    t = mm(bk[:, 0:n], xT[:, k, i * P:(i + 1) * P], w[:, k, :], k == 0, k == nk - 1, t_w, fr, *toks)
                give(b, ev(i, bk, t))
            ring.done(s, t)
            return t

        def out_T(src, nk, dst, stoks, *toks):
            for k in range(nk):
                b, bk, w = allb.take()
                for i in range(NT):
                    t = tr(bk[:, i * P:(i + 1) * P], src(i, k), w, stoks, inc=(i == 3))
                t2 = evac(dst[:, k, :], bk[:, :], t, *toks)
                give(b, t2)
            return [A.last(), V.last()]

        def post_norm(g_src, tg_, otoks):
            rowb, t_row = g_src
            ms, rs = NST[nst[0] % 2]
            nst[0] += 1
            for i in range(NT):
                t1 = A.do(lambda e, i=i: e.activation(U[:, i * 1024:(i + 1) * 1024], T16[:, i, :], ACT.Square,
                                                      scale=1 / 32.0, accum_out=ms[:, i:i + 1]), otoks)
                t2 = rsqrt4(rs[:, i:i + 1], ms[:, i:i + 1], 1, eps6, t1)
                V.do(lambda e, i=i: e.scalar_tensor_tensor(T16[:, i, :], T16[:, i, :], rs[:, i:i + 1], ROW[:, rowb, :],
                                                           ALU.mult, ALU.mult), t2, t_row)
                t3 = V.do(lambda e, i=i: e.tensor_tensor(X[:, i, :], X[:, i, :], T16[:, i, :], ALU.add), tg_)
            row_used[rowb] = t3
            return t3

        def dump(name, ap, *toks):
            if dbg is not None and name in dbg:
                d = Dma(f"s_dbg_{name}")
                stores.append(d.start(SP, dbg[name], ap, *toks))
                for q in (pe, V, A, G):
                    q.wait(stores[-1])
            return stop == name

        def finish():
            for t in stores:
                SP.wait(t)
            block = ctx.enter_context(nc.Block())

            @block.sync
            def _(e):
                SP.play(e)

            @block.tensor
            def _(e):
                pe.play(e)

            @block.vector
            def _(e):
                V.play(e)

            @block.scalar
            def _(e):
                A.play(e)

            @block.gpsimd
            def _(e):
                G.play(e)

        t_memT, _ = norm_T(lambda i: T16[:, i, :], 2, D, lambda i: T16[:, 2 + i, :], gcol("mem_norm_g"), MEMT,
                           lambda i: t_mem, None)

        xt = t_x
        for l in range(2):
            s, slot, t_w = ring.take()
            w = slot_w(512)(slot)
            KM = U[:, 0:512].rearrange("p (i m) -> p i m", i=2)
            for i in range(2):
                b, bk, fr = allb.take()
                for k in range(8):
                    t = mm(bk[:, :], MEMT[:, k, i * P:(i + 1) * P], w[:, k, :], k == 0, k == 7, t_w, t_memT, fr, xt)
                A.free(lambda e, bk=bk, i=i: e.activation(KM[:, i, :], bk[:, 0:256], ACT.Copy), t, xt)
                t2 = A.free(lambda e, bk=bk, i=i: e.activation(VM[:, i, :], bk[:, 256:512], ACT.Copy), t, pe.last())
                give(b, t2)
            ring.done(s, t)
            b, bk, fr = allb.take()
            for k in range(2):
                for i in range(2):
                    t = tr(bk[:, (2 * k + i) * P:(2 * k + i + 1) * P], KM[:, i, k * P:(k + 1) * P], t2, fr)
            t_km = A.free(lambda e, bk=bk: e.activation(KMT, bk[:, :].rearrange("p (k m) -> p k m", k=2), ACT.Copy), t)
            give(b, t_km)

            t_h, _ = norm_T(lambda i: X[:, i, :], NT, D, lambda i: T16[:, i, :], gcol("g_mix_pre", l), HT,
                            lambda i: xt, [pe.last(), V.last()])
            QKV = U[:, 0:5632].rearrange("p (i n) -> p i n", i=NT)
            QT = U[:, 5632:9728].rearrange("p (k t) -> p k t", k=8)
            KT = U[:, 9728:11264].rearrange("p (k t) -> p k t", k=3)
            for c0, n in ((0, 512), (512, 512), (1024, 384)):
                gemm_tok(HT, 8, n, lambda i, bk, t, c0=c0, n=n: evac(QKV[:, i, c0:c0 + n], bk[:, 0:n], t, t_km, pe.last()),
                         t_h)
            t_q = [A.last(), V.last()]
            if dump(f"qkv{l}", QKV, *t_q):
                return finish()
            KR = T16[:, :, 0:384].rearrange("p i (g r d) -> p i g r d", g=3, r=2)
            TM = U[:, 11264:12288]
            if l == 0:
                H15 = QKV[:, :, 0:960].rearrange("p i (h d) -> p i h d", d=64)
                x1, x2 = H15[:, :, :, 0:8], H15[:, :, :, 8:16]
                cb = k_("cosp").rearrange("p (i c) -> p i c", i=NT).unsqueeze(2).broadcast_to((P, NT, 15, 8))
                sb_ = k_("sinp").rearrange("p (i c) -> p i c", i=NT).unsqueeze(2).broadcast_to((P, NT, 15, 8))
                t1 = TM[:, 0:480].rearrange("p (i h c) -> p i h c", i=NT, c=8)
                t2 = TM[:, 480:960].rearrange("p (i h c) -> p i h c", i=NT, c=8)
                t_r = rotate(x1, x2, x1, x2, cb, sb_, t1, t2, t_q, t_c)
            else:
                for i in range(NT):
                    H = QKV[:, i, 0:960].rearrange("p (h d) -> p h d", d=64)
                    sq = PB[:, 0, 0:2, :].rearrange("p a n -> p (a n)")[:, 0:960].rearrange("p (h d) -> p h d", d=64)
                    ms = TM[:, 0:15]
                    rs = TM[:, 16:31]
                    V.do(lambda e, H=H, sq=sq: e.tensor_tensor(sq, H, H, ALU.mult), t_q, pv_done[0])
                    V.do(lambda e, ms=ms, sq=sq: e.tensor_reduce(ms, sq, AX, ALU.add))
                    V.do(lambda e, ms=ms: e.tensor_scalar(ms, ms, 1 / 64.0, eps6, ALU.mult, ALU.add))
                    t = A.do(lambda e, ms=ms: e.activation(ms, ms, ACT.Sqrt), V.last())
                    V.do(lambda e, ms=ms, rs=rs: e.reciprocal(rs, ms), t)
                    V.do(lambda e, H=H, rs=rs: e.tensor_tensor(H, H, rs.unsqueeze(2).broadcast_to((P, 15, 64)), ALU.mult))
                    V.do(lambda e, H=H: e.tensor_tensor(H[:, 0:12, :], H[:, 0:12, :],
                                                        qkg[:, 0:64].unsqueeze(1).broadcast_to((P, 12, 64)), ALU.mult))
                    V.do(lambda e, H=H: e.tensor_tensor(H[:, 12:15, :], H[:, 12:15, :],
                                                        qkg[:, 64:128].unsqueeze(1).broadcast_to((P, 3, 64)), ALU.mult))
                    G5 = QKV[:, i, 0:960].rearrange("p (h a b c) -> p h a b c", a=2, b=2, c=16)
                    cx = k_("cosx").rearrange("p (i a c) -> p i a c", i=NT, a=2)[:, i]
                    sx = k_("sinx").rearrange("p (i a c) -> p i a c", i=NT, a=2)[:, i]
                    T = [TM[:, 32:512].rearrange("p (h a c) -> p h a c", a=2, c=16),
                         TM[:, 512:992].rearrange("p (h a c) -> p h a c", a=2, c=16)]
                    t_r = rotate(G5[:, :, :, 0, :], G5[:, :, :, 1, :], G5[:, :, :, 0, :], G5[:, :, :, 1, :],
                                 cx.unsqueeze(1).broadcast_to((P, 15, 2, 16)), sx.unsqueeze(1).broadcast_to((P, 15, 2, 16)),
                                 *T)
            k3 = QKV[:, :, 768:960].rearrange("p i (g d) -> p i g d", g=3)
            for r in range(2):
                t_kr = V.do(lambda e, r=r: e.tensor_copy(KR[:, :, :, r, :], k3), pe.last())
            t_qT = out_T(lambda i, k: QKV[:, i, k * P:(k + 1) * P] if k < 6 else QKV[:, i, 1152 + (k - 6) * P:1280 + (k - 6) * P],
                         8, QT, [t_q, t_r, t_kr])
            t_kT = out_T(lambda i, k: T16[:, i, k * P:(k + 1) * P], 3, KT, [t_kr])
            t_att = [t_qT, t_kT, t_km]
            if dump(f"qT{l}", QT, *t_qT):
                return finish()
            units = []
            for i in range(NT):
                for g in range(3):
                    k0, k1 = (max(0, i - 1), min(4, i + 2)) if l == 0 else (0, 4)
                    u = dict(n=(k1 - k0) * P, scale=SCALE, tok=t_att, otok=pe.last(),
                             q=[QT[64 * (h % 2):64 * (h % 2) + 64, (4 * g + h) // 2, i * P:(i + 1) * P] for h in range(4)],
                             k=[KT[64 * (h % 2):64 * (h % 2) + 64, g, k0 * P:k1 * P] for h in range(4)],
                             v=[[QKV[:, kt, 960 + 64 * g:1024 + 64 * g] for kt in range(k0, k1)]] * 4,
                             o=T16[:, i, 256 * g:256 * g + 256].rearrange("p (h d) -> p h d", h=4))
                    if l == 0:
                        u["sink"] = g
                        off = 128 if k0 == i else 0
                        u["mask"] = k_("band")[:, off:off + u["n"]]
                    units.append(u)
                units.append(dict(n=256, scale=SCALE, tok=t_att, otok=pe.last(),
                                  q=[QT[64 * (h % 2):64 * (h % 2) + 64, 6 + h // 2, i * P:(i + 1) * P] for h in range(4)],
                                  k=[KMT[64 * (h % 2):64 * (h % 2) + 64, h // 2, :] for h in range(4)],
                                  v=[[VM[:, kt, 64 * h:64 * h + 64] for kt in range(2)] for h in range(4)],
                                  o=T16[:, i, 768:1024].rearrange("p (h d) -> p h d", h=4)))
            t_o = attention(units, allb)
            if dump(f"mix{l}", T16, t_o):
                return finish()
            row = load_row(I["g_mix_post"][l])
            t_oT = out_T(lambda i, k: T16[:, i, k * P:(k + 1) * P], 8, HT, [t_o])
            for h in range(2):
                gemm_tok(HT, 8, 512, lambda i, bk, t, h=h: evac(T16[:, i, 512 * h:512 * h + 512], bk[:, :], t, pe.last()),
                         t_oT)
            xt = post_norm(row, None, [A.last(), V.last(), pe.last()])
            if dump(f"xa{l}", X, xt):
                return finish()

            t_h, _ = norm_T(lambda i: X[:, i, :], NT, D, lambda i: T16[:, i, :], gcol("g_ffn_pre", l), HT,
                            lambda i: xt, pe.last())
            FT = U[:, 0:22 * 512].rearrange("p (k t) -> p k t", k=22)
            tmp = PB[:, :, :, :].rearrange("p b h n -> p (b h) n")
            for c in range(11):
                s, slot, t_w = ring.take()
                wv = [slot_w(256)(slot), slot_w(256, 2048)(slot)]
                for q in range(2):
                    two = []
                    for j in range(2):
                        b, bk, fr = allb.take()
                        for k in range(8):
                            t = mm(bk[:, :], wv[j][:, k, q * P:(q + 1) * P], HT[:, k, :], k == 0, k == 7, t_w, t_h, fr)
                        two.append((b, bk, t))
                    z = (2 * c + q) % 4
                    (b0, g0, t0), (b1, g1, t1) = two
                    ta = A.free(lambda e, z=z, g0=g0: e.activation(tmp[:, z, :], g0[:, :], ACT.Tanh, scale=0.5), t0,
                                V.last(), pe.last())
                    tb = V.do(lambda e, z=z, g0=g0: e.scalar_tensor_tensor(tmp[:, z, :], tmp[:, z, :], 1.0, g0[:, :],
                                                                           ALU.add, ALU.mult), ta)
                    give(b0, tb)
                    tc_ = V.do(lambda e, z=z, g1=g1, f=2 * c + q: e.scalar_tensor_tensor(
                        FT[:, f, :], tmp[:, z, :], 0.5, g1[:, :], ALU.mult, ALU.mult), t1)
                    give(b1, tc_)
                ring.done(s, t1)
            if dump(f"ft{l}", FT, tc_):
                return finish()
            row = load_row(I["g_ffn_post"][l])
            t_last = pe.last()
            for h in range(2):
                four = [allb.take() for _ in range(NT)]
                for k0, k1 in ((0, 8), (8, 16), (16, 22)):
                    s, slot, t_w = ring.take()
                    w = slot_w(512, 0, k1 - k0)(slot)
                    for i in range(NT):
                        b, bk, fr = four[i]
                        for k in range(k0, k1):
                            t = mm(bk[:, :], FT[:, k, i * P:(i + 1) * P], w[:, k - k0, :], k == 0, k == 21, t_w, tc_, fr,
                                   inc=(k == k1 - 1))
                        if k1 == 22:
                            give(b, A.free(lambda e, i=i, bk=bk, h=h: e.activation(
                                T16[:, i, 512 * h:512 * h + 512], bk[:, :], ACT.Copy), t, t_last))
                    ring.done(s, t)
            xt = post_norm(row, None, [A.last(), pe.last()])
            if dump(f"xb{l}", X, xt):
                return finish()
        if stop == "block1":
            return finish()
        R = arena[:, U0:U0 + 27136]

        def at(a, n):
            assert a + n <= 27136
            return R[:, a:a + n]

        w0h, a0h, oka = small(4), small(4), small(4)
        V.do(lambda e: e.tensor_scalar(w0h, gcol("rw_w0_2")[:, 0:4], 0.5, None, ALU.mult))
        V.do(lambda e: e.tensor_scalar(a0h, gcol("rw_a0_2")[:, 0:4], 0.5, None, ALU.mult))
        t_cols = V.do(lambda e: e.tensor_scalar(oka, gcol("rw_k_a_2")[:, 0:4], -1.0, 1.0, ALU.mult, ALU.add))

        t_h, _ = norm_T(lambda i: X[:, i, :], NT, D, lambda i: T16[:, i, :], gcol("mix_norm_g_2"), HT,
                        lambda i: xt, pe.last())
        Z = at(0, 7168).rearrange("p (c t) -> p c t", t=512)
        ZI = at(24064, 1026).rearrange("p (b t) -> p b t", t=513)
        for b_ in range(2):
            t_zi = V.do(lambda e, b_=b_: e.memset(ZI[:, b_, 0:1], 0.0), pe.last())
        mu = gcol("rw_mu_2")
        zl = [None, None]
        for s4, nc_ in enumerate((4, 4, 4, 2)):
            s, slot, t_w = ring.take()
            w = slot_w(nc_ * P)(slot)
            for q in range(nc_):
                c = 4 * s4 + q
                b, bk, fr = allb.take()
                for k in range(8):
                    t = mm(bk[:, :], w[:, k, q * P:(q + 1) * P], HT[:, k, :], k == 0, k == 7, t_w, t_h, fr)
                zi = ZI[:, c % 2, :]
                t1 = A.free(lambda e, zi=zi, bk=bk: e.activation(zi[:, 1:513], bk[:, :], ACT.Copy), t, t_zi, zl[c % 2])
                give(b, t1)
                zc = Z[:, c, :]
                V.do(lambda e, zi=zi, zc=zc: e.tensor_tensor(zc, zi[:, 0:512], zi[:, 1:513], ALU.subtract), t1, pe.last())
                zl[c % 2] = V.do(lambda e, zi=zi, zc=zc, c=c: e.scalar_tensor_tensor(zc, zc, mu[:, c:c + 1], zi[:, 1:513],
                                                                                   ALU.mult, ALU.add))
            ring.done(s, t)
        A.do(lambda e: e.activation(Z[0:64, 12, :], Z[0:64, 12, :], ACT.Tanh), V.last())
        t1 = A.do(lambda e: e.activation(Z[:, 13, :], Z[:, 13, :], ACT.Tanh, scale=0.5))
        t_z = V.do(lambda e: e.tensor_scalar(Z[:, 13, :], Z[:, 13, :], 0.5, 0.5, ALU.mult, ALU.add), t1)
        if dump("z", Z, t_z):
            return finish()

        o_ = [7168]

        def buf(n):
            o_[0] += n
            return at(o_[0] - n, n)

        ARt = buf(1024).rearrange("p (m n) -> p m n", m=4)
        KH, BH = buf(512), buf(512)
        Vt, Kt, Bt, At = [buf(512).rearrange("p (m n) -> p m n", m=4) for _ in range(4)]
        GMf = buf(4096)
        GM = GMf.rearrange("p (i n) -> p i n", i=8)
        XXf = buf(2048)
        XX = XXf.rearrange("p (i n) -> p i n", i=8)
        LM = buf(1024).rearrange("p (i n) -> p i n", i=8)
        T1b = buf(1024).rearrange("p (i n) -> p i n", i=8)
        PP = buf(1024).rearrange("p (i n) -> p i n", i=8)
        Us = buf(512).rearrange("p (i n) -> p i n", i=8)
        Q2 = buf(512).rearrange("p (m n) -> p m n", m=4)
        Fm, Ec, Sst = buf(512), buf(512), buf(512)
        BON = buf(512)
        tmpj = [GMf[:, 512 * i:512 * i + 512] for i in range(8)] + [XXf[:, 512 * i:512 * i + 512] for i in range(4)]
        Wc = small(8)
        C1 = -0.5 * float(np.exp(-0.5))
        s_misc, slot, t_misc = ring.take()
        wu, au, gu = slot[0:64, 0:512], slot[64:128, 0:512], slot[:, 512:1024]
        v4 = lambda ap: ap.rearrange("p (m n) -> p m n", m=4)

        for j in range(4):
            r_, k0_, v_ = Z[:, j, :], Z[:, 4 + j, :], Z[:, 8 + j, :]
            js = slice(j, j + 1)
            th, LW, L, E0, E1, E2, a_, kk, kp, b2, rk, sq = tmpj
            cs = slice(j * P, (j + 1) * P)

            def elementwise(j, r_, k0_, v_, js, cs):
                b, bk, fr = allb.take()
                t = mm(bk[:, :], wu[:, cs], Z[0:64, 12, :], True, True, t_misc, t_z, fr)
                t1 = A.do(lambda e: e.activation(th, bk[:, :], ACT.Tanh, bias=w0h[:, js], scale=0.5), t, t_cols, pe.last(),
                          V.last())
                give(b, t1)
                V.do(lambda e: e.tensor_scalar(LW, th, C1, C1, ALU.mult, ALU.add), t1)
                t1 = V.do(lambda e: e.tensor_tensor_scan(L, k_("keep"), LW, 0.0, ALU.mult, ALU.add))
                A.do(lambda e: e.activation(E1, L, ACT.Exp), t1)
                A.do(lambda e: e.activation(E2, L, ACT.Exp, scale=-1.0))
                t1 = V.do(lambda e: e.tensor_tensor(LW, L, LW, ALU.subtract))
                A.do(lambda e: e.activation(E0, LW, ACT.Exp), t1)
                b, ba, fr = allb.take()
                t = mm(ba[:, :], au[:, cs], Z[64:128, 12, :], True, True, fr)
                t1 = A.do(lambda e: e.activation(a_, ba[:, :], ACT.Tanh, bias=a0h[:, js], scale=0.5), t)
                give(b, t1)
                V.do(lambda e: e.tensor_scalar(a_, a_, 0.5, 0.5, ALU.mult, ALU.add), t1)
                V.do(lambda e: e.tensor_scalar(kk, k0_, gcol("rw_k_k_2")[:, js], None, ALU.mult))
                t1 = V.do(lambda e: e.tensor_tensor(sq, kk, kk, ALU.mult))
                b, bs, fr = allb.take()
                t = mm(bs[:, :], k_("bones"), sq, True, True, t1, fr)
                t1 = V.do(lambda e: e.tensor_scalar(sq, bs[:, :], 1e-24, None, ALU.max), t)
                give(b, t1)
                t1 = A.do(lambda e: e.activation(sq, sq, ACT.Sqrt), t1)
                V.do(lambda e: e.reciprocal(sq, sq), t1)
                V.do(lambda e: e.tensor_tensor(kk, kk, sq, ALU.mult))
                V.do(lambda e: e.tensor_scalar(kp, a_, gcol("rw_k_a_2")[:, js], oka[:, js], ALU.mult, ALU.add))
                V.do(lambda e: e.tensor_tensor(kp, kp, k0_, ALU.mult))
                V.do(lambda e: e.tensor_tensor(b2, kk, a_, ALU.mult))
                V.do(lambda e: e.scalar_tensor_tensor(ARt[:, :, 0:128], v4(E0), -1.0, v4(kk), ALU.mult, ALU.mult))
                V.do(lambda e: e.tensor_tensor(ARt[:, :, 128:256], v4(E1), v4(r_), ALU.mult))
                V.do(lambda e: e.tensor_tensor(KH, kp, E2, ALU.mult))
                V.do(lambda e: e.tensor_tensor(BH, b2, E2, ALU.mult))
                V.do(lambda e: e.tensor_copy(Wc, E1.rearrange("p (c n) -> p c n", n=64)[:, :, 63]))
                t1 = V.do(lambda e: e.scalar_tensor_tensor(rk, r_, gcol("rw_r_k_2")[:, js], kp, ALU.mult, ALU.mult))
                b, bb, fr = allb.take()
                t = mm(bb[:, :], k_("bones"), rk, True, True, t1, fr)
                t1 = V.do(lambda e: e.tensor_tensor(BON, bb[:, :], v_, ALU.mult), t)
                give(b, t1)
                return t1

            t_e = elementwise(j, r_, k0_, v_, js, cs)
            for src, dst in ((lambda m: v_[:, m * P:(m + 1) * P], Vt), (lambda m: KH[:, m * P:(m + 1) * P], Kt),
                             (lambda m: BH[:, m * P:(m + 1) * P], Bt), (lambda m: ARt[:, m, 0:128], At)):
                b, bk, fr = allb.take()
                for m in range(4):
                    t = tr(bk[:, m * P:(m + 1) * P], src(m), t_e, fr, inc=(m == 3))
                give(b, evac(dst, v4(bk[:, :]), t))
            t_T = [A.last(), V.last()]

            def item(it):
                hh, m = it // 4, it % 4
                return m, hh, slice(64 * hh, 64 * hh + 64)

            for it in range(8):
                m, hh, ps = item(it)
                b, bk, fr = allb.take()
                ms = slice(m * P, (m + 1) * P)
                mm(bk[:, 0:256], BH[ps, ms], ARt[ps, m, :], True, True, t_e, fr, inc=False)
                t = mm(bk[:, 256:512], KH[ps, ms], ARt[ps, m, :], True, True)
                t1 = V.free(lambda e, it=it, bk=bk: e.tensor_tensor(GM[:, it, :], bk[:, :], k_("mgram"), ALU.mult), t, V.last())
                give(b, t1)
            for q in range(2):
                b, bk, fr = allb.take()
                for r in range(4):
                    m, hh, ps = item(4 * q + r)
                    t = mm(bk[:, r * P:(r + 1) * P], ARt[ps, m, 0:128], BH[ps, m * P:(m + 1) * P], True, True, t_e, fr,
                           inc=(r == 3))
                xs = XX[:, 4 * q:4 * q + 4, 0:128]
                xt_ = XX[:, 4 * q:4 * q + 4, 128:256]
                bc = lambda n: k_(n).unsqueeze(1).broadcast_to((P, 4, P))
                t1 = V.do(lambda e, xs=xs, bk=bk: e.tensor_tensor(xs, v4(bk[:, :]), bc("low1"), ALU.mult), t)
                give(b, t1)
                V.do(lambda e, xs=xs: e.tensor_tensor(xs, xs, bc("ident"), ALU.add))
                V.do(lambda e, xt_=xt_, q=q: e.tensor_tensor(xt_, GM[:, 4 * q:4 * q + 4, 0:128], bc("up1"), ALU.mult))
                t_x2 = V.do(lambda e, xt_=xt_: e.tensor_tensor(xt_, xt_, bc("ident"), ALU.add))
            for n in (2, 4, 8, 16, 32):
                t_lm = G.do(lambda e, n=n: e.tensor_tensor(LM, GM[:, :, 0:128],
                                                           k_(f"up{n}").unsqueeze(1).broadcast_to((P, 8, P)), ALU.mult),
                            V.last(), pe.last())
                for q in range(2):
                    b, bk, fr = allb.take()
                    for r in range(4):
                        it = 4 * q + r
                        t = mm(bk[:, r * P:(r + 1) * P], LM[:, it, :], XX[:, it, 0:128], True, True, t_lm, t_x2, fr,
                               inc=(r == 3))
                    give(b, evac(T1b[:, 4 * q:4 * q + 4, :], v4(bk[:, :]), t))
                t_t1 = [A.last(), V.last()]
                for q in range(4):
                    b, bk, fr = allb.take()
                    for r in range(2):
                        it = 2 * q + r
                        mm(bk[:, r * 256:r * 256 + 128], XX[:, it, 128:256], T1b[:, it, :], True, True, t_t1, fr, inc=False)
                        t = mm(bk[:, r * 256 + 128:r * 256 + 256], T1b[:, it, :], XX[:, it, 128:256], True, True,
                               inc=(r == 1))
                    xs = XX[:, 2 * q:2 * q + 2, :]
                    t_x2 = V.do(lambda e, xs=xs, bk=bk: e.tensor_tensor(
                        xs, xs, bk[:, :].rearrange("p (i n) -> p i n", i=2), ALU.add), t)
                    give(b, t_x2)
            b, bk, fr = allb.take()
            for it in range(8):
                m, hh, ps = item(it)
                t = mm(bk[:, it * 64:it * 64 + 64], GM[:, it, 256:384], Vt[:, m, ps], True, True, t_T, fr, V.last(),
                       inc=(it == 7))
            t_us = evac(Us, bk[:, :].rearrange("p (i n) -> p i n", i=8), t)
            give(b, t_us)
            for q in range(2):
                b, bk, fr = allb.take()
                for r in range(4):
                    it = 4 * q + r
                    m, hh, ps = item(it)
                    mm(bk[:, r * P:r * P + 64], XX[:, it, 128:256], At[:, m, ps], True, True, t_x2, t_us, fr, inc=False)
                    t = mm(bk[:, r * P + 64:r * P + 128], XX[:, it, 128:256], Us[:, it, :], True, True, inc=(r == 3))
                give(b, evac(PP[:, 4 * q:4 * q + 4, :], v4(bk[:, :]), t))
            t_pp = [A.last(), V.last()]
            b, bq, fq = allb.take()
            v8 = lambda ap: ap.rearrange("p (c n) -> p c n", c=8)
            by_half = lambda ap, cc: ap.rearrange("p (m c n) -> p m c n", c=2, n=64)[:, :, cc, :]
            for it in range(8):
                m, hh, ps = item(it)
                t = mm(bq[ps, m * P:(m + 1) * P], PP[:, it, 0:64], GM[:, it, 128:256], True, True, t_pp, fq, inc=(it == 7))
            t_q2 = V.do(lambda e, bq=bq: e.tensor_tensor(Q2, v4(bq[:, :]), ARt[:, :, 128:256], ALU.add), t)
            give(b, t_q2)
            for cc in range(2):
                cr = slice(64 * cc, 64 * cc + 64)
                b, bk, fr = allb.take()
                for it in range(8):
                    m, hh, ps = item(it)
                    t = mm(bk[ps, m * 64:m * 64 + 64], PP[cr, it, 0:64], Bt[cr, m, ps], True, True, fr, inc=(it == 7))
                t_f = V.do(lambda e, bk=bk, cc=cc: e.tensor_tensor(
                    by_half(Fm, cc), bk[:, 0:256].rearrange("p (m n) -> p m n", m=4),
                    k_("ident64").unsqueeze(1).broadcast_to((P, 4, 64)), ALU.add), t)
                give(b, t_f)
                b, bk, fr = allb.take()
                for it in range(8):
                    m, hh, ps = item(it)
                    mm(bk[ps, m * 64:m * 64 + 64], Bt[cr, m, ps], PP[cr, it, 64:128], True, False, fr)
                    t = mm(bk[ps, m * 64:m * 64 + 64], Kt[cr, m, ps], Vt[cr, m, ps], False, True, inc=(it == 7))
                t_ec = V.do(lambda e, bk=bk, cc=cc: e.tensor_tensor(
                    by_half(Ec, cc), bk[:, 0:256].rearrange("p (m n) -> p m n", m=4),
                    Wc.rearrange("p (m c) -> p m c", c=2)[:, :, cc:cc + 1].broadcast_to((P, 4, 64)), ALU.mult), t)
                give(b, t_ec)
            ts_ = V.do(lambda e: e.tensor_copy(Sst[:, 64:128], Ec[:, 0:64]), pe.last())
            for c in range(1, 7):
                b, bk, fr = allb.take()
                for hh in range(2):
                    ps = slice(64 * hh, 64 * hh + 64)
                    t = mm(bk[ps, 0:64], Fm[ps, c * 64:c * 64 + 64], Sst[ps, c * 64:c * 64 + 64], True, True, t_f, ts_, fr,
                           inc=(hh == 1))
                ts_ = V.do(lambda e, bk=bk, c=c: e.scalar_tensor_tensor(
                    Sst[:, c * 64 + 64:c * 64 + 128], bk[:, 0:64], Wc[:, c:c + 1], Ec[:, c * 64:c * 64 + 64],
                    ALU.mult, ALU.add), t)
                give(b, ts_)
            b, by, fr = allb.take()
            for it in range(8):
                m, hh, ps = item(it)
                ms = slice(m * P, (m + 1) * P)
                mm(by[ps, ms], PP[:, it, 64:128], GM[:, it, 128:256], True, False, t_pp, ts_, fr)
                t = mm(by[ps, ms], Vt[:, m, ps], GM[:, it, 384:512], False, True, inc=False)
                for cc in range(2):
                    c = 2 * m + cc
                    if c:
                        t = mm(by[ps, c * 64:c * 64 + 64], Sst[ps, c * 64:c * 64 + 64], Q2[ps, m, cc * 64:cc * 64 + 64],
                               False, True, inc=(it == 7))
            y_, yc, q_, rs_ = tmpj[8:12]
            t1 = V.do(lambda e, by=by: e.tensor_copy(y_, by[:, :]), t)
            give(b, t1)
            if dump(f"ys{j}", y_, t1):
                return finish()

            def group_norm(j, js, cs, t1):
                b, bk, fr = allb.take()
                t = mm(bk[:, :], k_("bmean"), y_, True, True, t1, fr)
                t1 = V.do(lambda e: e.tensor_tensor(yc, y_, bk[:, :], ALU.subtract), t)
                give(b, t1)
                t1 = V.do(lambda e: e.tensor_tensor(q_, yc, yc, ALU.mult))
                b, b2_, fr = allb.take()
                t = mm(b2_[:, :], k_("bmean"), q_, True, True, t1, fr)
                t1 = V.do(lambda e: e.tensor_scalar(rs_, b2_[:, :], 64e-5, None, ALU.add), t)
                give(b, t1)
                t1 = A.do(lambda e: e.activation(rs_, rs_, ACT.Sqrt), t1)
                V.do(lambda e: e.reciprocal(rs_, rs_), t1)
                V.do(lambda e: e.tensor_tensor(yc, yc, rs_, ALU.mult))
                V.do(lambda e: e.tensor_scalar(yc, yc, gcol("rw_gn_w_2")[:, js], gcol("rw_gn_b_2")[:, js], ALU.mult, ALU.add))
                V.do(lambda e: e.tensor_tensor(yc, yc, BON, ALU.add))
                b, b3_, fr = allb.take()
                t = mm(b3_[:, :], gu[:, cs], Z[:, 13, :], True, True, fr)
                t1 = V.do(lambda e: e.tensor_tensor(Z[:, j, :], yc, b3_[:, :], ALU.mult), t)
                give(b, t1)
                return t, t1

            t, t_yr = group_norm(j, js, cs, t1)
        ring.done(s_misc, t)
        YR = Z[:, 0:4, :]
        if dump("yr", YR, t_yr):
            return finish()

        CK = at(2048, 1152).rearrange("p (i n) -> p i n", i=4)
        CQ = at(3200, 1536).rearrange("p (i n) -> p i n", i=4)
        SC = at(4736, 1536).rearrange("p (i n) -> p i n", i=4)
        KF = at(3200, 3072).rearrange("p (i h d) -> p i h d", i=4, h=8)
        QDT = at(6272, 1536).rearrange("p (k t) -> p k t", k=3)
        KDT = at(7808, 1024).rearrange("p (k t) -> p k t", k=2)
        YM = at(6272, 2048).rearrange("p (i n) -> p i n", i=4)
        YMT = at(2048, 2048).rearrange("p (k t) -> p k t", k=4)
        QS = at(8832, 3072).rearrange("p (i h d) -> p i h d", i=4, h=8)
        QTh = at(11904, 2048).rearrange("p (h t) -> p h t", h=4)
        KTh = at(13952, 2048).rearrange("p (h t) -> p h t", h=4)
        VV = at(22016, 2048).rearrange("p (i h d) -> p i h d", i=4, h=8)
        TMP = at(24064, 1024)
        MT = at(8832, 4096).rearrange("p (k t) -> p k t", k=8)

        ang, nn, cosm, sinm = [TMP[:, 64 * q:64 * q + 64] for q in range(4)]
        ni = TMP[:, 256:320].bitcast(I32)
        a3 = lambda ap: ap.rearrange("p (i c) -> p i c", i=4)
        posf = small(4)
        V.do(lambda e: e.tensor_copy(posf, posi.bitcast(I32)), t_small, t_z)
        V.do(lambda e: e.tensor_tensor(a3(ang), posf.unsqueeze(2).broadcast_to((P, 4, 16)),
                                       k_("invf").unsqueeze(1).broadcast_to((P, 4, 16)), ALU.mult), A.last())
        V.do(lambda e: e.tensor_scalar(nn, ang, float(1 / (2 * np.pi)), None, ALU.mult))
        V.do(lambda e: e.tensor_copy(ni, nn))
        V.do(lambda e: e.tensor_copy(nn, ni))
        c1 = 6.28125
        c2 = float(np.float32(np.round((2 * np.pi - c1) * 2 ** 20) / 2 ** 20))
        c3 = float(2 * np.pi - c1 - c2)
        for c_ in (c1, c2, c3):
            V.do(lambda e, c_=c_: e.scalar_tensor_tensor(ang, nn, -c_, ang, ALU.mult, ALU.add))
        pi_ = 3.1415925
        V.do(lambda e: e.tensor_scalar(ang, ang, pi_, -pi_, ALU.min, ALU.max))
        V.do(lambda e: e.tensor_scalar(nn, ang, -1.0, None, ALU.mult))
        V.do(lambda e: e.tensor_tensor(nn, nn, ang, ALU.max))
        t1 = V.do(lambda e: e.tensor_scalar(nn, nn, -1.0, float(np.pi / 2), ALU.mult, ALU.add))
        A.do(lambda e: e.activation(sinm, ang, ACT.Sin), t1)
        t_cs = A.do(lambda e: e.activation(cosm, nn, ACT.Sin))

        gemm_tok(HT, 8, 384, lambda i, bk, t: evac(CQ[:, i, :], bk[:, 0:384], t, V.last()))
        gemm_tok(HT, 8, 288, lambda i, bk, t: evac(CK[:, i, :], bk[:, 0:288], t))
        t_ck = [A.last(), V.last()]
        t_qd, _ = norm_T(lambda i: CQ[:, i, :], NT, 384, lambda i: SC[:, i, :], gcol("mla_g_qa_2"), QDT,
                         lambda i: t_ck, pe.last())
        t_kd, _ = norm_T(lambda i: CK[:, i, 0:256], NT, 256, lambda i: SC[:, i, 0:256], gcol("mla_g_kva_2"), KDT,
                         lambda i: t_ck, pe.last())
        s, slot, t_w = ring.take()
        w = slot_w(768, 0, 3)(slot)
        for i in range(NT):
            for h in range(2):
                b, bk, fr = allb.take()
                for k in range(3):
                    t = mm(bk[:, 0:384], QDT[:, k, i * P:(i + 1) * P], w[:, k, 384 * h:384 * h + 384], k == 0, k == 2,
                           t_w, t_qd, fr)
                give(b, evac(QS[:, i, 4 * h:4 * h + 4, :], bk[:, 0:384].rearrange("p (h d) -> p h d", h=4), t))
        ring.done(s, t)
        s, slot, t_w = ring.take()
        w = slot_w(1024, 0, 2)(slot)
        for i in range(NT):
            for h in range(2):
                b, bk, fr = allb.take()
                for k in range(2):
                    t = mm(bk[:, :], KDT[:, k, i * P:(i + 1) * P], w[:, k, 512 * h:512 * h + 512], k == 0, k == 1,
                           t_w, t_kd, fr)
                b4 = bk[:, :].rearrange("p (h d) -> p h d", h=4)
                A.free(lambda e, b4=b4, i=i, h=h: e.activation(KF[:, i, 4 * h:4 * h + 4, 0:64], b4[:, :, 0:64], ACT.Copy), t)
                give(b, A.free(lambda e, b4=b4, i=i, h=h: e.activation(VV[:, i, 4 * h:4 * h + 4, :], b4[:, :, 64:128], ACT.Copy), t))
        ring.done(s, t)
        cb = lambda ap, h: a3(ap).unsqueeze(2).broadcast_to((P, 4, h, 16))
        T4 = lambda a, h: TMP[:, a:a + 64 * h].rearrange("p (i h c) -> p i h c", i=4, h=h)
        q1, q2 = (TMP[:, 320:832], PT[:, 0, :])
        qv = lambda ap: ap.rearrange("p (i h c) -> p i h c", i=4, h=8)
        t_e1 = [A.last(), V.last(), t_cs]
        rotate(QS[:, :, :, 64:80], QS[:, :, :, 80:96], QS[:, :, :, 64:80], QS[:, :, :, 80:96],
               cb(cosm, 8), cb(sinm, 8), qv(q1), qv(q2), t_e1)
        rotate(CK[:, :, 256:272], CK[:, :, 272:288], CK[:, :, 256:272], CK[:, :, 272:288],
               a3(cosm), a3(sinm), a3(TMP[:, 832:896]), a3(TMP[:, 896:960]))
        t_kf = V.do(lambda e: e.tensor_copy(KF[:, :, :, 64:96],
                                            CK[:, :, 256:288].unsqueeze(2).broadcast_to((P, 4, 8, 32))), t_e1)
        for g in range(2):
            for src, dst in ((QS, QTh), (KF, KTh)):
                for h in range(4):
                    b, bk, fr = allb.take()
                    for i in range(4):
                        t = tr(bk[0:96, i * P:(i + 1) * P], src[:, i, 4 * g + h, :], t_kf, fr, inc=(i == 3))
                    give(b, evac(dst[0:96, h, :], bk[0:96, :], t, pe.last()))
            t_T = [A.last(), V.last()]
            units = []
            for i in range(4):
                n = (i + 1) * P
                units.append(dict(n=n, scale=float(MSCALE), tok=t_T, mask=k_("causal")[:, 512 - n:512], otok=t_kf,
                                  q=[QTh[0:96, h, i * P:(i + 1) * P] for h in range(4)],
                                  k=[KTh[0:96, h, 0:n] for h in range(4)],
                                  v=[[VV[:, kt, 4 * g + h, :] for kt in range(i + 1)] for h in range(4)],
                                  o=YM[:, i, 256 * g:256 * g + 256].rearrange("p (h d) -> p h d", h=4)))
            t_ym = attention(units, allb)
        if dump("ym", YM, t_ym):
            return finish()
        t_yt = out_T(lambda i, k: YM[:, i, k * P:(k + 1) * P], 4, YMT, [t_ym])

        SG = at(12928, 2048).rearrange("p (b t) -> p b t", b=4)
        sgn = 0
        for h in range(2):
            sb_, slb, t_wb = ring.take()
            wb = [slot_w(512, 0, 4)(slb), slot_w(512, 2048, 4)(slb)]
            for q in range(2):
                s, slot, t_w = ring.take()
                wg = [slot_w(256)(slot), slot_w(256, 2048)(slot)]
                for c in range(2):
                    jj = 2 * q + c
                    prods = []
                    for br, (src, tk) in enumerate(((YR, t_yr), (YMT, t_yt))):
                        b, bk, fr = allb.take()
                        for k in range(8):
                            t = mm(bk[:, :], wg[br][:, k, c * P:(c + 1) * P], HT[:, k, :], k == 0, k == 7, t_w, fr)
                        x = sgn % 4
                        sgn += 1
                        t1 = A.do(lambda e, x=x, bk=bk: e.activation(SG[:, x, :], bk[:, :], ACT.Tanh, scale=0.5), t,
                                  V.last())
                        give(b, t1)
                        b, bk2, fr = allb.take()
                        for k in range(4):
                            t = mm(bk2[:, :], wb[br][:, k, jj * P:(jj + 1) * P], src[:, k, :], k == 0, k == 3, t_wb, tk, fr)
                        t2 = V.do(lambda e, x=x, bk2=bk2: e.scalar_tensor_tensor(SG[:, x, :], SG[:, x, :], 1.0, bk2[:, :],
                                                                                 ALU.add, ALU.mult), t1, t)
                        give(b, t2)
                        prods.append(x)
                    V.do(lambda e, p_=tuple(prods): e.tensor_tensor(SG[:, p_[1], :], SG[:, p_[0], :], SG[:, p_[1], :],
                                                                   ALU.add))
                    t_m = V.do(lambda e, p_=tuple(prods), f=4 * h + jj: e.tensor_scalar(MT[:, f, :], SG[:, p_[1], :], 0.5,
                                                                                     None, ALU.mult))
                ring.done(s, t)
            ring.done(sb_, t)
        if dump("mt", MT, t_m):
            return finish()
        for h in range(2):
            gemm_tok(MT, 8, 512, lambda i, bk, t, h=h: V.do(lambda e: e.tensor_tensor(
                X[:, i, 512 * h:512 * h + 512], X[:, i, 512 * h:512 * h + 512], bk[:, :], ALU.add), t), t_m)
        xt = V.last()
        if dump("x2", X, xt):
            return finish()

        t_h, hns = norm_T(lambda i: X[:, i, :], NT, D, lambda i: T16[:, i, :], gcol("ffn_norm_g_2"), HT,
                          lambda i: xt, pe.last())
        d_hn = Dma("s_hn")
        hn_v = hn_scr.rearrange("(i p) d -> p i d", p=P)
        for i in range(NT):
            t_hn = d_hn.start(SP, hn_v[:, i, :], T16[:, i, :], hns[i])
        frow = load_row(I["final_norm_g_2"])
        RB = at(22016, 3072)
        rp = [0]

        def rbuf(n):
            rp[0] += n
            assert rp[0] <= 3072
            return RB[:, rp[0] - n:rp[0]]

        LG = rbuf(144).rearrange("p (i n) -> p i n", i=4)
        GL = rbuf(32).rearrange("p (i n) -> p i n", i=4)
        M8 = rbuf(32).rearrange("p (i n) -> p i n", i=4)
        I8 = rbuf(32).rearrange("p (i n) -> p i n", i=4)
        F8 = rbuf(32).rearrange("p (i n) -> p i n", i=4)
        OG = rbuf(16).rearrange("p (i n) -> p i n", i=4)
        OM = rbuf(16).rearrange("p (i n) -> p i n", i=4)
        EG = rbuf(16).rearrange("p (i n) -> p i n", i=4)
        N8 = rbuf(32).rearrange("p (i n) -> p i n", i=4)
        J8 = rbuf(32).rearrange("p (i n) -> p i n", i=4)
        K8 = rbuf(32).rearrange("p (i n) -> p i n", i=4)
        FMk = rbuf(128).rearrange("p (i n) -> p i n", i=4)
        OH = [rbuf(128).rearrange("p (i n) -> p i n", i=4) for _ in range(2)]
        MM_ = rbuf(128).rearrange("p (i n) -> p i n", i=4)
        POS = rbuf(128).rearrange("p (i n) -> p i n", i=4)
        TQ = rbuf(128).rearrange("p (i n) -> p i n", i=4)
        CNT, NBK, END, STA = rbuf(32), rbuf(32), rbuf(32), rbuf(32)
        OHP = [rbuf(128) for _ in range(2)]
        OHB = [rbuf(40) for _ in range(2)]
        EB = rbuf(1248)
        ng, sg, gg, e2, w1, w2, dn = [small(4) for _ in range(7)]
        pq = [[small(4) for _ in range(4)] for _ in range(2)]
        slotu = [small(4), small(4)]
        IDX = small(40)
        ebf, ebi = small(40), small(40)

        b, bk, fr = allb.take()
        for i in range(NT):
            for k in range(8):
                t = mm(bk[:, i * 36:i * 36 + 36], HT[:, k, i * P:(i + 1) * P], rw[:, k, :], k == 0, k == 7, t_h, t_small,
                       fr, inc=(i == 3 and k == 7))
        V.do(lambda e, bk=bk: e.tensor_tensor(LG, bk[:, 0:144].rearrange("p (i n) -> p i n", i=4),
                                              rb.unsqueeze(1).broadcast_to((P, 4, 36)), ALU.add), t)
        give(b, V.last())
        V.do(lambda e: e.memset(GL, 2 * NEG))
        V.do(lambda e: e.tensor_copy(GL[:, :, 0:4], LG[:, :, 0:4]))
        for i in range(NT):
            V.do(lambda e, i=i: e.max(M8[:, i, :], GL[:, i, :]))
            V.do(lambda e, i=i: e.max_index(I8[:, i, :].bitcast(U32), M8[:, i, :], GL[:, i, :]))
        V.do(lambda e: e.tensor_copy(F8, I8.bitcast(U32)))
        t1 = V.do(lambda e: e.tensor_scalar(ng, M8[:, :, 0], -1.0, None, ALU.mult))
        for i in range(NT):
            t2 = A.do(lambda e, i=i: e.activation(EG[:, i, :], LG[:, i, 0:4], ACT.Exp, bias=ng[:, i:i + 1],
                                                  accum_out=sg[:, i:i + 1]), t1)
        V.do(lambda e: e.reciprocal(gg, sg), t2)
        i4 = k_("iota")[:, 0:4].unsqueeze(1).broadcast_to((P, 4, 4))
        V.do(lambda e: e.tensor_tensor(OG, i4, F8[:, :, 0:1].broadcast_to((P, 4, 4)), ALU.is_equal))
        V.do(lambda e: e.tensor_scalar(OM, OG, 1.0, -NEG, ALU.subtract, ALU.mult))
        f4 = lambda ap: ap.rearrange("p i (g n) -> p i g n", g=4)
        gb4 = lambda ap: ap.unsqueeze(3).broadcast_to((P, 4, 4, 8))
        V.do(lambda e: e.tensor_tensor(f4(FMk), f4(LG[:, :, 4:36]), gb4(OG), ALU.mult))
        V.do(lambda e: e.tensor_tensor(f4(FMk), f4(FMk), gb4(OM), ALU.add))
        for i in range(NT):
            V.do(lambda e, i=i: e.max(N8[:, i, :], FMk[:, i, :]))
            V.do(lambda e, i=i: e.max_index(J8[:, i, :].bitcast(U32), N8[:, i, :], FMk[:, i, :]))
        V.do(lambda e: e.tensor_copy(K8, J8.bitcast(U32)))
        t1 = V.do(lambda e: e.tensor_tensor(dn, N8[:, :, 1], N8[:, :, 0], ALU.subtract))
        t1 = A.do(lambda e: e.activation(e2, dn, ACT.Exp), t1)
        V.do(lambda e: e.tensor_scalar(w1, e2, 1.0, None, ALU.add), t1)
        V.do(lambda e: e.reciprocal(w1, w1))
        V.do(lambda e: e.tensor_tensor(w1, w1, gg, ALU.mult))
        V.do(lambda e: e.tensor_tensor(w2, w1, e2, ALU.mult))
        i32_ = k_("iota")[:, 0:32].unsqueeze(1).broadcast_to((P, 4, 32))
        for q in range(2):
            V.do(lambda e, q=q: e.tensor_tensor(OH[q], i32_, K8[:, :, q:q + 1].broadcast_to((P, 4, 32)), ALU.is_equal))
        t1 = V.do(lambda e: e.tensor_tensor(MM_, OH[0], OH[1], ALU.add))
        b, bk, fr = allb.take()
        for i in range(NT):
            for i2 in range(i):
                mm(bk[:, i * 32:i * 32 + 32], k_("ones"), MM_[:, i2, :], i2 == 0, False, t1, fr)
            mm(bk[:, i * 32:i * 32 + 32], k_("triu"), MM_[:, i, :], i == 0, True, t1, fr, inc=False)
        for i in range(NT):
            t = mm(bk[:, 128:160], k_("ones"), MM_[:, i, :], i == 0, i == 3)
        V.do(lambda e, bk=bk: e.tensor_copy(POS, bk[:, 0:128].rearrange("p (i n) -> p i n", i=4)), t)
        V.do(lambda e, bk=bk: e.tensor_copy(CNT, bk[:, 128:160]))
        give(b, V.last())
        V.do(lambda e: e.tensor_scalar(NBK, CNT, 0.0, None, ALU.is_gt))
        for c_ in (128.0, 256.0, 384.0):
            V.do(lambda e, c_=c_: e.scalar_tensor_tensor(NBK, CNT, c_, NBK, ALU.is_gt, ALU.add))
        V.do(lambda e: e.tensor_tensor_scan(END, k_("ones")[:, 0:32], NBK, 0.0, ALU.mult, ALU.add))
        V.do(lambda e: e.tensor_tensor(STA, END, NBK, ALU.subtract))
        EB3 = EB[0:1, :].rearrange("p (b n) -> p b n", b=NB)
        V.do(lambda e: e.tensor_tensor(EB3, END[0:1, :].unsqueeze(1).broadcast_to((1, NB, 32)),
                                       k_("iota")[0:1, 0:NB].unsqueeze(2).broadcast_to((1, NB, 32)), ALU.is_le))
        V.do(lambda e: e.tensor_reduce(ebf[0:1, 0:NB], EB3, AX, ALU.add))
        V.do(lambda e: e.tensor_scalar(ebf[0:1, 0:NB], ebf[0:1, 0:NB], 31.0, None, ALU.min))
        t_eb = V.do(lambda e: e.tensor_copy(ebi[0:1, 0:NB].bitcast(I32), ebf[0:1, 0:NB]))
        for q in range(2):
            ps_, sq_, gq, bq_ = pq[q]
            V.do(lambda e, q=q: e.tensor_tensor(TQ, OH[q], POS, ALU.mult))
            V.do(lambda e, ps_=ps_: e.tensor_reduce(ps_, TQ, AX, ALU.add))
            V.do(lambda e, q=q: e.tensor_tensor(TQ, OH[q], STA.unsqueeze(1).broadcast_to((P, 4, 32)), ALU.mult))
            V.do(lambda e, sq_=sq_: e.tensor_reduce(sq_, TQ, AX, ALU.add))
            V.do(lambda e, gq=gq, ps_=ps_: e.tensor_scalar(gq, ps_, 128.0, None, ALU.is_ge))
            for c_ in (256.0, 384.0):
                V.do(lambda e, c_=c_, gq=gq, ps_=ps_: e.scalar_tensor_tensor(gq, ps_, c_, gq, ALU.is_ge, ALU.add))
            V.do(lambda e, gq=gq, sq_=sq_, bq_=bq_: e.tensor_tensor(bq_, sq_, gq, ALU.add))
            V.do(lambda e, gq=gq, ps_=ps_: e.scalar_tensor_tensor(ps_, gq, -128.0, ps_, ALU.mult, ALU.add))
            V.do(lambda e, gq=gq, bq_=bq_, ps_=ps_: e.scalar_tensor_tensor(gq, bq_, 128.0, ps_, ALU.mult, ALU.add))
            t_slot = V.do(lambda e, gq=gq, q=q: e.tensor_copy(slotu[q].bitcast(U32), gq))
        b, bk, fr = allb.take()
        for q in range(2):
            for i in range(NT):
                ps_, sq_, gq, bq_ = pq[q]
                x = i % 2
                V.do(lambda e, x=x, i=i, ps_=ps_: e.tensor_scalar(OHP[x], k_("iota"), ps_[:, i:i + 1], None, ALU.is_equal),
                     pe.last())
                t1 = V.do(lambda e, x=x, i=i, bq_=bq_: e.tensor_scalar(OHB[x][:, 0:NB], k_("iota")[:, 0:NB], bq_[:, i:i + 1],
                                                                       k_("tokid")[:, i:i + 1], ALU.is_equal, ALU.mult))
                t = mm(bk[:, 0:NB], OHP[x], OHB[x][:, 0:NB], q == 0 and i == 0, q == 1 and i == 3, t1, fr, inc=True)
        t_idx = V.do(lambda e, bk=bk: e.tensor_copy(IDX[:, 0:NB].bitcast(U32), bk[:, 0:NB]), t)
        give(b, t_idx)
        if dump("slots", slotu[0].bitcast(F32), t_idx):
            return finish()

        ms_sem = [Dma(f"s_moe{i}") for i in range(4)]
        mslot = [RINGC[:, 0:6144], RINGC[:, 6144:12288], at(4096, 6144), at(10240, 6144)]
        XG = [at(16384 + 1024 * q, 1024) for q in range(3)]
        YB = [at(19456, 1024), at(0, 1024)]
        XTm = [at(1024 + 1024 * q, 1024).rearrange("p (k t) -> p k t", k=8) for q in range(2)]
        ACTB = [at(20480 + 256 * q, 256) for q in range(2)]
        AT_ = [at(20992 + 256 * q, 256).rearrange("p (k t) -> p k t", k=2) for q in range(2)]
        THm = [at(21504 + 256 * q, 256) for q in range(2)]
        gat_sem = [Dma(f"s_gat{i}") for i in range(3)]
        yst_sem = [Dma(f"s_yst{i}") for i in range(2)]
        fg = gcol("ffn_norm_g_2")
        Wgu, Wdn = I["moe_w_gu_2"][0], I["moe_w_down_2"][0]
        before = [pe.last(), V.last(), A.last(), t_hn]
        moe_free = [None] * 4
        down_done, gath_done, ysto = {}, {}, [None, None]
        wl, gl = {}, {}

        def load_w(n):
            x = n % 4
            SP.wait(t_eb, before if n < 4 else None, down_done.get(n - 4))
            ms_sem[x].n += 32
            s = mslot[x]

            def go(e, n=n, x=x, s=s):
                r = e.value_load(ebi[0:1, n:n + 1].bitcast(I32), min_val=0, max_val=31)
                gsrc = Wgu[bass.ds(r, 1), :, :].rearrange("o (k p) n -> p (o k) n", p=P)
                dsrc = Wdn[bass.ds(r, 1), :, :].rearrange("o (k p) n -> p (o k) n", p=P)
                e.dma_start(s[:, 0:4096].rearrange("p (k n) -> p k n", k=8), gsrc).then_inc(ms_sem[x].sem, 16)
                e.dma_start(s[:, 4096:6144].rearrange("p (k n) -> p k n", k=2), dsrc).then_inc(ms_sem[x].sem, 16)

            SP.items.append(go)
            wl[n] = (ms_sem[x].sem, ms_sem[x].n)

        def gather(n):
            x = n % 3
            G.wait(t_hn, t_idx, before if n < 3 else None, gath_done.get(n - 3))
            gat_sem[x].n += 16
            G.items.append(lambda e, n=n, x=x: e.indirect_dma_start(
                XG[x], None, hn_scr, bass.IndirectOffsetOnAxis(ap=IDX[:, n:n + 1].bitcast(U32), axis=0))
                .then_inc(gat_sem[x].sem, 16))
            gl[n] = (gat_sem[x].sem, gat_sem[x].n)

        def x_T(n):
            xg, x = XG[n % 3], XTm[n % 2]
            for hf in range(2):
                b, bk, fr = allb.take()
                for k in range(4):
                    t = tr(bk[:, k * P:(k + 1) * P], xg[:, (4 * hf + k) * P:(4 * hf + k + 1) * P], gl[n], fr, inc=(k == 3))
                t1 = V.free(lambda e, bk=bk, hf=hf, x=x: e.tensor_tensor(
                    x[:, 4 * hf:4 * hf + 4, :], bk[:, :].rearrange("p (k t) -> p k t", k=4),
                    fg[:, 4 * hf:4 * hf + 4].unsqueeze(2).broadcast_to((P, 4, P)), ALU.mult), t, before if n < 2 else None)
                give(b, t1)
            gath_done[n] = t
            return t1

        def up(n, t_x_):
            b, bk, fr = allb.take()
            w = mslot[n % 4][:, 0:4096].rearrange("p (k n) -> p k n", k=8)
            for k in range(8):
                t = mm(bk[:, :], XTm[n % 2][:, k, :], w[:, k, :], k == 0, k == 7, t_x_, wl[n], fr)
            a, th_ = ACTB[n % 2], THm[n % 2]
            t1 = A.free(lambda e: e.activation(th_, bk[:, 0:256], ACT.Tanh, scale=0.5), t, V.last())
            t2 = V.do(lambda e: e.scalar_tensor_tensor(th_, th_, 1.0, bk[:, 0:256], ALU.add, ALU.mult), t1)
            t3 = V.do(lambda e: e.scalar_tensor_tensor(a, th_, 0.5, bk[:, 256:512], ALU.mult, ALU.mult), pe.last())
            give(b, t3)
            return t3

        def down(n, t_a):
            b, bk, fr = allb.take()
            a, aT = ACTB[n % 2], AT_[n % 2]
            for k in range(2):
                t = tr(bk[:, k * P:(k + 1) * P], a[:, k * P:(k + 1) * P], t_a, fr, inc=(k == 1))
            t1 = A.free(lambda e: e.activation(aT, bk[:, 0:256].rearrange("p (k t) -> p k t", k=2), ACT.Copy), t)
            give(b, t1)
            w = mslot[n % 4][:, 4096:6144].rearrange("p (k n) -> p k n", k=2)
            yb = YB[n % 2]
            for h in range(2):
                b, bk2, fr = allb.take()
                for k in range(2):
                    t = mm(bk2[:, :], aT[:, k, :], w[:, k, 512 * h:512 * h + 512], k == 0, k == 1, t1, wl[n], fr)
                if h == 0:
                    t2 = A.free(lambda e, bk2=bk2: e.activation(yb[:, 0:512], bk2[:, :], ACT.Copy), t, ysto[n % 2])
                else:
                    t2 = V.free(lambda e, bk2=bk2: e.tensor_copy(yb[:, 512:1024], bk2[:, :]), t, ysto[n % 2])
                give(b, t2)
            down_done[n] = t
            ysto[n % 2] = yst_sem[n % 2].start(A, y_scr[n * P:(n + 1) * P, :], yb, A.last(), t2)

        for n in range(3):
            load_w(n)
            gather(n)
        load_w(3)
        t_x1 = x_T(0)
        t_a1 = up(0, t_x1)
        for n in range(NB):
            if n + 1 < NB:
                t_x1 = x_T(n + 1)
                if n + 3 < NB:
                    gather(n + 3)
                t_a2 = up(n + 1, t_x1)
            down(n, t_a1)
            if n + 4 < NB:
                load_w(n + 4)
            t_a1 = t_a2

        YG = [at(4096 + 1024 * q, 1024) for q in range(8)]
        y_sem = [Dma(f"s_yg{i}") for i in range(8)]
        tg = {}
        for i in range(NT):
            for q in range(2):
                x = 2 * i + q
                G.wait(ysto, pe.last())
                y_sem[x].n += 16
                G.items.append(lambda e, i=i, q=q, x=x: e.indirect_dma_start(
                    YG[x], None, y_scr, bass.IndirectOffsetOnAxis(ap=slotu[q][:, i:i + 1].bitcast(U32), axis=0))
                    .then_inc(y_sem[x].sem, 16))
                tg[x] = (y_sem[x].sem, y_sem[x].n)
        out_v = out[0].rearrange("(i p) d -> p i d", p=P)
        rowb, t_row = frow
        ms, rs = NST[nst[0] % 2]
        for i in range(NT):
            V.do(lambda e, i=i: e.scalar_tensor_tensor(X[:, i, :], YG[2 * i], w1[:, i:i + 1], X[:, i, :], ALU.mult, ALU.add),
                 tg[2 * i])
            t = V.do(lambda e, i=i: e.scalar_tensor_tensor(X[:, i, :], YG[2 * i + 1], w2[:, i:i + 1], X[:, i, :],
                                                           ALU.mult, ALU.add), tg[2 * i + 1])
            t1 = A.do(lambda e, i=i: e.activation(YG[2 * i], X[:, i, :], ACT.Square, scale=1 / 32.0,
                                                  accum_out=ms[:, i:i + 1]), t)
            t2 = rsqrt4(rs[:, i:i + 1], ms[:, i:i + 1], 1, eps6, t1)
            t3 = V.do(lambda e, i=i: e.scalar_tensor_tensor(X[:, i, :], X[:, i, :], rs[:, i:i + 1], ROW[:, rowb, :],
                                                            ALU.mult, ALU.mult), t2, t_row)
            d = Dma(f"s_out{i}")
            stores.append(d.start(SP, out_v[:, i, :], X[:, i, :], t3))
        return finish()


_INS = ["x", "mem", "mem_norm_g", "w_in", "w_mem_kv", "w_o", "g_mix_pre", "g_mix_post", "attn_sink", "qk_norm_g",
        "w_gate_up", "w_down", "g_ffn_pre", "g_ffn_post", "positions_2", "mix_norm_g_2", "w_in_2", "rw_mu_2",
        "rw_w0_2", "rw_w_up_2", "rw_a0_2", "rw_a_up_2", "rw_g_up_2", "rw_k_k_2", "rw_k_a_2", "rw_r_k_2", "rw_gn_w_2",
        "rw_gn_b_2", "mla_g_qa_2", "mla_w_q_up_2", "mla_g_kva_2", "mla_w_kv_up_2", "w_branch_rw_2",
        "w_branch_mla_2", "w_out_2", "ffn_norm_g_2", "moe_w_group_2", "moe_b_group_2", "moe_w_router_2",
        "moe_b_router_2", "moe_w_gu_2", "moe_w_down_2", "final_norm_g_2"]


def kernel(**inputs):
    import concourse.bacc as bacc
    from concourse.bass_utils import run_bass_kernel_spmd

    nc = bacc.Bacc("TRN2", target_bir_lowering=False, num_devices=1)
    arrays, aps = {}, {}
    for name in _INS:
        a = np.ascontiguousarray(inputs[name])
        arrays[f"in_{name}"] = a
        aps[name] = nc.dram_tensor(f"in_{name}", a.shape, mybir.dt.from_np(a.dtype), kind="ExternalInput").ap()
    table = const_table()
    arrays["tables"] = table
    consts = nc.dram_tensor("tables", table.shape, F32, kind="ExternalInput").ap()
    out = nc.dram_tensor("out_0", (1, S, D), F32, kind="ExternalOutput").ap()
    hn_scr = nc.dram_tensor("hn_scr", (S, D), F32).ap()
    y_scr = nc.dram_tensor("y_scr", (NB * P, D), F32).ap()
    build(nc, aps, out, hn_scr, y_scr, consts)
    r = run_bass_kernel_spmd(nc, [arrays], core_ids=[0])
    return r.results[0]["out_0"]
```

```python
from contextlib import ExitStack

import numpy as np
import concourse.bass as bass
from concourse import mybir

F32 = mybir.dt.float32
I32 = mybir.dt.int32
F32R = mybir.dt.float32r
U32 = mybir.dt.uint32
ALU = mybir.AluOpType
ACT = mybir.ActivationFunctionType
AX = mybir.AxisListType.X

P = 128
NT = 4
S = 512
D = 1024
NB = 39
SLOT = 4096
NEG = -1.0e30
SCALE = 64 ** -0.5
MSCALE = 1.0 / np.sqrt(96.0)

CONST = {}


def const_table():
    parts, at = [], [0]

    def put(name, a):
        a = np.asarray(a, np.float32)
        if a.ndim == 1:
            a = np.broadcast_to(a[None, :], (P, a.shape[0]))
        a = a.reshape(P, -1)
        CONST[name] = (at[0], at[0] + a.shape[1])
        at[0] += a.shape[1]
        parts.append(a)

    p = np.arange(P)
    s, t = p[:, None], p[None, :]
    put("ident", np.eye(P))
    put("bones", (s // 64 == t // 64))
    put("bmean", (s // 64 == t // 64) / 64.0)
    put("ident64", (s % 64 == np.arange(64)[None, :]))
    put("ones", np.ones((P, P)))
    put("triu", s < t)
    band = np.zeros((P, 384), np.float32)
    band[:, 0:128] = np.where(t >= s, 0.0, NEG)
    band[:, 256:384] = np.where(t <= s, 0.0, NEG)
    put("band", band)
    causal = np.zeros((P, 512), np.float32)
    causal[:, 384:] = np.where(t <= s, 0.0, NEG)
    put("causal", causal)
    same = s // 64 == t // 64
    strict, incl = same & (t > s), same & (t >= s)
    put("mgram", np.concatenate([strict, incl, strict, incl], 1))
    up = lambda n: (s // (2 * n) == t // (2 * n)) & (s % (2 * n) < n) & (t % (2 * n) >= n)
    put("low1", up(1).T)
    for n in (1, 2, 4, 8, 16, 32):
        put(f"up{n}", up(n))
    tok = np.arange(S).reshape(NT, P).T

    def angles(pos, dims, theta):
        inv = (theta ** (-(np.arange(0, dims, 2, dtype=np.float32) / np.float32(dims)))).astype(np.float32)
        return pos.astype(np.float32)[..., None] * inv

    a = angles(tok, 16, 500000.0)
    put("cosp", np.cos(a))
    put("sinp", np.sin(a))
    a = np.stack([angles(tok // 64, 32, 10000.0), angles(tok % 64, 32, 10000.0)], 2)
    put("cosx", np.cos(a))
    put("sinx", np.sin(a))
    put("invf", (np.float32(10000.0) ** (-np.arange(0, 32, 2, dtype=np.float32) / np.float32(32))).astype(np.float32))
    put("iota", np.arange(128))
    put("tokid", tok)
    put("keep", np.arange(S) % 64 != 0)
    return np.concatenate(parts, 1)


const_table()
NCONST = max(b for _, b in CONST.values())

GROWS = [("mem_norm_g", 0, 8), ("g_mix_pre", 0, 8), ("g_mix_pre", 1, 8), ("g_ffn_pre", 0, 8), ("g_ffn_pre", 1, 8),
         ("mix_norm_g_2", 0, 8), ("ffn_norm_g_2", 0, 8), ("rw_mu_2", 0, 14), ("rw_w0_2", 0, 4), ("rw_a0_2", 0, 4),
         ("rw_k_k_2", 0, 4), ("rw_k_a_2", 0, 4), ("rw_r_k_2", 0, 4), ("rw_gn_w_2", 0, 4), ("rw_gn_b_2", 0, 4),
         ("mla_g_qa_2", 0, 3), ("mla_g_kva_2", 0, 2)]


class Lane:

    def __init__(self, sem, chain):
        self.sem, self.chain, self.n, self.items, self.seen = sem, chain, 0, [], {}

    def wait(self, *toks):
        for t in toks:
            if t is None:
                continue
            if isinstance(t, list):
                self.wait(*t)
                continue
            sem, val = t
            if self.seen.get(sem.num, 0) < val:
                self.seen[sem.num] = val
                self.items.append(lambda e, sem=sem, val=val: e.wait_ge(sem, val))

    def do(self, fn, *toks):
        self.wait(*toks)
        if self.chain and self.n:
            self.wait((self.sem, self.n))
        self.n += 1
        self.items.append(lambda e: fn(e).then_inc(self.sem, 1))
        return (self.sem, self.n)

    def free(self, fn, *toks):
        self.wait(*toks)
        self.n += 1
        self.items.append(lambda e: fn(e).then_inc(self.sem, 1))
        return (self.sem, self.n)

    def quiet(self, fn, *toks):
        self.wait(*toks)
        self.items.append(lambda e: fn(e))

    def last(self):
        return (self.sem, self.n) if self.n else None

    def play(self, e):
        for f in self.items:
            f(e)


def build(nc, I, out, hn_scr, y_scr, x_scr, consts, dbg=None, stop=None):
    with ExitStack() as ctx:
        sem = lambda n: ctx.enter_context(nc.semaphore(n))
        pe = Lane(sem("s_pe"), False)
        V = Lane(sem("s_dve"), True)
        A = Lane(sem("s_act"), True)
        G = Lane(sem("s_pool"), True)
        SP = Lane(sem("s_sp"), False)
        stores = []

        class Dma:

            def __init__(self, name):
                self.sem, self.n = sem(name), 0

            def start(self, lane, out_, in_, *toks, **kw):
                self.n += 16
                lane.wait(*toks)
                lane.items.append(lambda e: e.dma_start(out_, in_, **kw).then_inc(self.sem, 16))
                return (self.sem, self.n)

        AR_N = 53200
        arena_at = -(-nc.sbuf_base // 32) * 32
        arena = ctx.enter_context(nc.sbuf_tensor("arena", [P, AR_N], F32))
        banks = [ctx.enter_context(nc.psum_tensor(f"ps{i}", [P, 512], F32)) for i in range(8)]
        top = [0]

        def col(n):
            a = top[0]
            top[0] += n
            assert top[0] <= AR_N, top[0]
            return arena[:, a:a + n]

        def rounded(name, c0, n):
            return nc.alloc_sbuf_tensor_at(name, [P, n], F32R, offset=arena_at + 4 * c0)[:, :]

        X = col(4096).rearrange("p (i d) -> p i d", i=NT)
        HT = col(4096).rearrange("p (k t) -> p k t", k=8)
        RINGC = col(3 * SLOT)
        C = col(NCONST)
        k_ = lambda n: C[:, CONST[n][0]:CONST[n][1]]
        GC = col(103)
        goff, o_ = {}, 0
        for name, l, n in GROWS:
            goff[(name, l)] = o_
            o_ += n
        gcol = lambda name, l=0: GC[:, goff[(name, l)]:]
        st = col(900)
        stp = [0]

        def small(n):
            a = stp[0]
            stp[0] += n
            assert stp[0] <= 900
            return st[:, a:a + n]

        base = top[0]
        ident = k_("ident")

        class Banks:

            free_after = [None] * 8

            def __init__(self, ids):
                self.ids, self.at = list(ids), 0

            def take(self):
                b = self.ids[self.at % len(self.ids)]
                self.at += 1
                w = Banks.free_after[b]
                assert w != "held", b
                Banks.free_after[b] = "held"
                return b, banks[b], w

        def give(b, *toks):
            Banks.free_after[b] = list(toks)

        allb = Banks(range(8))

        def mm(o, l, r, start, stop_, *toks, inc=None):
            f = lambda e: e.matmul(o, l, r, start=start, stop=stop_, skip_group_check=True)
            return (pe.do if (stop_ if inc is None else inc) else pe.quiet)(f, *toks)

        def tr(o, i, *toks, inc=True):
            n = i.shape[0]
            f = lambda e: e.transpose(o, i, ident[0:n, 0:n])
            return (pe.do if inc else pe.quiet)(f, *toks)

        ring_sem = [Dma(f"s_ring{i}") for i in range(3)]
        jobs = []

        def job(*parts):
            jobs.append(parts)

        def w3(ap, k0, k1, c0, c1):
            return ap[k0 * P:k1 * P, c0:c1].rearrange("(k p) n -> p k n", p=P)

        def slot_w(n, off=0, k=8):
            return lambda s: s[:, off:off + k * n].rearrange("p (k n) -> p k n", n=n)

        for l in range(2):
            job((slot_w(512), w3(I["w_mem_kv"][l], 0, 8, 0, 512)))
            for c0, n in ((0, 512), (512, 512), (1024, 384)):
                job((slot_w(n), w3(I["w_in"][l], 0, 8, c0, c0 + n)))
            for h in range(2):
                job((slot_w(512), w3(I["w_o"][l], 0, 8, 512 * h, 512 * h + 512)))
            for c in range(11):
                job((slot_w(256), w3(I["w_gate_up"][l], 0, 8, 256 * c, 256 * c + 256)),
                    (slot_w(256, 2048), w3(I["w_gate_up"][l], 0, 8, 2816 + 256 * c, 3072 + 256 * c)))
            for h in range(2):
                for k0, k1 in ((0, 8), (8, 16), (16, 22)):
                    job((slot_w(512, 0, k1 - k0), w3(I["w_down"][l], k0, k1, 512 * h, 512 * h + 512)))
        W2 = I["w_in_2"][0]
        for c0, n in ((0, 512), (512, 512), (1024, 512), (1536, 256)):
            job((slot_w(n), w3(W2, 0, 8, c0, c0 + n)))
        job((lambda s: s[0:64, 0:512], I["rw_w_up_2"][0]), (lambda s: s[64:128, 0:512], I["rw_a_up_2"][0]),
            (lambda s: s[:, 512:1024], I["rw_g_up_2"][0]))
        job((slot_w(384), w3(W2, 0, 8, 1792, 2176)))
        job((slot_w(288), w3(W2, 0, 8, 2176, 2464)))
        job((slot_w(768, 0, 3), w3(I["mla_w_q_up_2"][0], 0, 3, 0, 768)))
        job((slot_w(1024, 0, 2), w3(I["mla_w_kv_up_2"][0], 0, 2, 0, 1024)))
        for h in range(2):
            job((slot_w(512, 0, 4), w3(I["w_branch_rw_2"][0], 0, 4, 512 * h, 512 * h + 512)),
                (slot_w(512, 2048, 4), w3(I["w_branch_mla_2"][0], 0, 4, 512 * h, 512 * h + 512)))
            for q in range(2):
                c0 = 512 * h + 256 * q
                job((slot_w(256), w3(W2, 0, 8, 2464 + c0, 2720 + c0)),
                    (slot_w(256, 2048), w3(W2, 0, 8, 3488 + c0, 3744 + c0)))
        for h in range(2):
            job((slot_w(512), w3(I["w_out_2"][0], 0, 8, 512 * h, 512 * h + 512)))

        class Ring:
            def __init__(self):
                self.loaded, self.taken, self.landed = 0, 0, []
                self.after = {}

            def pump(self):
                while self.loaded < len(jobs) and (self.loaded < 3 or (self.loaded - 3) in self.after):
                    n = self.loaded
                    s = RINGC[:, (n % 3) * SLOT:(n % 3 + 1) * SLOT]
                    tok = None
                    for view, src in jobs[n]:
                        tok = ring_sem[n % 3].start(SP, view(s), src, self.after.get(n - 3))
                    self.landed.append(tok)
                    self.loaded += 1

            def take(self):
                n = self.taken
                self.taken += 1
                self.pump()
                return n, RINGC[:, (n % 3) * SLOT:(n % 3 + 1) * SLOT], self.landed[n]

            def done(self, n, tok):
                self.after[n] = tok
                self.pump()

        ring = Ring()

        dc, dx, dg, dr, drow = Dma("s_const"), Dma("s_x"), Dma("s_g"), Dma("s_small"), Dma("s_rows")
        t_c = dc.start(SP, C, consts)
        top[0] = U0 = -(-top[0] // 8) * 8
        T16 = col(4096).rearrange("p (i d) -> p i d", i=NT)
        U = col(12288)
        PB = col(2 * 2048).rearrange("p (b h n) -> p b h n", b=2, h=4)
        HL = [col(768) for _ in range(2)]
        MEMT = col(2048).rearrange("p (k m) -> p k m", k=8)
        KMS = rounded("KMS", top[0], 2048).rearrange("p (v h m) -> p v h m", v=2, h=4)
        col(2048)
        VM = col(512).rearrange("p (k m) -> p k m", k=2)
        ROW = col(1024)
        GR = HL[0][0:103, 0:128]

        memv = I["mem"][0].rearrange("(i p) d -> p i d", p=P)
        t_mem = dx.start(SP, T16[:, 0:2, :], memv)
        r0 = 0
        t_gr = None
        for name, l, n in GROWS:
            v = I[name]
            v = v.rearrange("(c q) -> c q", q=P) if name == "mem_norm_g" else (
                v[0].rearrange("h d -> (h d)").rearrange("(c q) -> c q", q=P) if name == "rw_r_k_2"
                else v[l].rearrange("(c q) -> c q", q=P))
            t_gr = dg.start(SP, GR[r0:r0 + n, :], v)
            r0 += n
        dxx = Dma("s_xx")
        t_x = dxx.start(SP, X, I["x"][0].rearrange("(i p) d -> p i d", p=P))
        ring.pump()
        sink = small(12)
        qkg = small(128)
        rb = small(36)
        rw = small(288).rearrange("p (k n) -> p k n", n=36)
        posi = small(4)
        dr.start(SP, sink, I["attn_sink"][0].partition_broadcast(P))
        dr.start(SP, qkg, I["qk_norm_g"][0].rearrange("a d -> (a d)").partition_broadcast(P))
        dr.start(SP, rb[:, 0:4], I["moe_b_group_2"][0].partition_broadcast(P))
        dr.start(SP, rb[:, 4:36], I["moe_b_router_2"][0].partition_broadcast(P))
        dr.start(SP, rw[:, :, 0:4], w3(I["moe_w_group_2"][0], 0, 8, 0, 4), allow_slow_non_contiguous=True)
        dr.start(SP, rw[:, :, 4:36], w3(I["moe_w_router_2"][0], 0, 8, 0, 32))
        t_small = dr.start(SP, posi.bitcast(I32), I["positions_2"][0].rearrange("(i p) -> p i", p=P),
                           allow_slow_non_contiguous=True)

        rowd = Dma("s_row")
        row_used = [None]

        def load_row(src):
            return rowd.start(SP, ROW, src.partition_broadcast(P), row_used[0])

        nhalf = small(8)
        eps6 = 1e-6
        t_nh = G.do(lambda e: e.memset(nhalf, -0.5))
        nsink = small(12)
        V.do(lambda e: e.tensor_scalar(nsink, sink, -1.0, None, ALU.mult), t_small)

        b, bk, w = allb.take()
        t = tr(bk[:, 0:103], GR, t_c, t_gr, w)
        t_gc = V.do(lambda e, bk=bk: e.tensor_copy(GC, bk[:, 0:103]), t)
        give(b, t_gc)

        junk = small(4)

        def rsqrt4(o, ms, n, eps, *toks):
            t1 = V.do(lambda e: e.tensor_scalar(ms, ms, eps, None, ALU.add), *toks)
            return G.do(lambda e: e.tensor_tensor(o, ms, nhalf[:, 0:n], ALU.pow), t1, t_nh)

        nst = [0]
        NST = [(small(4), small(4)) for _ in range(2)]

        def norm_T(src, ntile, D_, scr, g, dst, src_tok, dst_tok, keep=False):
            ms, rs = NST[nst[0] % 2]
            nst[0] += 1
            nk = D_ // P
            toks, hn = [], []
            for i in range(ntile):
                t1 = A.do(lambda e, i=i: e.activation(scr(i), src(i), ACT.Square, scale=float(D_ ** -0.5),
                                                      accum_out=ms[:, i:i + 1]), src_tok(i), dst_tok if i == 0 else None)
                t2 = rsqrt4(rs[:, i:i + 1], ms[:, i:i + 1], 1, eps6, t1)
                t3 = V.do(lambda e, i=i: e.tensor_scalar(scr(i), src(i), rs[:, i:i + 1], None, ALU.mult), t2)
                hn.append(t3)
                for k0 in range(0, nk, 4):
                    n = min(4, nk - k0)
                    b, bk, w = allb.take()
                    for k in range(n):
                        t4 = tr(bk[:, k * P:k * P + P], scr(i)[:, (k0 + k) * P:(k0 + k + 1) * P], t3, w, t_c)
                    o = dst[:, k0:k0 + n, i * P:(i + 1) * P]
                    iv = bk[:, 0:n * P].rearrange("p (k t) -> p k t", k=n)
                    gb = g[:, k0:k0 + n].unsqueeze(2).broadcast_to((P, n, P))
                    t5 = V.do(lambda e, o=o, iv=iv, gb=gb: e.tensor_tensor(o, iv, gb, ALU.mult), t4, t_gc, dst_tok)
                    give(b, t5)
                    toks.append(t5)
            return toks[-1], hn

        AST = [[small(4) for _ in range(5)] for _ in range(2)]
        un = [0]
        pv_done = [None, None]
        PTB = T16.rearrange("p i d -> p (i d)").rearrange("p (b k n) -> p b k n", b=2, k=4)
        pt_at = [(0, PTB[:, 0]), (1, PTB[:, 1])]
        pt_used = [None, None]

        def scores(u, bp):
            i = un[0] % 2
            un[0] += 1
            u["b"] = i
            mS, ngm, den, rden, ske = AST[i]
            n = u["n"]
            u["src"] = []
            for h in range(4):
                b, bk, w = bp.take()
                pairs = u["qk"](h)
                for z, (l_, r_) in enumerate(pairs):
                    t1 = mm(bk[:, 0:n], l_, r_, z == 0, z == len(pairs) - 1, w, u["tok"])
                if u.get("mask") is not None:
                    t2 = V.free(lambda e, h=h, bk=bk: e.tensor_tensor_reduce(
                        PB[:, i, h, 0:n], bk[:, 0:n], u["mask"], 1.0, -3.0e38, ALU.add, ALU.max, mS[:, h:h + 1]),
                        t1, pv_done[i], t_c)
                    give(b, t2)
                    u["src"].append((None, PB[:, i, h, 0:n]))
                else:
                    V.free(lambda e, h=h, bk=bk: e.tensor_reduce(mS[:, h:h + 1], bk[:, 0:n], AX, ALU.max),
                           t1, pv_done[i])
                    u["src"].append((b, bk[:, 0:n]))
            if u.get("sink") is not None:
                sl = slice(4 * u["sink"], 4 * u["sink"] + 4)
                u["m"] = V.do(lambda e: e.scalar_tensor_tensor(ngm, mS, -u["scale"], nsink[:, sl], ALU.mult, ALU.min))
                u["m"] = V.do(lambda e: e.tensor_tensor(ske, ngm, sink[:, sl], ALU.add))
            else:
                u["m"] = V.do(lambda e: e.tensor_scalar(ngm, mS, -u["scale"], None, ALU.mult))

        def exps(u):
            i, n = u["b"], u["n"]
            mS, ngm, den, rden, ske = AST[i]
            for h in range(4):
                b, src = u["src"][h]
                t4 = A.free(lambda e, h=h, src=src: e.activation(PB[:, i, h, 0:n], src, ACT.Exp, bias=ngm[:, h:h + 1],
                                                                 scale=u["scale"], accum_out=den[:, h:h + 1]),
                            u["m"], pv_done[i])
                if b is not None:
                    give(b, t4)
            if u.get("sink") is not None:
                t4 = A.free(lambda e: e.activation(ske, ske, ACT.Exp))
            u["e"] = t4

        def divide(u):
            i, n = u["b"], u["n"]
            mS, ngm, den, rden, ske = AST[i]
            if u.get("sink") is not None:
                V.do(lambda e: e.tensor_tensor(den, den, ske, ALU.add), u["e"])
            V.do(lambda e: e.reciprocal(rden, den), u["e"])
            V.wait(V.last())
            for h in range(4):
                ph = PB[:, i, h, 0:n]
                u["p"] = V.free(lambda e, h=h, ph=ph: e.tensor_scalar(ph, ph, rden[:, h:h + 1], None, ALU.mult))

        def turn(u, bp):
            i, n = u["b"], u["n"]
            z, pt = pt_at[i]
            u["t"] = []
            for k in range(n // P):
                b, bk, w = bp.take()
                for x, h in enumerate((0, 2, 1, 3)):
                    t1 = tr(bk[:, x * P:(x + 1) * P], PB[:, i, h, k * P:(k + 1) * P], u["p"], w, inc=(x == 3))
                cp = (lambda e, k=k, bk=bk: e.activation(pt[:, k, :], bk[:, :], ACT.Copy)) if k != 1 else (
                    lambda e, k=k, bk=bk: e.tensor_copy(pt[:, k, :], bk[:, :]))
                u["t"].append((A if k != 1 else V).free(cp, t1, pt_used[z]))
                give(b, u["t"][-1])
            pv_done[i] = t1

        def values(u, bp):
            z, pt = pt_at[u["b"]]
            b, bk, w = bp.take()
            t3 = u["pv"](bk, pt, u["t"], w)
            pt_used[z] = t3
            give(b, evac(u["o"], bk[:, 0:256].rearrange("p (m q) -> p m q", m=2), t3, u.get("otok")))

        def pv_shared(v):
            def go(bk, pt, t2s, w):
                for k in range(len(v)):
                    for r in range(2):
                        t = mm(bk[64 * r:64 * r + 64, 0:256], v[k], pt[:, k, 256 * r:256 * r + 256], k == 0,
                               k == len(v) - 1, t2s[k], w)
                return t
            return go

        def pv_own(v):
            def go(bk, pt, t2s, w):
                for h in range(4):
                    r, m = h % 2, h // 2
                    for k in range(len(v[h])):
                        t = mm(bk[64 * r:64 * r + 64, m * P:(m + 1) * P], v[h][k],
                               pt[:, k, (2 * r + m) * P:(2 * r + m + 1) * P], k == 0, k == len(v[h]) - 1, t2s[k], w)
                return t
            return go

        def attention(units, bp, before_scores=None):
            scores(units[0], bp)
            exps(units[0])
            for n, u in enumerate(units):
                divide(u)
                if n + 1 < len(units):
                    if before_scores:
                        before_scores(n + 1)
                    scores(units[n + 1], bp)
                turn(u, bp)
                if n + 1 < len(units):
                    exps(units[n + 1])
                values(u, bp)
            return [A.last(), V.last()]

        def rotate(dst1, dst2, x1, x2, c, s, t1, t2, *toks):
            V.do(lambda e: e.tensor_tensor(t1, x1, s, ALU.mult), *toks)
            V.do(lambda e: e.tensor_tensor(t2, x2, s, ALU.mult))
            V.do(lambda e: e.tensor_tensor(dst1, x1, c, ALU.mult))
            V.do(lambda e: e.tensor_tensor(dst2, x2, c, ALU.mult))
            V.do(lambda e: e.tensor_tensor(dst1, dst1, t2, ALU.subtract))
            return V.do(lambda e: e.tensor_tensor(dst2, dst2, t1, ALU.add))

        def split(hi, lo, src, *toks):
            V.do(lambda e: e.tensor_scalar(hi.bitcast(I32), src.bitcast(I32), -4096, None, ALU.bitwise_and), *toks)
            return V.do(lambda e: e.tensor_tensor(lo, src, hi, ALU.subtract))

        evn = [0]

        def evac(o, i, *toks):
            evn[0] += 1
            if evn[0] % 2:
                return A.free(lambda e: e.activation(o, i, ACT.Copy), *toks)
            return V.free(lambda e: e.tensor_copy(o, i), *toks)

        def gemm_tok(xT, nk, n, ev, *toks):
            s, slot, t_w = ring.take()
            w = slot_w(n, 0, nk)(slot)
            for i in range(NT):
                b, bk, fr = allb.take()
                for k in range(nk):
                    t = mm(bk[:, 0:n], xT[:, k, i * P:(i + 1) * P], w[:, k, :], k == 0, k == nk - 1, t_w, fr, *toks)
                give(b, ev(i, bk, t))
            ring.done(s, t)
            return t

        def out_T(src, nk, dst, stoks, *toks):
            for k in range(nk):
                b, bk, w = allb.take()
                for i in range(NT):
                    t = tr(bk[:, i * P:(i + 1) * P], src(i, k), w, stoks, inc=(i == 3))
                t2 = evac(dst[:, k, :], bk[:, :], t, *toks)
                give(b, t2)
            return [A.last(), V.last()]

        def post_norm(g_src, tg_, otoks):
            t_row = g_src
            ms, rs = NST[nst[0] % 2]
            nst[0] += 1
            for i in range(NT):
                t1 = A.do(lambda e, i=i: e.activation(U[:, i * 1024:(i + 1) * 1024], T16[:, i, :], ACT.Square,
                                                      scale=1 / 32.0, accum_out=ms[:, i:i + 1]), otoks)
                t2 = rsqrt4(rs[:, i:i + 1], ms[:, i:i + 1], 1, eps6, t1)
                V.do(lambda e, i=i: e.scalar_tensor_tensor(T16[:, i, :], T16[:, i, :], rs[:, i:i + 1], ROW,
                                                           ALU.mult, ALU.mult), t2, t_row)
                t3 = V.do(lambda e, i=i: e.tensor_tensor(X[:, i, :], X[:, i, :], T16[:, i, :], ALU.add), tg_)
            row_used[0] = t3
            return t3

        def dump(name, ap, *toks):
            if dbg is not None and name in dbg:
                d = Dma(f"s_dbg_{name}")
                stores.append(d.start(SP, dbg[name], ap, *toks))
                for q in (pe, V, A, G):
                    q.wait(stores[-1])
            return stop == name

        def finish():
            for t in stores:
                SP.wait(t)
            block = ctx.enter_context(nc.Block())

            @block.sync
            def _(e):
                SP.play(e)

            @block.tensor
            def _(e):
                pe.play(e)

            @block.vector
            def _(e):
                V.play(e)

            @block.scalar
            def _(e):
                A.play(e)

            @block.gpsimd
            def _(e):
                G.play(e)

        t_memT, _ = norm_T(lambda i: T16[:, i, :], 2, D, lambda i: T16[:, 2 + i, :], gcol("mem_norm_g"), MEMT,
                           lambda i: t_mem, None)

        xt = t_x
        for l in range(2):
            s, slot, t_w = ring.take()
            w = slot_w(512)(slot)
            KM = U[:, 0:512].rearrange("p (i m) -> p i m", i=2)
            for i in range(2):
                b, bk, fr = allb.take()
                for k in range(8):
                    t = mm(bk[:, :], MEMT[:, k, i * P:(i + 1) * P], w[:, k, :], k == 0, k == 7, t_w, t_memT, fr, xt)
                A.free(lambda e, bk=bk, i=i: e.activation(KM[:, i, :], bk[:, 0:256], ACT.Copy), t, xt)
                t2 = A.free(lambda e, bk=bk, i=i: e.activation(VM[:, i, :], bk[:, 256:512], ACT.Copy), t, pe.last())
                give(b, t2)
            ring.done(s, t)
            t_km = None
            for i in range(2):
                q = HL[0][:, 0:512].rearrange("p (v d) -> p v d", v=2)
                for hp in range(2):
                    kk_ = KM[:, i, 128 * hp:128 * hp + 128].rearrange("p (h d) -> p h d", h=2)
                    o4 = HL[0][:, 0:512].rearrange("p (v h r d) -> p v h r d", v=2, h=2, r=2)
                    for r in range(2):
                        split(o4[:, 0, :, r, :], o4[:, 1, :, r, :], kk_, t2, pe.last())
                    b, bk, fr = allb.take()
                    for x in range(4):
                        t = tr(bk[:, x * P:(x + 1) * P], HL[0][:, x * P:(x + 1) * P], V.last(), fr, inc=(x == 3))
                    ov = KMS[:, :, 2 * hp:2 * hp + 2, i * P:(i + 1) * P]
                    t_km = evac(ov, bk[:, :].rearrange("p (v h q) -> p v h q", v=2, h=2), t)
                    give(b, t_km)
            t_km = [A.last(), V.last()]

            t_h, _ = norm_T(lambda i: X[:, i, :], NT, D, lambda i: T16[:, i, :], gcol("g_mix_pre", l), HT,
                            lambda i: xt, [pe.last(), V.last()])
            QKV = U[:, 0:5632].rearrange("p (i n) -> p i n", i=NT)
            QST = rounded(f"QST{l}", U0 + 4096 + 5632, 4096).rearrange("p (b h t) -> p b h t", b=2, h=4)
            KST = rounded(f"KST{l}", U0 + 4096 + 9728, 2048).rearrange("p (b v t) -> p b v t", b=2, v=2)
            for c0, n in ((0, 512), (512, 512), (1024, 384)):
                gemm_tok(HT, 8, n, lambda i, bk, t, c0=c0, n=n: evac(QKV[:, i, c0:c0 + n], bk[:, 0:n], t, t_km, pe.last()),
                         t_h)
            t_q = [A.last(), V.last()]
            if dump(f"qkv{l}", QKV, *t_q):
                return finish()
            TM = U[:, 5632:6656]
            if l == 0:
                H15 = QKV[:, :, 0:960].rearrange("p i (h d) -> p i h d", d=64)
                x1, x2 = H15[:, :, :, 0:8], H15[:, :, :, 8:16]
                cb = k_("cosp").rearrange("p (i c) -> p i c", i=NT).unsqueeze(2).broadcast_to((P, NT, 15, 8))
                sb_ = k_("sinp").rearrange("p (i c) -> p i c", i=NT).unsqueeze(2).broadcast_to((P, NT, 15, 8))
                t1 = TM[:, 0:480].rearrange("p (i h c) -> p i h c", i=NT, c=8)
                t2 = TM[:, 480:960].rearrange("p (i h c) -> p i h c", i=NT, c=8)
                t_r = rotate(x1, x2, x1, x2, cb, sb_, t1, t2, t_q, t_c)
            else:
                for i in range(NT):
                    H = QKV[:, i, 0:960].rearrange("p (h d) -> p h d", d=64)
                    sq = PB[:, 0, 0:2, :].rearrange("p a n -> p (a n)")[:, 0:960].rearrange("p (h d) -> p h d", d=64)
                    ms = TM[:, 0:15]
                    rs = TM[:, 16:31]
                    V.do(lambda e, H=H, sq=sq: e.tensor_tensor(sq, H, H, ALU.mult), t_q, pv_done[0])
                    V.do(lambda e, ms=ms, sq=sq: e.tensor_reduce(ms, sq, AX, ALU.add))
                    V.do(lambda e, ms=ms: e.tensor_scalar(ms, ms, 1 / 64.0, eps6, ALU.mult, ALU.add))
                    t = A.do(lambda e, ms=ms: e.activation(ms, ms, ACT.Sqrt), V.last())
                    V.do(lambda e, ms=ms, rs=rs: e.reciprocal(rs, ms), t)
                    V.do(lambda e, H=H, rs=rs: e.tensor_tensor(H, H, rs.unsqueeze(2).broadcast_to((P, 15, 64)), ALU.mult))
                    V.do(lambda e, H=H: e.tensor_tensor(H[:, 0:12, :], H[:, 0:12, :],
                                                        qkg[:, 0:64].unsqueeze(1).broadcast_to((P, 12, 64)), ALU.mult))
                    V.do(lambda e, H=H: e.tensor_tensor(H[:, 12:15, :], H[:, 12:15, :],
                                                        qkg[:, 64:128].unsqueeze(1).broadcast_to((P, 3, 64)), ALU.mult))
                    G5 = QKV[:, i, 0:960].rearrange("p (h a b c) -> p h a b c", a=2, b=2, c=16)
                    cx = k_("cosx").rearrange("p (i a c) -> p i a c", i=NT, a=2)[:, i]
                    sx = k_("sinx").rearrange("p (i a c) -> p i a c", i=NT, a=2)[:, i]
                    T = [TM[:, 32:512].rearrange("p (h a c) -> p h a c", a=2, c=16),
                         TM[:, 512:992].rearrange("p (h a c) -> p h a c", a=2, c=16)]
                    t_r = rotate(G5[:, :, :, 0, :], G5[:, :, :, 1, :], G5[:, :, :, 0, :], G5[:, :, :, 1, :],
                                 cx.unsqueeze(1).broadcast_to((P, 15, 2, 16)), sx.unsqueeze(1).broadcast_to((P, 15, 2, 16)),
                                 *T)
            t_pre = [t_q, t_r, t_km]
            group_used = [None, None]

            def prepare(g):
                gb = g % 2
                for i in range(NT):
                    hl = HL[i % 2]
                    c0 = 256 * g if g < 3 else 1152
                    q4 = QKV[:, i, c0:c0 + 256].rearrange("p (h d) -> p h d", h=4)
                    o4 = hl[:, 0:512].rearrange("p (h v d) -> p h v d", h=4, v=2)
                    t = split(o4[:, :, 0, :], o4[:, :, 1, :], q4, t_pre, hl_used[i % 2])
                    b, bk, fr = allb.take()
                    for h in range(4):
                        t1 = tr(bk[:, h * P:(h + 1) * P], hl[:, h * P:(h + 1) * P], t, fr, inc=(h == 3))
                    give(b, evac(QST[:, gb, :, i * P:(i + 1) * P], bk[:, :].rearrange("p (h q) -> p h q", h=4), t1,
                                 group_used[gb]))
                    if g < 3:
                        k2 = QKV[:, i, 768 + 64 * g:832 + 64 * g].unsqueeze(1).broadcast_to((P, 2, 64))
                        kv = hl[:, 512:768].rearrange("p (v r d) -> p v r d", v=2, r=2)
                        t = split(kv[:, 0], kv[:, 1], k2)
                        b, bk, fr = allb.take()
                        for v in range(2):
                            t1 = tr(bk[:, v * P:(v + 1) * P], hl[:, 512 + v * P:640 + v * P], t, fr, inc=(v == 1))
                        give(b, evac(KST[:, gb, :, i * P:(i + 1) * P], bk[:, 0:256].rearrange("p (v q) -> p v q", v=2),
                                     t1, group_used[gb]))
                    hl_used[i % 2] = t1
                return [A.last(), V.last()]

            hl_used = [pe.last(), pe.last()]
            t_pt = pe.last()
            pt_used[0] = pt_used[1] = t_pt

            def units_of(g, tk):
                out_ = []
                gb = g % 2
                for i in range(NT):
                    qs = slice(i * P, (i + 1) * P)
                    if g < 3:
                        k0, k1 = (max(0, i - 1), min(4, i + 2)) if l == 0 else (0, 4)
                        ks = slice(k0 * P, k1 * P)
                        u = dict(n=(k1 - k0) * P,
                                 qk=lambda h, qs=qs, ks=ks: [(QST[:, gb, h, qs], KST[:, gb, 0, ks]),
                                                            (QST[:, gb, h, qs], KST[:, gb, 1, ks])],
                                 pv=pv_shared([QKV[:, kt, 960 + 64 * g:1024 + 64 * g] for kt in range(k0, k1)]))
                        if l == 0:
                            u["sink"] = g
                            off = 128 if k0 == i else 0
                            u["mask"] = k_("band")[:, off:off + u["n"]]
                    else:
                        u = dict(n=256,
                                 qk=lambda h, qs=qs: [(QST[:, gb, h, qs], KMS[:, 0, h, :]),
                                                      (QST[:, gb, h, qs], KMS[:, 1, h, :])],
                                 pv=pv_own([[VM[:, kt, 64 * h:64 * h + 64] for kt in range(2)] for h in range(4)]))
                    u.update(scale=SCALE, tok=tk, otok=t_pt, o=HT[:, 2 * g:2 * g + 2, qs])
                    out_.append(u)
                return out_

            units = []
            for g in range(4):
                units += units_of(g, None)
            t_g = prepare(0)
            for u in units[0:4]:
                u["tok"] = t_g

            def next_group(n):
                g = n // 4
                if n % 4 == 0:
                    group_used[(g - 1) % 2] = pe.last()
                if n % 4 == 2 and g < 3:
                    t = prepare(g + 1)
                    for v in units[4 * g + 4:4 * g + 8]:
                        v["tok"] = t

            attention(units, allb, next_group)
            t_oT = [A.last(), V.last()]
            if dump(f"oT{l}", HT, *t_oT):
                return finish()
            row = load_row(I["g_mix_post"][l])
            for h in range(2):
                gemm_tok(HT, 8, 512, lambda i, bk, t, h=h: evac(T16[:, i, 512 * h:512 * h + 512], bk[:, :], t, pe.last()),
                         t_oT)
            xt = post_norm(row, None, [A.last(), V.last(), pe.last()])
            if dump(f"xa{l}", X, xt):
                return finish()

            t_h, _ = norm_T(lambda i: X[:, i, :], NT, D, lambda i: T16[:, i, :], gcol("g_ffn_pre", l), HT,
                            lambda i: xt, pe.last())
            FT = U[:, 0:22 * 512].rearrange("p (k t) -> p k t", k=22)
            tmp = PB[:, :, :, :].rearrange("p b h n -> p (b h) n")
            for c in range(11):
                s, slot, t_w = ring.take()
                wv = [slot_w(256)(slot), slot_w(256, 2048)(slot)]
                for q in range(2):
                    two = []
                    for j in range(2):
                        b, bk, fr = allb.take()
                        for k in range(8):
                            t = mm(bk[:, :], wv[j][:, k, q * P:(q + 1) * P], HT[:, k, :], k == 0, k == 7, t_w, t_h, fr)
                        two.append((b, bk, t))
                    z = (2 * c + q) % 4
                    (b0, g0, t0), (b1, g1, t1) = two
                    ta = A.free(lambda e, z=z, g0=g0: e.activation(tmp[:, z, :], g0[:, :], ACT.Tanh, scale=0.5), t0,
                                V.last(), pe.last())
                    tb = V.do(lambda e, z=z, g0=g0: e.scalar_tensor_tensor(tmp[:, z, :], tmp[:, z, :], 1.0, g0[:, :],
                                                                           ALU.add, ALU.mult), ta)
                    give(b0, tb)
                    tc_ = V.do(lambda e, z=z, g1=g1, f=2 * c + q: e.scalar_tensor_tensor(
                        FT[:, f, :], tmp[:, z, :], 0.5, g1[:, :], ALU.mult, ALU.mult), t1)
                    give(b1, tc_)
                ring.done(s, t1)
            if dump(f"ft{l}", FT, tc_):
                return finish()
            row = load_row(I["g_ffn_post"][l])
            t_last = pe.last()
            for h in range(2):
                four = [allb.take() for _ in range(NT)]
                for k0, k1 in ((0, 8), (8, 16), (16, 22)):
                    s, slot, t_w = ring.take()
                    w = slot_w(512, 0, k1 - k0)(slot)
                    for i in range(NT):
                        b, bk, fr = four[i]
                        for k in range(k0, k1):
                            t = mm(bk[:, :], FT[:, k, i * P:(i + 1) * P], w[:, k - k0, :], k == 0, k == 21, t_w, tc_, fr,
                                   inc=(k == k1 - 1))
                        if k1 == 22:
                            give(b, A.free(lambda e, i=i, bk=bk, h=h: e.activation(
                                T16[:, i, 512 * h:512 * h + 512], bk[:, :], ACT.Copy), t, t_last))
                    ring.done(s, t)
            xt = post_norm(row, None, [A.last(), pe.last()])
            if dump(f"xb{l}", X, xt):
                return finish()
        if stop == "block1":
            return finish()
        R = arena[:, U0:U0 + 27648]

        def at(a, n):
            assert a + n <= 27648
            return R[:, a:a + n]

        w0h, a0h, oka = small(4), small(4), small(4)
        V.do(lambda e: e.tensor_scalar(w0h, gcol("rw_w0_2")[:, 0:4], 0.5, None, ALU.mult))
        V.do(lambda e: e.tensor_scalar(a0h, gcol("rw_a0_2")[:, 0:4], 0.5, None, ALU.mult))
        t_cols = V.do(lambda e: e.tensor_scalar(oka, gcol("rw_k_a_2")[:, 0:4], -1.0, 1.0, ALU.mult, ALU.add))

        t_h, _ = norm_T(lambda i: X[:, i, :], NT, D, lambda i: T16[:, i, :], gcol("mix_norm_g_2"), HT,
                        lambda i: xt, pe.last())
        Z = at(0, 7168).rearrange("p (c t) -> p c t", t=512)
        ZI = at(24064, 1026).rearrange("p (b t) -> p b t", t=513)
        for b_ in range(2):
            t_zi = V.do(lambda e, b_=b_: e.memset(ZI[:, b_, 0:1], 0.0), pe.last())
        mu = gcol("rw_mu_2")
        zl = [None, None]
        for s4, nc_ in enumerate((4, 4, 4, 2)):
            s, slot, t_w = ring.take()
            w = slot_w(nc_ * P)(slot)
            for q in range(nc_):
                c = 4 * s4 + q
                b, bk, fr = allb.take()
                for k in range(8):
                    t = mm(bk[:, :], w[:, k, q * P:(q + 1) * P], HT[:, k, :], k == 0, k == 7, t_w, t_h, fr)
                zi = ZI[:, c % 2, :]
                t1 = A.free(lambda e, zi=zi, bk=bk: e.activation(zi[:, 1:513], bk[:, :], ACT.Copy), t, t_zi, zl[c % 2])
                give(b, t1)
                zc = Z[:, c, :]
                V.do(lambda e, zi=zi, zc=zc: e.tensor_tensor(zc, zi[:, 0:512], zi[:, 1:513], ALU.subtract), t1, pe.last())
                zl[c % 2] = V.do(lambda e, zi=zi, zc=zc, c=c: e.scalar_tensor_tensor(zc, zc, mu[:, c:c + 1], zi[:, 1:513],
                                                                                   ALU.mult, ALU.add))
            ring.done(s, t)
        A.do(lambda e: e.activation(Z[0:64, 12, :], Z[0:64, 12, :], ACT.Tanh), V.last())
        t1 = A.do(lambda e: e.activation(Z[:, 13, :], Z[:, 13, :], ACT.Tanh, scale=0.5))
        t_z = V.do(lambda e: e.tensor_scalar(Z[:, 13, :], Z[:, 13, :], 0.5, 0.5, ALU.mult, ALU.add), t1)
        if dump("z", Z, t_z):
            return finish()

        x_io = Dma("s_xio")
        xs_v = x_scr.rearrange("(i p) d -> p i d", p=P)
        t_xout = x_io.start(SP, xs_v, X, xt)
        XC = X.rearrange("p i d -> p (i d)")
        o_ = [7168]

        def buf(n):
            o_[0] += n
            return at(o_[0] - n, n)

        SETS = []
        for base_ in (at(7168, 2560), XC[:, 0:2560]):
            SETS.append(dict(AR=base_[:, 0:1024].rearrange("p (m n) -> p m n", m=4), KH=base_[:, 1024:1536],
                             BH=base_[:, 1536:2048], BON=base_[:, 2048:2560], W=small(8)))
        y_, yc, q_ = [XC[:, 2560 + 512 * q:3072 + 512 * q] for q in range(3)]
        o_[0] = 9728
        Vt, Kt, Bt, At = [buf(512).rearrange("p (m n) -> p m n", m=4) for _ in range(4)]
        GM = buf(4096).rearrange("p (i n) -> p i n", i=8)
        XX = buf(2048).rearrange("p (i n) -> p i n", i=8)
        LM = [buf(1024).rearrange("p (i n) -> p i n", i=8) for _ in range(2)]
        T1b = buf(1024).rearrange("p (i n) -> p i n", i=8)
        PP = buf(1024).rearrange("p (i n) -> p i n", i=8)
        Us = buf(512).rearrange("p (i n) -> p i n", i=8)
        Q2 = buf(512).rearrange("p (m n) -> p m n", m=4)
        Fm, Ec, Sst = buf(512), buf(512), buf(512)
        T0, T1, T2, T3, T4, T5 = [buf(512) for _ in range(6)]
        C1 = -0.5 * float(np.exp(-0.5))
        s_misc, slot, t_misc = ring.take()
        wu, au, gu = slot[0:64, 0:512], slot[64:128, 0:512], slot[:, 512:1024]
        v4 = lambda ap: ap.rearrange("p (m n) -> p m n", m=4)
        v8 = lambda ap: ap.rearrange("p (c n) -> p c n", c=8)
        by_half = lambda ap, cc: ap.rearrange("p (m c n) -> p m c n", c=2, n=64)[:, :, cc, :]
        mainb, sideb = Banks(range(6)), Banks((6, 7))
        ready, set_free, y_done = {}, [None, None], {}

        def item(it):
            hh, m = it // 4, it % 4
            return m, hh, slice(64 * hh, 64 * hh + 64)

        def rows(j):
            D_ = SETS[j % 2]
            ARt, KH, BH, BON, Wc = D_["AR"], D_["KH"], D_["BH"], D_["BON"], D_["W"]
            fr0 = set_free[j % 2]
            r_, k0_, v_ = Z[:, j, :], Z[:, 4 + j, :], Z[:, 8 + j, :]
            js, cs = slice(j, j + 1), slice(j * P, (j + 1) * P)
            b, bk, fr = sideb.take()
            t = mm(bk[:, :], wu[:, cs], Z[0:64, 12, :], True, True, t_misc, t_z, fr)
            t1 = A.do(lambda e: e.activation(T0, bk[:, :], ACT.Tanh, bias=w0h[:, js], scale=0.5), t, t_cols, fr0, V.last(),
                      t_xout)
            give(b, t1)
            b, ba, fr = sideb.take()
            t = mm(ba[:, :], au[:, cs], Z[64:128, 12, :], True, True, fr)
            t2 = A.do(lambda e: e.activation(T4, ba[:, :], ACT.Tanh, bias=a0h[:, js], scale=0.5), t)
            give(b, t2)
            yield
            V.do(lambda e: e.tensor_scalar(T0, T0, C1, C1, ALU.mult, ALU.add), t1)
            t1 = V.do(lambda e: e.tensor_tensor_scan(T1, k_("keep"), T0, 0.0, ALU.mult, ALU.add))
            yield
            A.do(lambda e: e.activation(T2, T1, ACT.Exp), t1)
            A.do(lambda e: e.activation(T3, T1, ACT.Exp, scale=-1.0))
            t1 = V.do(lambda e: e.tensor_tensor(T0, T1, T0, ALU.subtract))
            t_e0 = A.do(lambda e: e.activation(T0, T0, ACT.Exp), t1)
            yield
            V.do(lambda e: e.tensor_scalar(T4, T4, 0.5, 0.5, ALU.mult, ALU.add), t2)
            V.do(lambda e: e.tensor_scalar(T5, k0_, gcol("rw_k_k_2")[:, js], None, ALU.mult))
            t1 = V.do(lambda e: e.tensor_tensor(BON, T5, T5, ALU.mult), fr0, t_xout)
            yield
            b, bs, fr = sideb.take()
            t = mm(bs[:, :], k_("bones"), BON, True, True, t1, fr)
            yield
            t1 = V.do(lambda e: e.tensor_scalar(BON, bs[:, :], 1e-24, None, ALU.max), t)
            give(b, t1)
            t1 = A.do(lambda e: e.activation(BON, BON, ACT.Sqrt), t1)
            yield
            yield
            V.do(lambda e: e.reciprocal(BON, BON), t1)
            yield
            V.do(lambda e: e.tensor_tensor(T5, T5, BON, ALU.mult))
            V.do(lambda e: e.scalar_tensor_tensor(ARt[:, :, 0:128], v4(T0), -1.0, v4(T5), ALU.mult, ALU.mult), t_e0)
            yield
            V.do(lambda e: e.tensor_tensor(ARt[:, :, 128:256], v4(T2), v4(r_), ALU.mult))
            V.do(lambda e: e.tensor_scalar(T0, T4, gcol("rw_k_a_2")[:, js], oka[:, js], ALU.mult, ALU.add))
            yield
            V.do(lambda e: e.tensor_tensor(T0, T0, k0_, ALU.mult))
            V.do(lambda e: e.tensor_tensor(T5, T5, T4, ALU.mult))
            yield
            V.do(lambda e: e.tensor_tensor(KH, T0, T3, ALU.mult))
            V.do(lambda e: e.tensor_tensor(BH, T5, T3, ALU.mult))
            yield
            V.do(lambda e: e.tensor_copy(Wc, T2.rearrange("p (c n) -> p c n", n=64)[:, :, 63]))
            t1 = V.do(lambda e: e.scalar_tensor_tensor(T1, r_, gcol("rw_r_k_2")[:, js], T0, ALU.mult, ALU.mult))
            b, bb, fr = sideb.take()
            t = mm(bb[:, :], k_("bones"), T1, True, True, t1, fr)
            yield
            t1 = V.do(lambda e: e.tensor_tensor(BON, bb[:, :], v_, ALU.mult), t)
            give(b, t1)
            ready[j] = t1

        def group_norm(j):
            BON = SETS[j % 2]["BON"]
            js, cs = slice(j, j + 1), slice(j * P, (j + 1) * P)
            b, bk, fr = sideb.take()
            t = mm(bk[:, :], k_("bmean"), y_, True, True, y_done[j], fr)
            yield
            t1 = V.do(lambda e: e.tensor_tensor(yc, y_, bk[:, :], ALU.subtract), t)
            give(b, t1)
            t1 = V.do(lambda e: e.tensor_tensor(q_, yc, yc, ALU.mult))
            b, b2_, fr = sideb.take()
            t = mm(b2_[:, :], k_("bmean"), q_, True, True, t1, fr)
            yield
            t1 = V.do(lambda e: e.tensor_scalar(q_, b2_[:, :], 64e-5, None, ALU.add), t)
            give(b, t1)
            t1 = A.do(lambda e: e.activation(q_, q_, ACT.Sqrt), t1)
            yield
            yield
            V.do(lambda e: e.reciprocal(q_, q_), t1)
            yield
            V.do(lambda e: e.tensor_tensor(yc, yc, q_, ALU.mult))
            V.do(lambda e: e.tensor_scalar(yc, yc, gcol("rw_gn_w_2")[:, js], gcol("rw_gn_b_2")[:, js], ALU.mult, ALU.add))
            b, b3_, fr = sideb.take()
            t = mm(b3_[:, :], gu[:, cs], Z[:, 13, :], True, True, fr)
            yield
            V.do(lambda e: e.tensor_tensor(yc, yc, BON, ALU.add))
            t1 = V.do(lambda e: e.tensor_tensor(Z[:, j, :], yc, b3_[:, :], ALU.mult), t)
            give(b, t1)
            set_free[j % 2] = [t1, t]
            y_done["yr"] = (t, t1)

        def chunks(j):
            D_ = SETS[j % 2]
            ARt, KH, BH, Wc = D_["AR"], D_["KH"], D_["BH"], D_["W"]
            v_ = Z[:, 8 + j, :]
            t_e = ready[j]
            gm = {}
            for it in range(8):
                m, hh, ps = item(it)
                b, bk, fr = mainb.take()
                ms = slice(m * P, (m + 1) * P)
                mm(bk[:, 0:256], BH[ps, ms], ARt[ps, m, :], True, True, t_e, fr, inc=False)
                t = mm(bk[:, 256:512], KH[ps, ms], ARt[ps, m, :], True, True)
                gm[it] = V.free(lambda e, it=it, bk=bk: e.tensor_tensor(GM[:, it, :], bk[:, :], k_("mgram"), ALU.mult), t,
                                chunk_done[0])
                give(b, gm[it])
                if it % 2:
                    yield
            x2 = [None, None]
            tl = {}
            for q in range(2):
                b, bk, fr = mainb.take()
                for r in range(4):
                    m, hh, ps = item(4 * q + r)
                    t = mm(bk[:, r * P:(r + 1) * P], ARt[ps, m, 0:128], BH[ps, m * P:(m + 1) * P], True, True, t_e, fr,
                           inc=(r == 3))
                tl[q] = (b, bk, t)

            def lm(n, x):
                return G.do(lambda e: e.tensor_tensor(LM[x], GM[:, :, 0:128],
                                                      k_(f"up{n}").unsqueeze(1).broadcast_to((P, 8, P)), ALU.mult),
                            gm[7], lm_used[x])

            t_lm = [lm(2, 0), lm(4, 1)]
            for q in range(2):
                b, bk, t = tl[q]
                xs = XX[:, 4 * q:4 * q + 4, 0:128]
                xt_ = XX[:, 4 * q:4 * q + 4, 128:256]
                bc = lambda n: k_(n).unsqueeze(1).broadcast_to((P, 4, P))
                t1 = V.do(lambda e, xs=xs, bk=bk: e.tensor_tensor(xs, v4(bk[:, :]), bc("low1"), ALU.mult), t)
                give(b, t1)
                V.free(lambda e, xt_=xt_, q=q: e.tensor_tensor(xt_, GM[:, 4 * q:4 * q + 4, 0:128], bc("up1"), ALU.mult))
                V.do(lambda e, xs=xs: e.tensor_tensor(xs, xs, bc("ident"), ALU.add))
                x2[q] = V.free(lambda e, xt_=xt_: e.tensor_tensor(xt_, xt_, bc("ident"), ALU.add))
            t_T = []
            for src, dst in ((lambda m: v_[:, m * P:(m + 1) * P], Vt), (lambda m: KH[:, m * P:(m + 1) * P], Kt),
                             (lambda m: BH[:, m * P:(m + 1) * P], Bt), (lambda m: ARt[:, m, 0:128], At)):
                b, bk, fr = mainb.take()
                for m in range(4):
                    t = tr(bk[:, m * P:(m + 1) * P], src(m), t_e, fr, inc=(m == 3))
                t_T.append(A.free(lambda e, dst=dst, bk=bk: e.activation(dst, v4(bk[:, :]), ACT.Copy), t, chunk_done[0]))
                give(b, t_T[-1])
            yield
            b, bk, fr = mainb.take()
            for it in range(8):
                m, hh, ps = item(it)
                t = mm(bk[:, it * 64:it * 64 + 64], GM[:, it, 256:384], Vt[:, m, ps], True, True, t_T, fr, gm[7],
                       inc=(it == 7))
            t_us = A.free(lambda e, bk=bk: e.activation(Us, bk[:, :].rearrange("p (i n) -> p i n", i=8), ACT.Copy), t)
            give(b, t_us)
            t1u = [None, None]
            for lv, n in enumerate((2, 4, 8, 16, 32)):
                x = lv % 2
                tt = [None, None]
                for q in range(2):
                    b, bk, fr = mainb.take()
                    for r in range(4):
                        it = 4 * q + r
                        t = mm(bk[:, r * P:(r + 1) * P], LM[x][:, it, :], XX[:, it, 0:128], True, True, t_lm[x], x2[q], fr,
                               inc=(r == 3))
                    tt[q] = A.free(lambda e, q=q, bk=bk: e.activation(T1b[:, 4 * q:4 * q + 4, :], v4(bk[:, :]), ACT.Copy), t,
                                   t1u[q])
                    give(b, tt[q])
                lm_used[x] = t
                if lv + 2 < 5:
                    t_lm[x] = lm((8, 16, 32)[lv], x)
                yield
                for q in range(4):
                    b, bk, fr = mainb.take()
                    for r in range(2):
                        it = 2 * q + r
                        if n < 32:
                            mm(bk[:, r * 256:r * 256 + 128], XX[:, it, 128:256], T1b[:, it, :], True, True, tt[q // 2], fr,
                               inc=False)
                        t = mm(bk[:, r * 256 + 128:r * 256 + 256], T1b[:, it, :], XX[:, it, 128:256], True, True,
                               tt[q // 2], fr, inc=(r == 1))
                    a0_ = 0 if n < 32 else 128
                    xs = XX[:, 2 * q:2 * q + 2, a0_:256]
                    x2[q // 2] = V.free(lambda e, xs=xs, bk=bk, a0_=a0_: e.tensor_tensor(
                        xs, xs, bk[:, :].rearrange("p (i n) -> p i n", i=2)[:, :, a0_:256], ALU.add), t)
                    give(b, x2[q // 2])
                    t1u[q // 2] = t
                    if q == 1:
                        yield
            t_pp = []
            for q in range(2):
                b, bk, fr = mainb.take()
                for r in range(4):
                    it = 4 * q + r
                    m, hh, ps = item(it)
                    mm(bk[:, r * P:r * P + 64], XX[:, it, 128:256], At[:, m, ps], True, True, x2[q], t_us, fr, inc=False)
                    t = mm(bk[:, r * P + 64:r * P + 128], XX[:, it, 128:256], Us[:, it, :], True, True, inc=(r == 3))
                t_pp.append(A.free(lambda e, q=q, bk=bk: e.activation(PP[:, 4 * q:4 * q + 4, :], v4(bk[:, :]), ACT.Copy), t))
                give(b, t_pp[-1])
            yield
            t_f, t_ec = [], []
            for cc in range(2):
                cr = slice(64 * cc, 64 * cc + 64)
                b, bk, fr = mainb.take()
                for it in range(8):
                    m, hh, ps = item(it)
                    t = mm(bk[ps, m * 64:m * 64 + 64], PP[cr, it, 0:64], Bt[cr, m, ps], True, True, fr, t_pp[hh],
                           inc=(it == 7))
                t_f.append(V.free(lambda e, bk=bk, cc=cc: e.tensor_tensor(
                    by_half(Fm, cc), bk[:, 0:256].rearrange("p (m n) -> p m n", m=4),
                    k_("ident64").unsqueeze(1).broadcast_to((P, 4, 64)), ALU.add), t))
                give(b, t_f[-1])
                b, bk, fr = mainb.take()
                for it in range(8):
                    m, hh, ps = item(it)
                    mm(bk[ps, m * 64:m * 64 + 64], Bt[cr, m, ps], PP[cr, it, 64:128], True, False, fr)
                    t = mm(bk[ps, m * 64:m * 64 + 64], Kt[cr, m, ps], Vt[cr, m, ps], False, True, inc=(it == 7))
                t_ec.append(V.free(lambda e, bk=bk, cc=cc: e.tensor_tensor(
                    by_half(Ec, cc), bk[:, 0:256].rearrange("p (m n) -> p m n", m=4),
                    Wc.rearrange("p (m c) -> p m c", c=2)[:, :, cc:cc + 1].broadcast_to((P, 4, 64)), ALU.mult), t))
                give(b, t_ec[-1])
                yield
            b, bq, fr = mainb.take()
            for it in range(8):
                m, hh, ps = item(it)
                t = mm(bq[ps, m * P:(m + 1) * P], PP[:, it, 0:64], GM[:, it, 128:256], True, True, fr, inc=(it == 7))
            t_q2 = V.free(lambda e, bq=bq: e.tensor_tensor(Q2, v4(bq[:, :]), ARt[:, :, 128:256], ALU.add), t)
            give(b, t_q2)
            ts_ = V.do(lambda e: e.tensor_copy(Sst[:, 64:128], Ec[:, 0:64]))
            for c in range(1, 7):
                b, bk, fr = mainb.take()
                for hh in range(2):
                    ps = slice(64 * hh, 64 * hh + 64)
                    t = mm(bk[ps, 0:64], Fm[ps, c * 64:c * 64 + 64], Sst[ps, c * 64:c * 64 + 64], True, True, t_f, ts_, fr,
                           inc=(hh == 1))
                ts_ = V.do(lambda e, bk=bk, c=c: e.scalar_tensor_tensor(
                    Sst[:, c * 64 + 64:c * 64 + 128], bk[:, 0:64], Wc[:, c:c + 1], Ec[:, c * 64:c * 64 + 64],
                    ALU.mult, ALU.add), t)
                give(b, ts_)
                yield
            b, by, fr = mainb.take()
            for it in range(8):
                m, hh, ps = item(it)
                ms = slice(m * P, (m + 1) * P)
                mm(by[ps, ms], PP[:, it, 64:128], GM[:, it, 128:256], True, False, t_pp, ts_, t_q2, fr)
                t = mm(by[ps, ms], Vt[:, m, ps], GM[:, it, 384:512], False, True, inc=False)
                for cc in range(2):
                    c = 2 * m + cc
                    if c:
                        t = mm(by[ps, c * 64:c * 64 + 64], Sst[ps, c * 64:c * 64 + 64], Q2[ps, m, cc * 64:cc * 64 + 64],
                               False, True, inc=(it == 7))
            t1 = V.do(lambda e, by=by: e.tensor_copy(y_, by[:, :]), t, t_xout)
            give(b, t1)
            y_done[j] = t1
            chunk_done[0] = [t, t1]

        chunk_done, lm_used = [None], [None, None]
        for _ in rows(0):
            pass
        for j in range(4):

            def side(j=j):
                if j:
                    yield from group_norm(j - 1)
                if j < 3:
                    yield from rows(j + 1)

            other = side()
            for _ in chunks(j):
                next(other, None)
            for _ in other:
                pass
            if dump(f"ys{j}", y_, y_done[j]):
                return finish()
        for _ in group_norm(3):
            pass
        t, t_yr = y_done["yr"]
        ring.done(s_misc, t)
        t_xin = x_io.start(SP, X, xs_v, pe.last(), V.last(), A.last(), G.last())
        YR = Z[:, 0:4, :]
        if dump("yr", YR, t_yr):
            return finish()

        CK = at(2048, 1152).rearrange("p (i n) -> p i n", i=4)
        CQ = at(3200, 1536).rearrange("p (i n) -> p i n", i=4)
        SC = at(4736, 1536).rearrange("p (i n) -> p i n", i=4)
        KF = at(3200, 3072).rearrange("p (i h d) -> p i h d", i=4, h=8)
        QDT = at(6272, 1536).rearrange("p (k t) -> p k t", k=3)
        KDT = at(7808, 1024).rearrange("p (k t) -> p k t", k=2)
        YMT = at(6272, 2048).rearrange("p (k t) -> p k t", k=4)
        QS = at(8832, 3072).rearrange("p (i h d) -> p i h d", i=4, h=8)
        QTh = at(11904, 2048).rearrange("p (h t) -> p h t", h=4)
        KTh = at(13952, 2048).rearrange("p (h t) -> p h t", h=4)
        VV = at(22016, 2048).rearrange("p (i h d) -> p i h d", i=4, h=8)
        TMP = at(26112, 512)
        pt_at[0] = pt_at[1] = (0, at(24064, 2048).rearrange("p (k n) -> p k n", k=4))
        MT = at(8832, 4096).rearrange("p (k t) -> p k t", k=8)

        ang, nn, cosm, sinm = [TMP[:, 64 * q:64 * q + 64] for q in range(4)]
        ni = TMP[:, 256:320].bitcast(I32)
        a3 = lambda ap: ap.rearrange("p (i c) -> p i c", i=4)
        posf = small(4)
        V.do(lambda e: e.tensor_copy(posf, posi.bitcast(I32)), t_small, t_z)
        V.do(lambda e: e.tensor_tensor(a3(ang), posf.unsqueeze(2).broadcast_to((P, 4, 16)),
                                       k_("invf").unsqueeze(1).broadcast_to((P, 4, 16)), ALU.mult), A.last())
        V.do(lambda e: e.tensor_scalar(nn, ang, float(1 / (2 * np.pi)), None, ALU.mult))
        V.do(lambda e: e.tensor_copy(ni, nn))
        V.do(lambda e: e.tensor_copy(nn, ni))
        c1 = 6.28125
        c2 = float(np.float32(np.round((2 * np.pi - c1) * 2 ** 20) / 2 ** 20))
        c3 = float(2 * np.pi - c1 - c2)
        for c_ in (c1, c2, c3):
            V.do(lambda e, c_=c_: e.scalar_tensor_tensor(ang, nn, -c_, ang, ALU.mult, ALU.add))
        pi_ = 3.1415925
        V.do(lambda e: e.tensor_scalar(ang, ang, pi_, -pi_, ALU.min, ALU.max))
        V.do(lambda e: e.tensor_scalar(nn, ang, -1.0, None, ALU.mult))
        V.do(lambda e: e.tensor_tensor(nn, nn, ang, ALU.max))
        t1 = V.do(lambda e: e.tensor_scalar(nn, nn, -1.0, float(np.pi / 2), ALU.mult, ALU.add))
        A.do(lambda e: e.activation(sinm, ang, ACT.Sin), t1)
        t_cs = A.do(lambda e: e.activation(cosm, nn, ACT.Sin))

        gemm_tok(HT, 8, 384, lambda i, bk, t: evac(CQ[:, i, :], bk[:, 0:384], t, V.last()))
        gemm_tok(HT, 8, 288, lambda i, bk, t: evac(CK[:, i, :], bk[:, 0:288], t))
        t_ck = [A.last(), V.last()]
        t_qd, _ = norm_T(lambda i: CQ[:, i, :], NT, 384, lambda i: SC[:, i, :], gcol("mla_g_qa_2"), QDT,
                         lambda i: t_ck, pe.last())
        t_kd, _ = norm_T(lambda i: CK[:, i, 0:256], NT, 256, lambda i: SC[:, i, 0:256], gcol("mla_g_kva_2"), KDT,
                         lambda i: t_ck, pe.last())
        s, slot, t_w = ring.take()
        w = slot_w(768, 0, 3)(slot)
        for i in range(NT):
            for h in range(2):
                b, bk, fr = allb.take()
                for k in range(3):
                    t = mm(bk[:, 0:384], QDT[:, k, i * P:(i + 1) * P], w[:, k, 384 * h:384 * h + 384], k == 0, k == 2,
                           t_w, t_qd, fr)
                give(b, evac(QS[:, i, 4 * h:4 * h + 4, :], bk[:, 0:384].rearrange("p (h d) -> p h d", h=4), t))
        ring.done(s, t)
        s, slot, t_w = ring.take()
        w = slot_w(1024, 0, 2)(slot)
        for i in range(NT):
            for h in range(2):
                b, bk, fr = allb.take()
                for k in range(2):
                    t = mm(bk[:, :], KDT[:, k, i * P:(i + 1) * P], w[:, k, 512 * h:512 * h + 512], k == 0, k == 1,
                           t_w, t_kd, fr)
                b4 = bk[:, :].rearrange("p (h d) -> p h d", h=4)
                A.free(lambda e, b4=b4, i=i, h=h: e.activation(KF[:, i, 4 * h:4 * h + 4, 0:64], b4[:, :, 0:64], ACT.Copy), t)
                give(b, A.free(lambda e, b4=b4, i=i, h=h: e.activation(VV[:, i, 4 * h:4 * h + 4, :], b4[:, :, 64:128], ACT.Copy), t))
        ring.done(s, t)
        cb = lambda ap, h: a3(ap).unsqueeze(2).broadcast_to((P, 4, h, 16))
        TV4 = lambda a, h: TMP[:, a:a + 64 * h].rearrange("p (i h c) -> p i h c", i=4, h=h)
        q1, q2 = (HL[1][:, 0:512], HL[0][:, 0:512])
        qv = lambda ap: ap.rearrange("p (i h c) -> p i h c", i=4, h=8)
        t_e1 = [A.last(), V.last(), t_cs]
        rotate(QS[:, :, :, 64:80], QS[:, :, :, 80:96], QS[:, :, :, 64:80], QS[:, :, :, 80:96],
               cb(cosm, 8), cb(sinm, 8), qv(q1), qv(q2), t_e1)
        rotate(CK[:, :, 256:272], CK[:, :, 272:288], CK[:, :, 256:272], CK[:, :, 272:288],
               a3(cosm), a3(sinm), a3(TMP[:, 320:384]), a3(TMP[:, 384:448]))
        t_kf = V.do(lambda e: e.tensor_copy(KF[:, :, :, 64:96],
                                            CK[:, :, 256:288].unsqueeze(2).broadcast_to((P, 4, 8, 32))), t_e1)
        for g in range(2):
            for src, dst in ((QS, QTh), (KF, KTh)):
                for h in range(4):
                    b, bk, fr = allb.take()
                    for i in range(4):
                        t = tr(bk[0:96, i * P:(i + 1) * P], src[:, i, 4 * g + h, :], t_kf, fr, inc=(i == 3))
                    give(b, evac(dst[0:96, h, :], bk[0:96, :], t, pe.last()))
            t_T = [A.last(), V.last()]
            units = []
            for i in range(4):
                n = (i + 1) * P
                units.append(dict(n=n, scale=float(MSCALE), tok=t_T, mask=k_("causal")[:, 512 - n:512], otok=t_kf,
                                  qk=lambda h, i=i, n=n: [(QTh[0:96, h, i * P:(i + 1) * P], KTh[0:96, h, 0:n])],
                                  pv=pv_own([[VV[:, kt, 4 * g + h, :] for kt in range(i + 1)] for h in range(4)]),
                                  o=YMT[:, 2 * g:2 * g + 2, i * P:(i + 1) * P]))
            t_yt = attention(units, allb)
        if dump("yt", YMT, *t_yt):
            return finish()

        SG = at(12928, 2048).rearrange("p (b t) -> p b t", b=4)
        sgn = 0
        for h in range(2):
            sb_, slb, t_wb = ring.take()
            wb = [slot_w(512, 0, 4)(slb), slot_w(512, 2048, 4)(slb)]
            for q in range(2):
                s, slot, t_w = ring.take()
                wg = [slot_w(256)(slot), slot_w(256, 2048)(slot)]
                for c in range(2):
                    jj = 2 * q + c
                    prods = []
                    for br, (src, tk) in enumerate(((YR, t_yr), (YMT, t_yt))):
                        b, bk, fr = allb.take()
                        for k in range(8):
                            t = mm(bk[:, :], wg[br][:, k, c * P:(c + 1) * P], HT[:, k, :], k == 0, k == 7, t_w, fr)
                        x = sgn % 4
                        sgn += 1
                        t1 = A.do(lambda e, x=x, bk=bk: e.activation(SG[:, x, :], bk[:, :], ACT.Tanh, scale=0.5), t,
                                  V.last())
                        give(b, t1)
                        b, bk2, fr = allb.take()
                        for k in range(4):
                            t = mm(bk2[:, :], wb[br][:, k, jj * P:(jj + 1) * P], src[:, k, :], k == 0, k == 3, t_wb, tk, fr)
                        t2 = V.do(lambda e, x=x, bk2=bk2: e.scalar_tensor_tensor(SG[:, x, :], SG[:, x, :], 1.0, bk2[:, :],
                                                                                 ALU.add, ALU.mult), t1, t)
                        give(b, t2)
                        prods.append(x)
                    V.do(lambda e, p_=tuple(prods): e.tensor_tensor(SG[:, p_[1], :], SG[:, p_[0], :], SG[:, p_[1], :],
                                                                   ALU.add))
                    t_m = V.do(lambda e, p_=tuple(prods), f=4 * h + jj: e.tensor_scalar(MT[:, f, :], SG[:, p_[1], :], 0.5,
                                                                                     None, ALU.mult))
                ring.done(s, t)
            ring.done(sb_, t)
        if dump("mt", MT, t_m):
            return finish()
        for h in range(2):
            gemm_tok(MT, 8, 512, lambda i, bk, t, h=h: V.do(lambda e: e.tensor_tensor(
                X[:, i, 512 * h:512 * h + 512], X[:, i, 512 * h:512 * h + 512], bk[:, :], ALU.add), t, t_xin), t_m)
        xt = V.last()
        if dump("x2", X, xt):
            return finish()

        t_h, hns = norm_T(lambda i: X[:, i, :], NT, D, lambda i: T16[:, i, :], gcol("ffn_norm_g_2"), HT,
                          lambda i: xt, pe.last())
        d_hn = Dma("s_hn")
        hn_v = hn_scr.rearrange("(i p) d -> p i d", p=P)
        for i in range(NT):
            t_hn = d_hn.start(SP, hn_v[:, i, :], T16[:, i, :], hns[i])
        frow = load_row(I["final_norm_g_2"])
        RB = at(22016, 3072)
        rp = [0]

        def rbuf(n):
            rp[0] += n
            assert rp[0] <= 3072
            return RB[:, rp[0] - n:rp[0]]

        LG = rbuf(144).rearrange("p (i n) -> p i n", i=4)
        GL = rbuf(32).rearrange("p (i n) -> p i n", i=4)
        M8 = rbuf(32).rearrange("p (i n) -> p i n", i=4)
        I8 = rbuf(32).rearrange("p (i n) -> p i n", i=4)
        F8 = rbuf(32).rearrange("p (i n) -> p i n", i=4)
        OG = rbuf(16).rearrange("p (i n) -> p i n", i=4)
        OM = rbuf(16).rearrange("p (i n) -> p i n", i=4)
        EG = rbuf(16).rearrange("p (i n) -> p i n", i=4)
        N8 = rbuf(32).rearrange("p (i n) -> p i n", i=4)
        J8 = rbuf(32).rearrange("p (i n) -> p i n", i=4)
        K8 = rbuf(32).rearrange("p (i n) -> p i n", i=4)
        FMk = rbuf(128).rearrange("p (i n) -> p i n", i=4)
        OH = [rbuf(128).rearrange("p (i n) -> p i n", i=4) for _ in range(2)]
        MM_ = rbuf(128).rearrange("p (i n) -> p i n", i=4)
        POS = rbuf(128).rearrange("p (i n) -> p i n", i=4)
        TQ = rbuf(128).rearrange("p (i n) -> p i n", i=4)
        CNT, NBK, END, STA = rbuf(32), rbuf(32), rbuf(32), rbuf(32)
        OHP = [rbuf(128) for _ in range(2)]
        OHB = [rbuf(40) for _ in range(2)]
        EB = rbuf(1248)
        ng, sg, gg, e2, w1, w2, dn = [small(4) for _ in range(7)]
        pq = [[small(4) for _ in range(4)] for _ in range(2)]
        slotu = [small(4), small(4)]
        IDX = small(40)
        ebf, ebi = small(40), small(40)

        b, bk, fr = allb.take()
        for i in range(NT):
            for k in range(8):
                t = mm(bk[:, i * 36:i * 36 + 36], HT[:, k, i * P:(i + 1) * P], rw[:, k, :], k == 0, k == 7, t_h, t_small,
                       fr, inc=(i == 3 and k == 7))
        V.do(lambda e, bk=bk: e.tensor_tensor(LG, bk[:, 0:144].rearrange("p (i n) -> p i n", i=4),
                                              rb.unsqueeze(1).broadcast_to((P, 4, 36)), ALU.add), t)
        give(b, V.last())
        V.do(lambda e: e.memset(GL, 2 * NEG))
        V.do(lambda e: e.tensor_copy(GL[:, :, 0:4], LG[:, :, 0:4]))
        for i in range(NT):
            V.do(lambda e, i=i: e.max(M8[:, i, :], GL[:, i, :]))
            V.do(lambda e, i=i: e.max_index(I8[:, i, :].bitcast(U32), M8[:, i, :], GL[:, i, :]))
        V.do(lambda e: e.tensor_copy(F8, I8.bitcast(U32)))
        t1 = V.do(lambda e: e.tensor_scalar(ng, M8[:, :, 0], -1.0, None, ALU.mult))
        for i in range(NT):
            t2 = A.do(lambda e, i=i: e.activation(EG[:, i, :], LG[:, i, 0:4], ACT.Exp, bias=ng[:, i:i + 1],
                                                  accum_out=sg[:, i:i + 1]), t1)
        V.do(lambda e: e.reciprocal(gg, sg), t2)
        i4 = k_("iota")[:, 0:4].unsqueeze(1).broadcast_to((P, 4, 4))
        V.do(lambda e: e.tensor_tensor(OG, i4, F8[:, :, 0:1].broadcast_to((P, 4, 4)), ALU.is_equal))
        V.do(lambda e: e.tensor_scalar(OM, OG, 1.0, -NEG, ALU.subtract, ALU.mult))
        f4 = lambda ap: ap.rearrange("p i (g n) -> p i g n", g=4)
        gb4 = lambda ap: ap.unsqueeze(3).broadcast_to((P, 4, 4, 8))
        V.do(lambda e: e.tensor_tensor(f4(FMk), f4(LG[:, :, 4:36]), gb4(OG), ALU.mult))
        V.do(lambda e: e.tensor_tensor(f4(FMk), f4(FMk), gb4(OM), ALU.add))
        for i in range(NT):
            V.do(lambda e, i=i: e.max(N8[:, i, :], FMk[:, i, :]))
            V.do(lambda e, i=i: e.max_index(J8[:, i, :].bitcast(U32), N8[:, i, :], FMk[:, i, :]))
        V.do(lambda e: e.tensor_copy(K8, J8.bitcast(U32)))
        t1 = V.do(lambda e: e.tensor_tensor(dn, N8[:, :, 1], N8[:, :, 0], ALU.subtract))
        t1 = A.do(lambda e: e.activation(e2, dn, ACT.Exp), t1)
        V.do(lambda e: e.tensor_scalar(w1, e2, 1.0, None, ALU.add), t1)
        V.do(lambda e: e.reciprocal(w1, w1))
        V.do(lambda e: e.tensor_tensor(w1, w1, gg, ALU.mult))
        V.do(lambda e: e.tensor_tensor(w2, w1, e2, ALU.mult))
        i32_ = k_("iota")[:, 0:32].unsqueeze(1).broadcast_to((P, 4, 32))
        for q in range(2):
            V.do(lambda e, q=q: e.tensor_tensor(OH[q], i32_, K8[:, :, q:q + 1].broadcast_to((P, 4, 32)), ALU.is_equal))
        t1 = V.do(lambda e: e.tensor_tensor(MM_, OH[0], OH[1], ALU.add))
        b, bk, fr = allb.take()
        for i in range(NT):
            for i2 in range(i):
                mm(bk[:, i * 32:i * 32 + 32], k_("ones"), MM_[:, i2, :], i2 == 0, False, t1, fr)
            mm(bk[:, i * 32:i * 32 + 32], k_("triu"), MM_[:, i, :], i == 0, True, t1, fr, inc=False)
        for i in range(NT):
            t = mm(bk[:, 128:160], k_("ones"), MM_[:, i, :], i == 0, i == 3)
        V.do(lambda e, bk=bk: e.tensor_copy(POS, bk[:, 0:128].rearrange("p (i n) -> p i n", i=4)), t)
        V.do(lambda e, bk=bk: e.tensor_copy(CNT, bk[:, 128:160]))
        give(b, V.last())
        V.do(lambda e: e.tensor_scalar(NBK, CNT, 0.0, None, ALU.is_gt))
        for c_ in (128.0, 256.0, 384.0):
            V.do(lambda e, c_=c_: e.scalar_tensor_tensor(NBK, CNT, c_, NBK, ALU.is_gt, ALU.add))
        V.do(lambda e: e.tensor_tensor_scan(END, k_("ones")[:, 0:32], NBK, 0.0, ALU.mult, ALU.add))
        V.do(lambda e: e.tensor_tensor(STA, END, NBK, ALU.subtract))
        EB3 = EB[0:1, :].rearrange("p (b n) -> p b n", b=NB)
        V.do(lambda e: e.tensor_tensor(EB3, END[0:1, :].unsqueeze(1).broadcast_to((1, NB, 32)),
                                       k_("iota")[0:1, 0:NB].unsqueeze(2).broadcast_to((1, NB, 32)), ALU.is_le))
        V.do(lambda e: e.tensor_reduce(ebf[0:1, 0:NB], EB3, AX, ALU.add))
        V.do(lambda e: e.tensor_scalar(ebf[0:1, 0:NB], ebf[0:1, 0:NB], 31.0, None, ALU.min))
        t_eb = V.do(lambda e: e.tensor_copy(ebi[0:1, 0:NB].bitcast(I32), ebf[0:1, 0:NB]))
        for q in range(2):
            ps_, sq_, gq, bq_ = pq[q]
            V.do(lambda e, q=q: e.tensor_tensor(TQ, OH[q], POS, ALU.mult))
            V.do(lambda e, ps_=ps_: e.tensor_reduce(ps_, TQ, AX, ALU.add))
            V.do(lambda e, q=q: e.tensor_tensor(TQ, OH[q], STA.unsqueeze(1).broadcast_to((P, 4, 32)), ALU.mult))
            V.do(lambda e, sq_=sq_: e.tensor_reduce(sq_, TQ, AX, ALU.add))
            V.do(lambda e, gq=gq, ps_=ps_: e.tensor_scalar(gq, ps_, 128.0, None, ALU.is_ge))
            for c_ in (256.0, 384.0):
                V.do(lambda e, c_=c_, gq=gq, ps_=ps_: e.scalar_tensor_tensor(gq, ps_, c_, gq, ALU.is_ge, ALU.add))
            V.do(lambda e, gq=gq, sq_=sq_, bq_=bq_: e.tensor_tensor(bq_, sq_, gq, ALU.add))
            V.do(lambda e, gq=gq, ps_=ps_: e.scalar_tensor_tensor(ps_, gq, -128.0, ps_, ALU.mult, ALU.add))
            V.do(lambda e, gq=gq, bq_=bq_, ps_=ps_: e.scalar_tensor_tensor(gq, bq_, 128.0, ps_, ALU.mult, ALU.add))
            t_slot = V.do(lambda e, gq=gq, q=q: e.tensor_copy(slotu[q].bitcast(U32), gq))
        b, bk, fr = allb.take()
        for q in range(2):
            for i in range(NT):
                ps_, sq_, gq, bq_ = pq[q]
                x = i % 2
                V.do(lambda e, x=x, i=i, ps_=ps_: e.tensor_scalar(OHP[x], k_("iota"), ps_[:, i:i + 1], None, ALU.is_equal),
                     pe.last())
                t1 = V.do(lambda e, x=x, i=i, bq_=bq_: e.tensor_scalar(OHB[x][:, 0:NB], k_("iota")[:, 0:NB], bq_[:, i:i + 1],
                                                                       k_("tokid")[:, i:i + 1], ALU.is_equal, ALU.mult))
                t = mm(bk[:, 0:NB], OHP[x], OHB[x][:, 0:NB], q == 0 and i == 0, q == 1 and i == 3, t1, fr, inc=True)
        t_idx = V.do(lambda e, bk=bk: e.tensor_copy(IDX[:, 0:NB].bitcast(U32), bk[:, 0:NB]), t)
        give(b, t_idx)
        if dump("slots", slotu[0].bitcast(F32), t_idx):
            return finish()

        ms_sem = [Dma(f"s_moe{i}") for i in range(4)]
        mslot = [RINGC[:, 0:6144], RINGC[:, 6144:12288], at(4096, 6144), at(10240, 6144)]
        XG = [at(16384 + 1024 * q, 1024) for q in range(3)]
        YB = [at(19456, 1024), at(0, 1024)]
        XTm = [at(1024 + 1024 * q, 1024).rearrange("p (k t) -> p k t", k=8) for q in range(2)]
        ACTB = [at(20480 + 256 * q, 256) for q in range(2)]
        AT_ = [at(20992 + 256 * q, 256).rearrange("p (k t) -> p k t", k=2) for q in range(2)]
        THm = [at(21504 + 256 * q, 256) for q in range(2)]
        gat_sem = [Dma(f"s_gat{i}") for i in range(3)]
        yst_sem = [Dma(f"s_yst{i}") for i in range(2)]
        fg = gcol("ffn_norm_g_2")
        Wgu, Wdn = I["moe_w_gu_2"][0], I["moe_w_down_2"][0]
        before = [pe.last(), V.last(), A.last(), t_hn]
        moe_free = [None] * 4
        down_done, gath_done, ysto = {}, {}, [None, None]
        wl, gl = {}, {}

        def load_w(n):
            x = n % 4
            SP.wait(t_eb, before if n < 4 else None, down_done.get(n - 4))
            ms_sem[x].n += 32
            s = mslot[x]

            def go(e, n=n, x=x, s=s):
                r = e.value_load(ebi[0:1, n:n + 1].bitcast(I32), min_val=0, max_val=31)
                gsrc = Wgu[bass.ds(r, 1), :, :].rearrange("o (k p) n -> p (o k) n", p=P)
                dsrc = Wdn[bass.ds(r, 1), :, :].rearrange("o (k p) n -> p (o k) n", p=P)
                e.dma_start(s[:, 0:4096].rearrange("p (k n) -> p k n", k=8), gsrc).then_inc(ms_sem[x].sem, 16)
                e.dma_start(s[:, 4096:6144].rearrange("p (k n) -> p k n", k=2), dsrc).then_inc(ms_sem[x].sem, 16)

            SP.items.append(go)
            wl[n] = (ms_sem[x].sem, ms_sem[x].n)

        def gather(n):
            x = n % 3
            G.wait(t_hn, t_idx, before if n < 3 else None, gath_done.get(n - 3))
            gat_sem[x].n += 16
            G.items.append(lambda e, n=n, x=x: e.indirect_dma_start(
                XG[x], None, hn_scr, bass.IndirectOffsetOnAxis(ap=IDX[:, n:n + 1].bitcast(U32), axis=0))
                .then_inc(gat_sem[x].sem, 16))
            gl[n] = (gat_sem[x].sem, gat_sem[x].n)

        def x_T(n):
            xg, x = XG[n % 3], XTm[n % 2]
            for hf in range(2):
                b, bk, fr = allb.take()
                for k in range(4):
                    t = tr(bk[:, k * P:(k + 1) * P], xg[:, (4 * hf + k) * P:(4 * hf + k + 1) * P], gl[n], fr, inc=(k == 3))
                t1 = V.free(lambda e, bk=bk, hf=hf, x=x: e.tensor_tensor(
                    x[:, 4 * hf:4 * hf + 4, :], bk[:, :].rearrange("p (k t) -> p k t", k=4),
                    fg[:, 4 * hf:4 * hf + 4].unsqueeze(2).broadcast_to((P, 4, P)), ALU.mult), t, before if n < 2 else None)
                give(b, t1)
            gath_done[n] = t
            return t1

        def up(n, t_x_):
            b, bk, fr = allb.take()
            w = mslot[n % 4][:, 0:4096].rearrange("p (k n) -> p k n", k=8)
            for k in range(8):
                t = mm(bk[:, :], XTm[n % 2][:, k, :], w[:, k, :], k == 0, k == 7, t_x_, wl[n], fr)
            a, th_ = ACTB[n % 2], THm[n % 2]
            t1 = A.free(lambda e: e.activation(th_, bk[:, 0:256], ACT.Tanh, scale=0.5), t, V.last())
            t2 = V.do(lambda e: e.scalar_tensor_tensor(th_, th_, 1.0, bk[:, 0:256], ALU.add, ALU.mult), t1)
            t3 = V.do(lambda e: e.scalar_tensor_tensor(a, th_, 0.5, bk[:, 256:512], ALU.mult, ALU.mult), pe.last())
            give(b, t3)
            return t3

        def down(n, t_a):
            b, bk, fr = allb.take()
            a, aT = ACTB[n % 2], AT_[n % 2]
            for k in range(2):
                t = tr(bk[:, k * P:(k + 1) * P], a[:, k * P:(k + 1) * P], t_a, fr, inc=(k == 1))
            t1 = A.free(lambda e: e.activation(aT, bk[:, 0:256].rearrange("p (k t) -> p k t", k=2), ACT.Copy), t)
            give(b, t1)
            w = mslot[n % 4][:, 4096:6144].rearrange("p (k n) -> p k n", k=2)
            yb = YB[n % 2]
            for h in range(2):
                b, bk2, fr = allb.take()
                for k in range(2):
                    t = mm(bk2[:, :], aT[:, k, :], w[:, k, 512 * h:512 * h + 512], k == 0, k == 1, t1, wl[n], fr)
                if h == 0:
                    t2 = A.free(lambda e, bk2=bk2: e.activation(yb[:, 0:512], bk2[:, :], ACT.Copy), t, ysto[n % 2])
                else:
                    t2 = V.free(lambda e, bk2=bk2: e.tensor_copy(yb[:, 512:1024], bk2[:, :]), t, ysto[n % 2])
                give(b, t2)
            down_done[n] = t
            ysto[n % 2] = yst_sem[n % 2].start(A, y_scr[n * P:(n + 1) * P, :], yb, A.last(), t2)

        for n in range(3):
            load_w(n)
            gather(n)
        load_w(3)
        t_x1 = x_T(0)
        t_a1 = up(0, t_x1)
        for n in range(NB):
            if n + 1 < NB:
                t_x1 = x_T(n + 1)
                if n + 3 < NB:
                    gather(n + 3)
                t_a2 = up(n + 1, t_x1)
            down(n, t_a1)
            if n + 4 < NB:
                load_w(n + 4)
            t_a1 = t_a2

        YG = [at(4096 + 1024 * q, 1024) for q in range(8)]
        y_sem = [Dma(f"s_yg{i}") for i in range(8)]
        tg = {}
        for i in range(NT):
            for q in range(2):
                x = 2 * i + q
                G.wait(ysto, pe.last())
                y_sem[x].n += 16
                G.items.append(lambda e, i=i, q=q, x=x: e.indirect_dma_start(
                    YG[x], None, y_scr, bass.IndirectOffsetOnAxis(ap=slotu[q][:, i:i + 1].bitcast(U32), axis=0))
                    .then_inc(y_sem[x].sem, 16))
                tg[x] = (y_sem[x].sem, y_sem[x].n)
        out_v = out[0].rearrange("(i p) d -> p i d", p=P)
        t_row = frow
        ms, rs = NST[nst[0] % 2]
        for i in range(NT):
            V.do(lambda e, i=i: e.scalar_tensor_tensor(X[:, i, :], YG[2 * i], w1[:, i:i + 1], X[:, i, :], ALU.mult, ALU.add),
                 tg[2 * i])
            t = V.do(lambda e, i=i: e.scalar_tensor_tensor(X[:, i, :], YG[2 * i + 1], w2[:, i:i + 1], X[:, i, :],
                                                           ALU.mult, ALU.add), tg[2 * i + 1])
            t1 = A.do(lambda e, i=i: e.activation(YG[2 * i], X[:, i, :], ACT.Square, scale=1 / 32.0,
                                                  accum_out=ms[:, i:i + 1]), t)
            t2 = rsqrt4(rs[:, i:i + 1], ms[:, i:i + 1], 1, eps6, t1)
            t3 = V.do(lambda e, i=i: e.scalar_tensor_tensor(X[:, i, :], X[:, i, :], rs[:, i:i + 1], ROW,
                                                            ALU.mult, ALU.mult), t2, t_row)
            d = Dma(f"s_out{i}")
            stores.append(d.start(SP, out_v[:, i, :], X[:, i, :], t3))
        return finish()


_INS = ["x", "mem", "mem_norm_g", "w_in", "w_mem_kv", "w_o", "g_mix_pre", "g_mix_post", "attn_sink", "qk_norm_g",
        "w_gate_up", "w_down", "g_ffn_pre", "g_ffn_post", "positions_2", "mix_norm_g_2", "w_in_2", "rw_mu_2",
        "rw_w0_2", "rw_w_up_2", "rw_a0_2", "rw_a_up_2", "rw_g_up_2", "rw_k_k_2", "rw_k_a_2", "rw_r_k_2", "rw_gn_w_2",
        "rw_gn_b_2", "mla_g_qa_2", "mla_w_q_up_2", "mla_g_kva_2", "mla_w_kv_up_2", "w_branch_rw_2",
        "w_branch_mla_2", "w_out_2", "ffn_norm_g_2", "moe_w_group_2", "moe_b_group_2", "moe_w_router_2",
        "moe_b_router_2", "moe_w_gu_2", "moe_w_down_2", "final_norm_g_2"]


def kernel(**inputs):
    import concourse.bacc as bacc
    from concourse.bass_utils import run_bass_kernel_spmd

    nc = bacc.Bacc("TRN2", target_bir_lowering=False, num_devices=1)
    arrays, aps = {}, {}
    for name in _INS:
        a = np.ascontiguousarray(inputs[name])
        arrays[f"in_{name}"] = a
        aps[name] = nc.dram_tensor(f"in_{name}", a.shape, mybir.dt.from_np(a.dtype), kind="ExternalInput").ap()
    table = const_table()
    arrays["tables"] = table
    consts = nc.dram_tensor("tables", table.shape, F32, kind="ExternalInput").ap()
    out = nc.dram_tensor("out_0", (1, S, D), F32, kind="ExternalOutput").ap()
    hn_scr = nc.dram_tensor("hn_scr", (S, D), F32).ap()
    y_scr = nc.dram_tensor("y_scr", (NB * P, D), F32).ap()
    x_scr = nc.dram_tensor("x_scr", (S, D), F32).ap()
    build(nc, aps, out, hn_scr, y_scr, x_scr, consts)
    r = run_bass_kernel_spmd(nc, [arrays], core_ids=[0])
    return r.results[0]["out_0"]
```

```python
from contextlib import ExitStack

import numpy as np
import concourse.bass as bass
from concourse import mybir

F32 = mybir.dt.float32
I32 = mybir.dt.int32
F32R = mybir.dt.float32r
U32 = mybir.dt.uint32
ALU = mybir.AluOpType
ACT = mybir.ActivationFunctionType
AX = mybir.AxisListType.X

P = 128
NT = 4
S = 512
D = 1024
NB = 39
SLOT = 4096
NEG = -1.0e30
SCALE = 64 ** -0.5
MSCALE = 1.0 / np.sqrt(96.0)

CONST = {}


def const_table():
    parts, at = [], [0]

    def put(name, a):
        a = np.asarray(a, np.float32)
        if a.ndim == 1:
            a = np.broadcast_to(a[None, :], (P, a.shape[0]))
        a = a.reshape(P, -1)
        CONST[name] = (at[0], at[0] + a.shape[1])
        at[0] += a.shape[1]
        parts.append(a)

    p = np.arange(P)
    s, t = p[:, None], p[None, :]
    put("ident", np.eye(P))
    put("bones", (s // 64 == t // 64))
    put("bmean", (s // 64 == t // 64) / 64.0)
    put("ident64", (s % 64 == np.arange(64)[None, :]))
    put("ones", np.ones((P, P)))
    put("triu", s < t)
    band = np.zeros((P, 384), np.float32)
    band[:, 0:128] = np.where(t >= s, 0.0, NEG)
    band[:, 256:384] = np.where(t <= s, 0.0, NEG)
    put("band", band)
    causal = np.zeros((P, 512), np.float32)
    causal[:, 384:] = np.where(t <= s, 0.0, NEG)
    put("causal", causal)
    same = s // 64 == t // 64
    strict, incl = same & (t > s), same & (t >= s)
    put("mgram", np.concatenate([strict, incl, strict, incl], 1))
    up = lambda n: (s // (2 * n) == t // (2 * n)) & (s % (2 * n) < n) & (t % (2 * n) >= n)
    put("low1", up(1).T)
    for n in (1, 2, 4, 8, 16, 32):
        put(f"up{n}", up(n))
    tok = np.arange(S).reshape(NT, P).T

    def angles(pos, dims, theta):
        inv = (theta ** (-(np.arange(0, dims, 2, dtype=np.float32) / np.float32(dims)))).astype(np.float32)
        return pos.astype(np.float32)[..., None] * inv

    a = angles(tok, 16, 500000.0)
    put("cosp", np.cos(a))
    put("sinp", np.sin(a))
    a = np.stack([angles(tok // 64, 32, 10000.0), angles(tok % 64, 32, 10000.0)], 2)
    put("cosx", np.cos(a))
    put("sinx", np.sin(a))
    put("invf", (np.float32(10000.0) ** (-np.arange(0, 32, 2, dtype=np.float32) / np.float32(32))).astype(np.float32))
    put("iota", np.arange(128))
    put("tokid", tok)
    put("keep", np.arange(S) % 64 != 0)
    return np.concatenate(parts, 1)


const_table()
NCONST = max(b for _, b in CONST.values())

GROWS = [("mem_norm_g", 0, 8), ("g_mix_pre", 0, 8), ("g_mix_pre", 1, 8), ("g_ffn_pre", 0, 8), ("g_ffn_pre", 1, 8),
         ("mix_norm_g_2", 0, 8), ("ffn_norm_g_2", 0, 8), ("rw_mu_2", 0, 14), ("rw_w0_2", 0, 4), ("rw_a0_2", 0, 4),
         ("rw_k_k_2", 0, 4), ("rw_k_a_2", 0, 4), ("rw_r_k_2", 0, 4), ("rw_gn_w_2", 0, 4), ("rw_gn_b_2", 0, 4),
         ("mla_g_qa_2", 0, 3), ("mla_g_kva_2", 0, 2)]


class Lane:

    def __init__(self, sem, chain):
        self.sem, self.chain, self.n, self.items, self.seen = sem, chain, 0, [], {}

    def wait(self, *toks):
        for t in toks:
            if t is None:
                continue
            if isinstance(t, list):
                self.wait(*t)
                continue
            sem, val = t
            if self.seen.get(sem.num, 0) < val:
                self.seen[sem.num] = val
                self.items.append(lambda e, sem=sem, val=val: e.wait_ge(sem, val))

    def do(self, fn, *toks):
        self.wait(*toks)
        if self.chain and self.n:
            self.wait((self.sem, self.n))
        self.n += 1
        self.items.append(lambda e: fn(e).then_inc(self.sem, 1))
        return (self.sem, self.n)

    def free(self, fn, *toks):
        self.wait(*toks)
        self.n += 1
        self.items.append(lambda e: fn(e).then_inc(self.sem, 1))
        return (self.sem, self.n)

    def quiet(self, fn, *toks):
        self.wait(*toks)
        self.items.append(lambda e: fn(e))

    def part(self):
        self.before, self.items = (self.items, dict(self.seen), self.n), []

    def part_if(self, count, limit, *counted):
        part, (self.items, self.seen, n0), n1 = self.items, self.before, self.n
        sems = [(self.sem, n0, n1)] + [(d.sem, a, d.n) for d, a in counted]

        def go(e):
            r = e.value_load(count, min_val=0, max_val=NB)
            with e.If(r < limit + 1):
                for sem, a, b in sems:
                    if b > a:
                        e.wait_ge(sem, a)
                        e.sem_inc(sem, b - a)
            with e.If(r > limit):
                for f in part:
                    f(e)

        self.items.append(go)

    def last(self):
        return (self.sem, self.n) if self.n else None

    def play(self, e):
        for f in self.items:
            f(e)


def build(nc, I, out, hn_scr, y_scr, x_scr, consts, dbg=None, stop=None):
    with ExitStack() as ctx:
        sem = lambda n: ctx.enter_context(nc.semaphore(n))
        pe = Lane(sem("s_pe"), False)
        V = Lane(sem("s_dve"), True)
        A = Lane(sem("s_act"), True)
        G = Lane(sem("s_pool"), True)
        SP = Lane(sem("s_sp"), False)
        stores = []

        class Dma:

            def __init__(self, name):
                self.sem, self.n = sem(name), 0

            def start(self, lane, out_, in_, *toks, **kw):
                self.n += 16
                lane.wait(*toks)
                lane.items.append(lambda e: e.dma_start(out_, in_, **kw).then_inc(self.sem, 16))
                return (self.sem, self.n)

        AR_N = 53200
        arena_at = -(-nc.sbuf_base // 32) * 32
        arena = ctx.enter_context(nc.sbuf_tensor("arena", [P, AR_N], F32))
        banks = [ctx.enter_context(nc.psum_tensor(f"ps{i}", [P, 512], F32)) for i in range(8)]
        top = [0]

        def col(n):
            a = top[0]
            top[0] += n
            assert top[0] <= AR_N, top[0]
            return arena[:, a:a + n]

        def rounded(name, c0, n):
            return nc.alloc_sbuf_tensor_at(name, [P, n], F32R, offset=arena_at + 4 * c0)[:, :]

        X = col(4096).rearrange("p (i d) -> p i d", i=NT)
        HT = col(4096).rearrange("p (k t) -> p k t", k=8)
        RINGC = col(3 * SLOT)
        C = col(NCONST)
        k_ = lambda n: C[:, CONST[n][0]:CONST[n][1]]
        GC = col(103)
        goff, o_ = {}, 0
        for name, l, n in GROWS:
            goff[(name, l)] = o_
            o_ += n
        gcol = lambda name, l=0: GC[:, goff[(name, l)]:]
        st = col(900)
        stp = [0]

        def small(n):
            a = stp[0]
            stp[0] += n
            assert stp[0] <= 900
            return st[:, a:a + n]

        base = top[0]
        ident = k_("ident")

        class Banks:

            free_after = [None] * 8

            def __init__(self, ids):
                self.ids, self.at = list(ids), 0

            def take(self):
                b = self.ids[self.at % len(self.ids)]
                self.at += 1
                w = Banks.free_after[b]
                assert w != "held", b
                Banks.free_after[b] = "held"
                return b, banks[b], w

        def give(b, *toks):
            Banks.free_after[b] = list(toks)

        allb = Banks(range(8))

        def mm(o, l, r, start, stop_, *toks, inc=None):
            f = lambda e: e.matmul(o, l, r, start=start, stop=stop_, skip_group_check=True)
            return (pe.do if (stop_ if inc is None else inc) else pe.quiet)(f, *toks)

        def tr(o, i, *toks, inc=True):
            n = i.shape[0]
            f = lambda e: e.transpose(o, i, ident[0:n, 0:n])
            return (pe.do if inc else pe.quiet)(f, *toks)

        ring_sem = [Dma(f"s_ring{i}") for i in range(3)]
        jobs = []

        def job(*parts):
            jobs.append(parts)

        def w3(ap, k0, k1, c0, c1):
            return ap[k0 * P:k1 * P, c0:c1].rearrange("(k p) n -> p k n", p=P)

        def slot_w(n, off=0, k=8):
            return lambda s: s[:, off:off + k * n].rearrange("p (k n) -> p k n", n=n)

        for l in range(2):
            job((slot_w(512), w3(I["w_mem_kv"][l], 0, 8, 0, 512)))
            for c0, n in ((0, 512), (512, 512), (1024, 384)):
                job((slot_w(n), w3(I["w_in"][l], 0, 8, c0, c0 + n)))
            for h in range(2):
                job((slot_w(512), w3(I["w_o"][l], 0, 8, 512 * h, 512 * h + 512)))
            for c in range(11):
                job((slot_w(256), w3(I["w_gate_up"][l], 0, 8, 256 * c, 256 * c + 256)),
                    (slot_w(256, 2048), w3(I["w_gate_up"][l], 0, 8, 2816 + 256 * c, 3072 + 256 * c)))
            for k0, k1 in ((0, 8), (8, 16), (16, 22)):
                for h in range(2):
                    job((slot_w(512, 0, k1 - k0), w3(I["w_down"][l], k0, k1, 512 * h, 512 * h + 512)))
        W2 = I["w_in_2"][0]
        for c0, n in ((1536, 256), (0, 512), (0, 0), (512, 512), (1024, 512)):
            if n:
                job((slot_w(n), w3(W2, 0, 8, c0, c0 + n)))
            else:
                job((lambda s: s[0:64, 0:512], I["rw_w_up_2"][0]), (lambda s: s[64:128, 0:512], I["rw_a_up_2"][0]),
                    (lambda s: s[:, 512:1024], I["rw_g_up_2"][0]))
        job((slot_w(384), w3(W2, 0, 8, 1792, 2176)))
        job((slot_w(288), w3(W2, 0, 8, 2176, 2464)))
        job((slot_w(768, 0, 3), w3(I["mla_w_q_up_2"][0], 0, 3, 0, 768)))
        job((slot_w(1024, 0, 2), w3(I["mla_w_kv_up_2"][0], 0, 2, 0, 1024)))
        for c0 in range(0, D, 256):
            job((slot_w(256, 0, 4), w3(I["w_branch_rw_2"][0], 0, 4, c0, c0 + 256)),
                (slot_w(256, 1024, 4), w3(I["w_branch_mla_2"][0], 0, 4, c0, c0 + 256)))
            job((slot_w(256), w3(W2, 0, 8, 2464 + c0, 2720 + c0)),
                (slot_w(256, 2048), w3(W2, 0, 8, 3488 + c0, 3744 + c0)))
        for h in range(2):
            job((slot_w(512), w3(I["w_out_2"][0], 0, 8, 512 * h, 512 * h + 512)))

        class Ring:
            def __init__(self):
                self.loaded, self.taken, self.landed = 0, 0, []
                self.after = {}

            def pump(self):
                while self.loaded < len(jobs) and (self.loaded < 3 or (self.loaded - 3) in self.after):
                    n = self.loaded
                    s = RINGC[:, (n % 3) * SLOT:(n % 3 + 1) * SLOT]
                    tok = None
                    for view, src in jobs[n]:
                        tok = ring_sem[n % 3].start(SP, view(s), src, self.after.get(n - 3))
                    self.landed.append(tok)
                    self.loaded += 1

            def take(self):
                n = self.taken
                self.taken += 1
                self.pump()
                return n, RINGC[:, (n % 3) * SLOT:(n % 3 + 1) * SLOT], self.landed[n]

            def done(self, n, tok):
                self.after[n] = tok
                self.pump()

        ring = Ring()

        dc, dx, dg, dr, drow = Dma("s_const"), Dma("s_x"), Dma("s_g"), Dma("s_small"), Dma("s_rows")
        t_c = dc.start(SP, C, consts)
        top[0] = U0 = -(-top[0] // 8) * 8
        T16 = col(4096).rearrange("p (i d) -> p i d", i=NT)
        U = col(12288)
        PB2 = arena[:, U0 + 19456:U0 + 20480]
        PB = col(2 * 2048).rearrange("p (b h n) -> p b h n", b=2, h=4)
        HL = [col(768) for _ in range(2)]
        KMS = rounded("KMS", top[0], 2048).rearrange("p (v h m) -> p v h m", v=2, h=4)
        col(2048)
        VM = col(512).rearrange("p (k m) -> p k m", k=2)
        MEMT = col(2048).rearrange("p (k m) -> p k m", k=8)
        ROW = col(1024)
        GR = HL[0][0:103, 0:128]

        memv = I["mem"][0].rearrange("(i p) d -> p i d", p=P)
        t_mem = dx.start(SP, T16[:, 0:2, :], memv)
        r0 = 0
        t_gr = None
        for name, l, n in GROWS:
            v = I[name]
            v = v.rearrange("(c q) -> c q", q=P) if name == "mem_norm_g" else (
                v[0].rearrange("h d -> (h d)").rearrange("(c q) -> c q", q=P) if name == "rw_r_k_2"
                else v[l].rearrange("(c q) -> c q", q=P))
            t_gr = dg.start(SP, GR[r0:r0 + n, :], v)
            r0 += n
        dxx = Dma("s_xx")
        t_x = dxx.start(SP, X, I["x"][0].rearrange("(i p) d -> p i d", p=P))
        ring.pump()
        sink = small(12)
        qkg = small(128)
        rb = small(36)
        rw = small(288).rearrange("p (k n) -> p k n", n=36)
        posi = small(4)
        dr.start(SP, sink, I["attn_sink"][0].partition_broadcast(P))
        dr.start(SP, qkg, I["qk_norm_g"][0].rearrange("a d -> (a d)").partition_broadcast(P))
        dr.start(SP, rb[:, 0:4], I["moe_b_group_2"][0].partition_broadcast(P))
        dr.start(SP, rb[:, 4:36], I["moe_b_router_2"][0].partition_broadcast(P))
        dr.start(SP, rw[:, :, 0:4], w3(I["moe_w_group_2"][0], 0, 8, 0, 4), allow_slow_non_contiguous=True)
        dr.start(SP, rw[:, :, 4:36], w3(I["moe_w_router_2"][0], 0, 8, 0, 32))
        t_small = dr.start(SP, posi.bitcast(I32), I["positions_2"][0].rearrange("(i p) -> p i", p=P),
                           allow_slow_non_contiguous=True)

        rowd = Dma("s_row")
        row_used = [None]

        def load_row(src):
            return rowd.start(SP, ROW, src.partition_broadcast(P), row_used[0])

        nhalf = small(8)
        eps6 = 1e-6
        t_nh = G.do(lambda e: e.memset(nhalf, -0.5))
        nsink = small(12)

        b, bk, w = allb.take()
        t = tr(bk[:, 0:103], GR, t_c, t_gr, w)
        t_gc = V.do(lambda e, bk=bk: e.tensor_copy(GC, bk[:, 0:103]), t)
        give(b, t_gc)

        junk = small(4)

        def rsqrt4(o, ms, n, eps, *toks):
            t1 = V.do(lambda e: e.tensor_scalar(ms, ms, eps, None, ALU.add), *toks)
            return G.do(lambda e: e.tensor_tensor(o, ms, nhalf[:, 0:n], ALU.pow), t1, t_nh)

        nst = [0]
        NST = [(small(4), small(4)) for _ in range(2)]

        def norm_T(src, ntile, D_, scr, g, dst, src_tok, dst_tok, each=None):
            ms, rs = NST[nst[0] % 2]
            nst[0] += 1
            nk = D_ // P
            toks, hn = [], []
            for i in range(ntile):
                t1 = A.do(lambda e, i=i: e.activation(scr(i), src(i), ACT.Square, scale=float(D_ ** -0.5),
                                                      accum_out=ms[:, i:i + 1]), src_tok(i), dst_tok if i == 0 else None)
                t2 = rsqrt4(rs[:, i:i + 1], ms[:, i:i + 1], 1, eps6, t1)
                t3 = V.do(lambda e, i=i: e.tensor_scalar(scr(i), src(i), rs[:, i:i + 1], None, ALU.mult), t2)
                hn.append(t3)
                for k0 in range(0, nk, 4):
                    n = min(4, nk - k0)
                    b, bk, w = allb.take()
                    for k in range(n):
                        t4 = tr(bk[:, k * P:k * P + P], scr(i)[:, (k0 + k) * P:(k0 + k + 1) * P], t3, w, t_c)
                    o = dst[:, k0:k0 + n, i * P:(i + 1) * P]
                    iv = bk[:, 0:n * P].rearrange("p (k t) -> p k t", k=n)
                    gb = g[:, k0:k0 + n].unsqueeze(2).broadcast_to((P, n, P))
                    t5 = V.do(lambda e, o=o, iv=iv, gb=gb: e.tensor_tensor(o, iv, gb, ALU.mult), t4, t_gc, dst_tok)
                    give(b, t5)
                    toks.append(t5)
                if each and i:
                    each(i - 1)
            if each:
                return each(ntile - 1), hn
            return toks[-1], hn

        AST = [[small(4) for _ in range(5)] for _ in range(2)]
        un = [0]
        pv_done = [None, None]
        PTB = T16.rearrange("p i d -> p (i d)").rearrange("p (b k n) -> p b k n", b=2, k=4)
        pt_at = [(0, PTB[:, 0]), (1, PTB[:, 1])]
        pt_used = [None, None]

        def scores(u, bp):
            u["b"] = un[0] % 2
            un[0] += 1
            n = u["n"]
            u["s"] = []
            for h in range(4):
                b, bk, w = bp.take()
                pairs = u["qk"](h)
                for z, (l_, r_) in enumerate(pairs):
                    t1 = mm(bk[:, 0:n], l_, r_, z == 0, z == len(pairs) - 1, w, u["tok"])
                u["s"].append((b, bk, t1))

        def maxima(u):
            i = u["b"]
            mS, ngm, den, rden, ske = AST[i]
            n = u["n"]
            u["src"] = []
            for h in range(4):
                b, bk, t1 = u["s"][h]
                if u.get("mask") is not None:
                    t2 = V.free(lambda e, h=h, bk=bk: e.tensor_tensor_reduce(
                        PB[:, i, h, 0:n], bk[:, 0:n], u["mask"], 1.0, -3.0e38, ALU.add, ALU.max, mS[:, h:h + 1]),
                        t1, pv_done[i], t_c)
                    give(b, t2)
                    u["src"].append((None, PB[:, i, h, 0:n]))
                else:
                    V.free(lambda e, h=h, bk=bk: e.tensor_reduce(mS[:, h:h + 1], bk[:, 0:n], AX, ALU.max),
                           t1, pv_done[i])
                    u["src"].append((b, bk[:, 0:n]))
            if u.get("sink") is not None:
                sl = slice(4 * u["sink"], 4 * u["sink"] + 4)
                u["m"] = V.do(lambda e: e.scalar_tensor_tensor(ngm, mS, -u["scale"], nsink[:, sl], ALU.mult, ALU.min))
                u["m"] = V.do(lambda e: e.tensor_tensor(ske, ngm, sink[:, sl], ALU.add))
            else:
                u["m"] = V.do(lambda e: e.tensor_scalar(ngm, mS, -u["scale"], None, ALU.mult))

        def exps(u):
            i, n = u["b"], u["n"]
            mS, ngm, den, rden, ske = AST[i]
            for h in range(4):
                b, src = u["src"][h]
                t4 = A.free(lambda e, h=h, src=src: e.activation(PB[:, i, h, 0:n], src, ACT.Exp, bias=ngm[:, h:h + 1],
                                                                 scale=u["scale"], accum_out=den[:, h:h + 1]),
                            u["m"], pv_done[i])
                if b is not None:
                    give(b, t4)
            if u.get("sink") is not None:
                t4 = A.free(lambda e: e.activation(ske, ske, ACT.Exp))
            u["e"] = t4

        def divide(u):
            i, n = u["b"], u["n"]
            mS, ngm, den, rden, ske = AST[i]
            if u.get("sink") is not None:
                V.do(lambda e: e.tensor_tensor(den, den, ske, ALU.add), u["e"])
            V.do(lambda e: e.reciprocal(rden, den), u["e"])
            V.wait(V.last())
            for h in range(4):
                ph = PB[:, i, h, 0:n]
                u["p"] = V.free(lambda e, h=h, ph=ph: e.tensor_scalar(ph, ph, rden[:, h:h + 1], None, ALU.mult))

        def turn(u, bp):
            i, n = u["b"], u["n"]
            z, pt = pt_at[i]
            u["t"] = []
            for k in range(n // P):
                b, bk, w = bp.take()
                for x, h in enumerate((0, 2, 1, 3)):
                    t1 = tr(bk[:, x * P:(x + 1) * P], PB[:, i, h, k * P:(k + 1) * P], u["p"], w, inc=(x == 3))
                cp = (lambda e, k=k, bk=bk: e.activation(pt[:, k, :], bk[:, :], ACT.Copy)) if k != 1 else (
                    lambda e, k=k, bk=bk: e.tensor_copy(pt[:, k, :], bk[:, :]))
                u["t"].append((A if k != 1 else V).free(cp, t1, pt_used[z]))
                give(b, u["t"][-1])
            pv_done[i] = t1

        def values(u, bp):
            z, pt = pt_at[u["b"]]
            b, bk, w = bp.take()
            t3 = u["pv"](bk, pt, u["t"], w)
            pt_used[z] = t3
            return lambda: give(b, V.free(lambda e: e.tensor_copy(
                u["o"], bk[:, 0:256].rearrange("p (m q) -> p m q", m=2)), t3, u.get("otok")))

        def pv_shared(v):
            def go(bk, pt, t2s, w):
                for k in range(len(v)):
                    for r in range(2):
                        t = mm(bk[64 * r:64 * r + 64, 0:256], v[k], pt[:, k, 256 * r:256 * r + 256], k == 0,
                               k == len(v) - 1, t2s[k], w)
                return t
            return go

        def pv_own(v):
            def go(bk, pt, t2s, w):
                for h in range(4):
                    r, m = h % 2, h // 2
                    for k in range(len(v[h])):
                        t = mm(bk[64 * r:64 * r + 64, m * P:(m + 1) * P], v[h][k],
                               pt[:, k, (2 * r + m) * P:(2 * r + m + 1) * P], k == 0, k == len(v[h]) - 1, t2s[k], w)
                return t
            return go

        def attention(units, bp, before_scores=None):
            for n in range(2):
                if n and before_scores:
                    before_scores(n)
                scores(units[n], bp)
                if n == 0:
                    maxima(units[0])
                    exps(units[0])
            out_ = None
            for n, u in enumerate(units):
                divide(u)
                if n + 1 < len(units):
                    maxima(units[n + 1])
                    exps(units[n + 1])
                if out_:
                    out_()
                turn(u, bp)
                if n + 2 < len(units):
                    if before_scores:
                        before_scores(n + 2)
                    scores(units[n + 2], bp)
                out_ = values(u, bp)
            out_()
            return [A.last(), V.last()]

        def rotate(dst1, dst2, x1, x2, c, s, t1, t2, *toks):
            V.do(lambda e: e.tensor_tensor(t1, x1, s, ALU.mult), *toks)
            V.do(lambda e: e.tensor_tensor(t2, x2, s, ALU.mult))
            V.do(lambda e: e.tensor_tensor(dst1, x1, c, ALU.mult))
            V.do(lambda e: e.tensor_tensor(dst2, x2, c, ALU.mult))
            V.do(lambda e: e.tensor_tensor(dst1, dst1, t2, ALU.subtract))
            return V.do(lambda e: e.tensor_tensor(dst2, dst2, t1, ALU.add))

        def split(hi, lo, src, *toks):
            V.do(lambda e: e.tensor_scalar(hi.bitcast(I32), src.bitcast(I32), -4096, None, ALU.bitwise_and), *toks)
            return V.do(lambda e: e.tensor_tensor(lo, src, hi, ALU.subtract))

        evn = [0]

        def evac(o, i, *toks):
            evn[0] += 1
            if evn[0] % 2:
                return A.free(lambda e: e.activation(o, i, ACT.Copy), *toks)
            return V.free(lambda e: e.tensor_copy(o, i), *toks)

        def mm3(o, l, r, start, stop_, *toks, inc=None):
            mm(o, l[0], r[1], start, False, *toks, inc=False)
            mm(o, l[1], r[0], False, False, inc=False)
            return mm(o, l[0], r[0], False, stop_, inc=inc)

        def split_r(hi, lo, view, *toks):
            h, rw_ = view(hi[0]), view(lo[0])
            V.do(lambda e: e.tensor_scalar(h.bitcast(I32), rw_.bitcast(I32), -4096, None, ALU.bitwise_and), *toks)
            t_ = V.do(lambda e: e.tensor_tensor(view(lo[1]), rw_, h, ALU.subtract))
            return A.free(lambda e: e.activation(view(hi[1]), h, ACT.Copy), t_)

        k3_ = lambda ap: ap.rearrange("p (k t) -> p k t", t=512)

        def both(name, c0, n):
            return arena[:, c0:c0 + n], rounded(name, c0, n)

        HT2, T162 = both("HTr", 4096, 4096), both("T16r", U0, 4096)
        FT2 = [both(f"FTr{q}", U0 + 4096 + 4096 * q, 4096 if q < 2 else 3072) for q in range(3)]
        SL2 = [both(f"slotr{x}", 8192 + SLOT * x, SLOT) for x in range(3)]
        WH2 = [both("WH0", U0 + 15360, 4096), both("WH1", U0 + 20480, 4096)]
        wh_n, wh_free = [0], [None, None]

        def take_split(n, *toks):
            s, slot, t_w = ring.take()
            x = wh_n[0] % 2
            wh_n[0] += 1
            for a in range(0, n, 1024):
                t_ = split_r(WH2[x], SL2[s % 3], lambda ap, a=a: ap[:, a:a + 1024], t_w, wh_free[x], *toks)
            return s, x, (WH2[x][1], SL2[s % 3][1]), t_

        def done_split(s, x, t_):
            wh_free[x] = t_
            ring.done(s, t_)

        def gemm_tok(xT, nk, n, ev, *toks):
            s, slot, t_w = ring.take()
            w = slot_w(n, 0, nk)(slot)
            for i in range(NT):
                b, bk, fr = allb.take()
                for k in range(nk):
                    t = mm(bk[:, 0:n], xT[:, k, i * P:(i + 1) * P], w[:, k, :], k == 0, k == nk - 1, t_w, fr, *toks)
                give(b, ev(i, bk, t))
            ring.done(s, t)
            return t

        def out_T(src, nk, dst, stoks, *toks):
            for k in range(nk):
                b, bk, w = allb.take()
                for i in range(NT):
                    t = tr(bk[:, i * P:(i + 1) * P], src(i, k), w, stoks, inc=(i == 3))
                t2 = evac(dst[:, k, :], bk[:, :], t, *toks)
                give(b, t2)
            return [A.last(), V.last()]

        class Turnover:

            ms_h, ms, rs, ms2, rs2 = small(8), small(4), small(4), small(4), small(4)

            def __init__(self, t_row, o, junk, scr, g, dst, each=None):
                self.t_row, self.o, self.junk, self.scr, self.g, self.dst, self.each = t_row, o, junk, scr, g, dst, each
                self.turned = {}
                self.t0 = pe.last()

            def half(self, i, h, bk, t):
                o, ms_h, junk = self.o(i)[:, 512 * h:512 * h + 512], self.ms_h, self.junk
                t1 = A.do(lambda e: e.activation(junk[:, 0:512], bk[:, :], ACT.Square, scale=1 / 32.0,
                                                   accum_out=ms_h[:, 4 * h + i:4 * h + i + 1]), t)
                return V.free(lambda e: e.tensor_tensor(o, bk[:, :], ROW[:, 512 * h:512 * h + 512], ALU.mult), t1,
                              self.t_row, self.t0)

            def first(self, i, t):
                c, ms_h, ms, rs = slice(i, i + 1), self.ms_h, self.ms, self.rs
                t1 = V.do(lambda e: e.scalar_tensor_tensor(ms[:, c], ms_h[:, c], eps6, ms_h[:, 4 + i:5 + i],
                                                           ALU.add, ALU.add), t)
                self.t_a = G.do(lambda e: e.tensor_tensor(rs[:, c], ms[:, c], nhalf[:, 0:1], ALU.pow), t1, t_nh)

            def second(self, i):
                c, rs, ms2, o, junk = slice(i, i + 1), self.rs, self.ms2, self.o(i), self.junk
                t3 = V.do(lambda e: e.scalar_tensor_tensor(X[:, i, :], o, rs[:, c], X[:, i, :], ALU.mult, ALU.add),
                          self.t_a)
                row_used[0] = t3
                self.t_b = A.do(lambda e: e.activation(junk, X[:, i, :], ACT.Square, scale=1 / 32.0, accum_out=ms2[:, c]),
                                t3)

            def third(self, i):
                self.t_c = rsqrt4(self.rs2[:, i:i + 1], self.ms2[:, i:i + 1], 1, eps6, self.t_b)

            def fourth(self, i):
                sc, rs2 = self.scr(i), self.rs2
                self.t_d = V.do(lambda e: e.tensor_scalar(sc, X[:, i, :], rs2[:, i:i + 1], None, ALU.mult), self.t_c,
                                self.turned.get(i - 2))

            def turn(self, i):
                sc, self.banks = self.scr(i), []
                for k0 in (0, 4):
                    b, bk, w = allb.take()
                    for k in range(4):
                        t4 = tr(bk[:, k * P:k * P + P], sc[:, (k0 + k) * P:(k0 + k + 1) * P], self.t_d, w, inc=(k == 3))
                    self.banks.append((b, bk, t4))
                self.turned[i] = t4

            def out(self, i, q):
                b, bk, t4 = self.banks[q]
                o, k0 = self.dst[:, 4 * q:4 * q + 4, i * P:(i + 1) * P], 4 * q
                iv = bk[:, :].rearrange("p (k t) -> p k t", k=4)
                gb = self.g[:, k0:k0 + 4].unsqueeze(2).broadcast_to((P, 4, P))
                give(b, V.do(lambda e: e.tensor_tensor(o, iv, gb, ALU.mult), t4))

            def step(self, i, t):
                if i:
                    self.turn(i - 1)
                self.first(i, t)
                if i:
                    self.out(i - 1, 0)
                self.second(i)
                if i:
                    self.out(i - 1, 1)
                self.third(i)
                if i and self.each:
                    self.each(i - 1)
                self.fourth(i)

            def end(self):
                i = NT - 1
                self.turn(i)
                self.out(i, 0)
                self.out(i, 1)
                if self.each:
                    self.each(i)
                return [A.last(), V.last()]

        def dump(name, ap, *toks):
            if dbg is not None and name in dbg:
                d = Dma(f"s_dbg_{name}")
                stores.append(d.start(SP, dbg[name], ap, *toks))
                for q in (pe, V, A, G):
                    q.wait(stores[-1])
            return stop == name

        def finish():
            for t in stores:
                SP.wait(t)
            block = ctx.enter_context(nc.Block())

            @block.sync
            def _(e):
                SP.play(e)

            @block.tensor
            def _(e):
                pe.play(e)

            @block.vector
            def _(e):
                V.play(e)

            @block.scalar
            def _(e):
                A.play(e)

            @block.gpsimd
            def _(e):
                G.play(e)

        t_memT, _ = norm_T(lambda i: T16[:, i, :], 2, D, lambda i: T16[:, 2 + i, :], gcol("mem_norm_g"), MEMT,
                           lambda i: t_mem, None)

        xt = t_x
        for l in range(2):
            s, slot, t_w = ring.take()
            w = slot_w(512)(slot)
            KM = U[:, 0:512].rearrange("p (i m) -> p i m", i=2)
            for i in range(2):
                b, bk, fr = allb.take()
                for k in range(8):
                    t = mm(bk[:, :], MEMT[:, k, i * P:(i + 1) * P], w[:, k, :], k == 0, k == 7, t_w, t_memT, fr, xt)
                A.free(lambda e, bk=bk, i=i: e.activation(KM[:, i, :], bk[:, 0:256], ACT.Copy), t, xt)
                t2 = A.free(lambda e, bk=bk, i=i: e.activation(VM[:, i, :], bk[:, 256:512], ACT.Copy), t, pe.last())
                give(b, t2)
            ring.done(s, t)
            t_km = None
            for i in range(2):
                q = HL[0][:, 0:512].rearrange("p (v d) -> p v d", v=2)
                for hp in range(2):
                    kk_ = KM[:, i, 128 * hp:128 * hp + 128].rearrange("p (h d) -> p h d", h=2)
                    o4 = HL[0][:, 0:512].rearrange("p (v h r d) -> p v h r d", v=2, h=2, r=2)
                    for r in range(2):
                        split(o4[:, 0, :, r, :], o4[:, 1, :, r, :], kk_, t2, pe.last())
                    b, bk, fr = allb.take()
                    for x in range(4):
                        t = tr(bk[:, x * P:(x + 1) * P], HL[0][:, x * P:(x + 1) * P], V.last(), fr, inc=(x == 3))
                    ov = KMS[:, :, 2 * hp:2 * hp + 2, i * P:(i + 1) * P]
                    t_km = evac(ov, bk[:, :].rearrange("p (v h q) -> p v h q", v=2, h=2), t)
                    give(b, t_km)
            t_km = [A.last(), V.last()]

            if l == 0:
                t_h, _ = norm_T(lambda i: X[:, i, :], NT, D, lambda i: T16[:, i, :], gcol("g_mix_pre", l), HT,
                                lambda i: xt, [pe.last(), V.last()])
            QKV = U[:, 0:5632].rearrange("p (i n) -> p i n", i=NT)
            QST = rounded(f"QST{l}", U0 + 4096 + 5632, 4096).rearrange("p (b h t) -> p b h t", b=2, h=4)
            KST = rounded(f"KST{l}", U0 + 4096 + 9728, 2048).rearrange("p (b v t) -> p b v t", b=2, v=2)
            TM = U[:, 5632:6656]
            t_m0 = pe.last()

            def head_norm(i):
                H = QKV[:, i, 0:960].rearrange("p (h d) -> p h d", d=64)
                sq = PB[:, 0, 0:2, :].rearrange("p a n -> p (a n)")[:, 0:960].rearrange("p (h d) -> p h d", d=64)
                ms, rs = TM[:, 0:15], TM[:, 16:31]
                V.do(lambda e: e.tensor_tensor(sq, H, H, ALU.mult), A.last(), t_m0)
                V.do(lambda e: e.tensor_reduce(ms, sq, AX, ALU.add))
                V.do(lambda e: e.tensor_scalar(ms, ms, 1 / 64.0, eps6, ALU.mult, ALU.add))
                t = A.do(lambda e: e.activation(ms, ms, ACT.Sqrt), V.last())
                V.do(lambda e: e.reciprocal(rs, ms), t)
                V.do(lambda e: e.tensor_tensor(H, H, rs.unsqueeze(2).broadcast_to((P, 15, 64)), ALU.mult))
                V.do(lambda e: e.tensor_tensor(H[:, 0:12, :], H[:, 0:12, :],
                                               qkg[:, 0:64].unsqueeze(1).broadcast_to((P, 12, 64)), ALU.mult))
                V.do(lambda e: e.tensor_tensor(H[:, 12:15, :], H[:, 12:15, :],
                                               qkg[:, 64:128].unsqueeze(1).broadcast_to((P, 3, 64)), ALU.mult))
                G5 = QKV[:, i, 0:960].rearrange("p (h a b c) -> p h a b c", a=2, b=2, c=16)
                cx = k_("cosx").rearrange("p (i a c) -> p i a c", i=NT, a=2)[:, i]
                sx = k_("sinx").rearrange("p (i a c) -> p i a c", i=NT, a=2)[:, i]
                T = [TM[:, 32:512].rearrange("p (h a c) -> p h a c", a=2, c=16),
                     TM[:, 512:992].rearrange("p (h a c) -> p h a c", a=2, c=16)]
                return rotate(G5[:, :, :, 0, :], G5[:, :, :, 1, :], G5[:, :, :, 0, :], G5[:, :, :, 1, :],
                              cx.unsqueeze(1).broadcast_to((P, 15, 2, 16)), sx.unsqueeze(1).broadcast_to((P, 15, 2, 16)),
                              *T)

            def proj_out(i, bk, t, c0, n):
                if l == 0:
                    return evac(QKV[:, i, c0:c0 + n], bk[:, 0:n], t, t_km, pe.last())
                t1 = A.free(lambda e: e.activation(QKV[:, i, c0:c0 + n], bk[:, 0:n], ACT.Copy), t, t_km)
                if i and c0 == 0:
                    head_norm(i - 1)
                return t1

            chunks_ = ((0, 512), (512, 512), (1024, 384))
            if l == 0:
                for c0, n in chunks_:
                    gemm_tok(HT, 8, n, lambda i, bk, t, c0=c0, n=n: proj_out(i, bk, t, c0, n), t_h)
            else:
                three = [ring.take() for _ in range(3)]
                for i in range(NT):
                    for (c0, n), (s, slot, t_w) in zip(chunks_, three):
                        w = slot_w(n)(slot)
                        b, bk, fr = allb.take()
                        for k in range(8):
                            t = mm(bk[:, 0:n], HT[:, k, i * P:(i + 1) * P], w[:, k, :], k == 0, k == 7, t_w, fr, t_h)
                        give(b, proj_out(i, bk, t, c0, n))
                        if i == NT - 1:
                            ring.done(s, t)
            t_q = [A.last(), V.last()]
            if dump(f"qkv{l}", QKV, *t_q):
                return finish()
            if l == 0:
                H15 = QKV[:, :, 0:960].rearrange("p i (h d) -> p i h d", d=64)
                x1, x2 = H15[:, :, :, 0:8], H15[:, :, :, 8:16]
                cb = k_("cosp").rearrange("p (i c) -> p i c", i=NT).unsqueeze(2).broadcast_to((P, NT, 15, 8))
                sb_ = k_("sinp").rearrange("p (i c) -> p i c", i=NT).unsqueeze(2).broadcast_to((P, NT, 15, 8))
                t1 = TM[:, 0:480].rearrange("p (i h c) -> p i h c", i=NT, c=8)
                t2 = TM[:, 480:960].rearrange("p (i h c) -> p i h c", i=NT, c=8)
                t_r = rotate(x1, x2, x1, x2, cb, sb_, t1, t2, t_q, t_c)
            else:
                t_r = head_norm(NT - 1)
            if l == 0:
                V.do(lambda e: e.tensor_scalar(nsink, sink, -1.0, None, ALU.mult), t_small)
            t_pre = [t_q, t_r, t_km]
            group_used = [None, None]

            evac_a = lambda o, i, *toks: A.free(lambda e: e.activation(o, i, ACT.Copy), *toks)

            def prepare(g, tiles):
                gb = g % 2
                for i in tiles:
                    hl = HL[i % 2]
                    c0 = 256 * g if g < 3 else 1152
                    q4 = QKV[:, i, c0:c0 + 256].rearrange("p (h d) -> p h d", h=4)
                    o4 = hl[:, 0:512].rearrange("p (h v d) -> p h v d", h=4, v=2)
                    t = split(o4[:, :, 0, :], o4[:, :, 1, :], q4, t_pre, hl_used[i % 2])
                    b, bk, fr = allb.take()
                    for h in range(4):
                        t1 = tr(bk[:, h * P:(h + 1) * P], hl[:, h * P:(h + 1) * P], t, fr, inc=(h == 3))
                    give(b, evac_a(QST[:, gb, :, i * P:(i + 1) * P], bk[:, :].rearrange("p (h q) -> p h q", h=4), t1,
                                 group_used[gb]))
                    if g < 3:
                        k2 = QKV[:, i, 768 + 64 * g:832 + 64 * g].unsqueeze(1).broadcast_to((P, 2, 64))
                        kv = hl[:, 512:768].rearrange("p (v r d) -> p v r d", v=2, r=2)
                        t = split(kv[:, 0], kv[:, 1], k2)
                        b, bk, fr = allb.take()
                        for v in range(2):
                            t1 = tr(bk[:, v * P:(v + 1) * P], hl[:, 512 + v * P:640 + v * P], t, fr, inc=(v == 1))
                        give(b, evac_a(KST[:, gb, :, i * P:(i + 1) * P], bk[:, 0:256].rearrange("p (v q) -> p v q", v=2),
                                     t1, group_used[gb]))
                    hl_used[i % 2] = t1
                return [A.last(), V.last()]

            hl_used = [pe.last(), pe.last()]
            t_pt = pe.last()
            pt_used[0] = pt_used[1] = t_pt

            def units_of(g, tk):
                out_ = []
                gb = g % 2
                for i in range(NT):
                    qs = slice(i * P, (i + 1) * P)
                    if g < 3:
                        k0, k1 = (max(0, i - 1), min(4, i + 2)) if l == 0 else (0, 4)
                        ks = slice(k0 * P, k1 * P)
                        u = dict(n=(k1 - k0) * P,
                                 qk=lambda h, qs=qs, ks=ks: [(QST[:, gb, h, qs], KST[:, gb, 0, ks]),
                                                            (QST[:, gb, h, qs], KST[:, gb, 1, ks])],
                                 pv=pv_shared([QKV[:, kt, 960 + 64 * g:1024 + 64 * g] for kt in range(k0, k1)]))
                        if l == 0:
                            u["sink"] = g
                            off = 128 if k0 == i else 0
                            u["mask"] = k_("band")[:, off:off + u["n"]]
                    else:
                        u = dict(n=256,
                                 qk=lambda h, qs=qs: [(QST[:, gb, h, qs], KMS[:, 0, h, :]),
                                                      (QST[:, gb, h, qs], KMS[:, 1, h, :])],
                                 pv=pv_own([[VM[:, kt, 64 * h:64 * h + 64] for kt in range(2)] for h in range(4)]))
                    u.update(scale=SCALE, tok=tk, otok=t_pt, o=HT[:, 2 * g:2 * g + 2, qs])
                    out_.append(u)
                return out_

            units = []
            for g in range(4):
                units += units_of(g, None)
            t_g = prepare(0, range(NT))
            for u in units[0:4]:
                u["tok"] = t_g

            def next_group(n):
                g = n // 4
                if n % 4 == 0:
                    group_used[(g - 1) % 2] = pe.last()
                if g < 3:
                    t = prepare(g + 1, ((0,), (1,) if g else (0, 1), (2, 3), ())[n % 4])
                if n % 4 == 2 and g < 3:
                    for v in units[4 * g + 4:4 * g + 8]:
                        v["tok"] = t

            attention(units, allb, next_group)
            t_oT = [A.last(), V.last()]
            if dump(f"oT{l}", HT, *t_oT):
                return finish()
            row = load_row(I["g_mix_post"][l])
            to = Turnover(row, lambda i: U[:, 4096 + i * D:4096 + (i + 1) * D], U[:, 8192:8192 + D],
                          lambda i: U[:, i * D:(i + 1) * D], gcol("g_ffn_pre", l), HT,
                          each=lambda i: split_r(T162, HT2, lambda ap: k3_(ap)[:, :, i * P:(i + 1) * P]))
            for h in range(2):
                so, slot, t_w = ring.take()
                if h:
                    nxt = take_split(4096, t_oT)
                w = slot_w(512)(slot)
                for i in range(NT):
                    b, bk, fr = allb.take()
                    for k in range(8):
                        t = mm(bk[:, :], HT[:, k, i * P:(i + 1) * P], w[:, k, :], k == 0, k == 7, t_w, fr, t_oT)
                    t1 = to.half(i, h, bk, t)
                    give(b, t1)
                    if h:
                        to.step(i, t1)
                ring.done(so, t)
            t_h = to.end()
            xt = V.last()
            if dump(f"xa{l}", X, xt):
                return finish()

            HH = (k3_(T162[1]), k3_(HT2[1]))
            FT = U[:, 0:22 * 512].rearrange("p (k t) -> p k t", k=22)
            tmp = PB2[:, 0:1024].rearrange("p (h n) -> p h n", h=2)
            for c in range(11):
                s, x, wv, t_w = nxt
                for q in range(2):
                    if not q:
                        nxt = take_split(4096)
                    two = []
                    for j in range(2):
                        b, bk, fr = allb.take()
                        for k in range(8):
                            o_ = j * 2048 + k * 256 + q * P
                            t = mm3(bk[:, :], [a[:, o_:o_ + P] for a in wv], [a[:, k, :] for a in HH], k == 0, k == 7,
                                    t_w, t_h, fr)
                        two.append((b, bk, t))
                    z = q
                    (b0, g0, t0), (b1, g1, t1) = two
                    ta = A.free(lambda e, z=z, g0=g0: e.activation(tmp[:, z, :], g0[:, :], ACT.Tanh, scale=0.5), t0,
                                V.last(), pe.last())
                    tb = V.do(lambda e, z=z, g0=g0: e.scalar_tensor_tensor(tmp[:, z, :], tmp[:, z, :], 1.0, g0[:, :],
                                                                           ALU.add, ALU.mult), ta)
                    give(b0, tb)
                    tc_ = V.do(lambda e, z=z, g1=g1, f=2 * c + q: e.scalar_tensor_tensor(
                        FT[:, f, :], tmp[:, z, :], 0.5, g1[:, :], ALU.mult, ALU.mult), t1)
                    give(b1, tc_)
                done_split(s, x, t1)
            if dump(f"ft{l}", FT, tc_):
                return finish()
            row = load_row(I["g_ffn_post"][l])
            FH = [HT2, T162, FT2[0]]

            def split_f(q, *toks):
                out_ = []
                for k in range(8 * q, min(8 * q + 8, 22), 2):
                    a, n = (k - 8 * q) * 512, 1024
                    out_.append(split_r([ap[:, a:a + n] for ap in FH[q]], [ap[:, a:a + n] for ap in FT2[q]],
                                        lambda ap: ap, *toks))
                return out_

            four = {(h, i): allb.take() for h in range(2) for i in range(NT)}
            t_f = {0: split_f(0, pe.last())}
            chunk_t = {}
            for n in range(6):
                q, h = n // 2, n % 2
                k0, k1 = 8 * q, min(8 * q + 8, 22)
                s, x, wv, t_w = nxt
                if n == 5 and l == 1:
                    nxt = take_split(2048)
                if n < 5:
                    nxt = take_split(512 * (min(8 * ((n + 1) // 2) + 8, 22) - 8 * ((n + 1) // 2)))
                if n == 0:
                    t_f[1] = split_f(1)
                if n == 2:
                    t_f[2] = split_f(2, chunk_t[0])
                hi_, lo_ = k3_(FH[q][1]), k3_(FT2[q][1])
                for i in range(NT):
                    b, bk, fr = four[(h, i)]
                    ts = slice(i * P, (i + 1) * P)
                    for k in range(k0, k1):
                        w_ = [a[:, (k - k0) * 512:(k - k0 + 1) * 512] for a in wv]
                        t = mm3(bk[:, :], (hi_[:, k - k0, ts], lo_[:, k - k0, ts]), w_, k == 0, k == 21, t_w,
                                t_f[q][(k - k0) // 2], fr, inc=(k == k1 - 1))
                    if q == 2:
                        t1 = to.half(i, h, bk, t)
                        give(b, t1)
                        if h:
                            to.step(i, t1)
                chunk_t[q] = t
                done_split(s, x, t)
                if n == 3:
                    to = Turnover(row, lambda i: T16[:, i, :], U[:, 3072:4096],
                                  lambda i: PB2 if i % 2 else U[:, 7168:8192],
                                  gcol("g_mix_pre", 1) if l == 0 else gcol("mix_norm_g_2"), HT)
            t_h = to.end()
            xt = V.last()
            if dump(f"xb{l}", X, xt):
                return finish()
        if stop == "block1":
            return finish()
        R = arena[:, U0:U0 + 27648]

        def at(a, n):
            assert a + n <= 27648
            return R[:, a:a + n]

        w0h, a0h, oka = small(4), small(4), small(4)
        V.do(lambda e: e.tensor_scalar(w0h, gcol("rw_w0_2")[:, 0:4], 0.5, None, ALU.mult))
        V.do(lambda e: e.tensor_scalar(a0h, gcol("rw_a0_2")[:, 0:4], 0.5, None, ALU.mult))
        t_cols = V.do(lambda e: e.tensor_scalar(oka, gcol("rw_k_a_2")[:, 0:4], -1.0, 1.0, ALU.mult, ALU.add))

        ZH, ZL = both("ZH", U0 + 7168, 4096), both("ZL", U0 + 11264, 4096)
        t_hs = [split_r([a[:, 1024 * q:1024 * q + 1024] for a in ZH],
                        [a[:, 1024 * q:1024 * q + 1024] for a in (HT2[0], ZL[1])], lambda ap: ap, pe.last())
                for q in range(4)]
        Z = at(0, 7168).rearrange("p (c t) -> p c t", t=512)
        x_io = Dma("s_xio")
        xs_v = x_scr.rearrange("(i p) d -> p i d", p=P)
        t_xout = x_io.start(SP, xs_v, X, xt)
        XC = X.rearrange("p i d -> p (i d)")
        y_fill = Dma("s_fill")
        y_fill.start(SP, y_scr[32 * P:36 * P, :], x_scr[0:4 * P, :], t_xout)
        t_fill = y_fill.start(SP, y_scr[36 * P:NB * P, :], x_scr[0:(NB - 36) * P, :])
        o_ = [7168]

        def buf(n):
            o_[0] += n
            return at(o_[0] - n, n)

        SETS = []
        for base_ in (XC[:, 0:2560], at(7168, 2560)):
            SETS.append(dict(AR=base_[:, 0:1024].rearrange("p (m n) -> p m n", m=4), KH=base_[:, 1024:1536],
                             BH=base_[:, 1536:2048], BON=base_[:, 2048:2560], W=small(8)))
        y_, yc, q_ = [XC[:, 2560 + 512 * q:3072 + 512 * q] for q in range(3)]
        o_[0] = 9728
        Vt, Kt, Bt, At = [buf(512).rearrange("p (m n) -> p m n", m=4) for _ in range(4)]
        GM = buf(4096).rearrange("p (i n) -> p i n", i=8)
        XX = buf(2048).rearrange("p (i n) -> p i n", i=8)
        LM = [buf(1024).rearrange("p (i n) -> p i n", i=8) for _ in range(2)]
        T1b = buf(1024).rearrange("p (i n) -> p i n", i=8)
        PP = buf(1024).rearrange("p (i n) -> p i n", i=8)
        Us = buf(512).rearrange("p (i n) -> p i n", i=8)
        Q2 = buf(512).rearrange("p (m n) -> p m n", m=4)
        Fm, Ec, Sst = buf(512), buf(512), buf(512)
        T0, T1, T2, T3, T4, T5 = [buf(512) for _ in range(6)]
        C1 = -0.5 * float(np.exp(-0.5))
        v4 = lambda ap: ap.rearrange("p (m n) -> p m n", m=4)
        v8 = lambda ap: ap.rearrange("p (c n) -> p c n", c=8)
        by_half = lambda ap, cc: ap.rearrange("p (m c n) -> p m c n", c=2, n=64)[:, :, cc, :]
        mainb, sideb = Banks(range(6)), Banks((6, 7))
        ready, set_free, y_done = {}, [None, None], {}

        def item(it):
            hh, m = it // 4, it % 4
            return m, hh, slice(64 * hh, 64 * hh + 64)

        def rows(j):
            D_ = SETS[j % 2]
            ARt, KH, BH, BON, Wc = D_["AR"], D_["KH"], D_["BH"], D_["BON"], D_["W"]
            fr0 = set_free[j % 2]
            r_, k0_, v_ = Z[:, j, :], Z[:, 4 + j, :], Z[:, 8 + j, :]
            js, cs = slice(j, j + 1), slice(j * P, (j + 1) * P)
            b, bk, fr = sideb.take()
            t = mm(bk[:, :], wu[:, cs], Z[0:64, 12, :], True, True, t_misc, t_z, fr)
            t1 = A.do(lambda e: e.activation(T0, bk[:, :], ACT.Tanh, bias=w0h[:, js], scale=0.5), t, t_cols, fr0, V.last(),
                      t_xout)
            give(b, t1)
            b, ba, fr = sideb.take()
            t = mm(ba[:, :], au[:, cs], Z[64:128, 12, :], True, True, fr)
            t2 = A.do(lambda e: e.activation(T4, ba[:, :], ACT.Tanh, bias=a0h[:, js], scale=0.5), t)
            give(b, t2)
            yield
            V.do(lambda e: e.tensor_scalar(T0, T0, C1, C1, ALU.mult, ALU.add), t1)
            t1 = V.do(lambda e: e.tensor_tensor_scan(T1, k_("keep"), T0, 0.0, ALU.mult, ALU.add))
            yield
            A.do(lambda e: e.activation(T2, T1, ACT.Exp), t1)
            A.do(lambda e: e.activation(T3, T1, ACT.Exp, scale=-1.0))
            t1 = V.do(lambda e: e.tensor_tensor(T0, T1, T0, ALU.subtract))
            t_e0 = A.do(lambda e: e.activation(T0, T0, ACT.Exp), t1)
            yield
            V.do(lambda e: e.tensor_scalar(T4, T4, 0.5, 0.5, ALU.mult, ALU.add), t2)
            V.do(lambda e: e.tensor_scalar(T5, k0_, gcol("rw_k_k_2")[:, js], None, ALU.mult))
            t1 = V.do(lambda e: e.tensor_tensor(BON, T5, T5, ALU.mult), fr0, t_xout)
            yield
            b, bs, fr = sideb.take()
            t = mm(bs[:, :], k_("bones"), BON, True, True, t1, fr)
            yield
            t1 = V.do(lambda e: e.tensor_scalar(BON, bs[:, :], 1e-24, None, ALU.max), t)
            give(b, t1)
            t1 = A.do(lambda e: e.activation(BON, BON, ACT.Sqrt), t1)
            yield
            yield
            V.do(lambda e: e.reciprocal(BON, BON), t1)
            yield
            V.do(lambda e: e.tensor_tensor(T5, T5, BON, ALU.mult))
            V.do(lambda e: e.scalar_tensor_tensor(ARt[:, :, 0:128], v4(T0), -1.0, v4(T5), ALU.mult, ALU.mult), t_e0)
            yield
            V.do(lambda e: e.tensor_tensor(ARt[:, :, 128:256], v4(T2), v4(r_), ALU.mult))
            V.do(lambda e: e.tensor_scalar(T0, T4, gcol("rw_k_a_2")[:, js], oka[:, js], ALU.mult, ALU.add))
            yield
            V.do(lambda e: e.tensor_tensor(T0, T0, k0_, ALU.mult))
            V.do(lambda e: e.tensor_tensor(T5, T5, T4, ALU.mult))
            yield
            V.do(lambda e: e.tensor_tensor(KH, T0, T3, ALU.mult))
            V.do(lambda e: e.tensor_tensor(BH, T5, T3, ALU.mult))
            yield
            V.do(lambda e: e.tensor_copy(Wc, T2.rearrange("p (c n) -> p c n", n=64)[:, :, 63]))
            t1 = V.do(lambda e: e.scalar_tensor_tensor(T1, r_, gcol("rw_r_k_2")[:, js], T0, ALU.mult, ALU.mult))
            b, bb, fr = sideb.take()
            t = mm(bb[:, :], k_("bones"), T1, True, True, t1, fr)
            yield
            t1 = V.do(lambda e: e.tensor_tensor(BON, bb[:, :], v_, ALU.mult), t)
            give(b, t1)
            ready[j] = t1

        def group_norm(j):
            BON = SETS[j % 2]["BON"]
            js, cs = slice(j, j + 1), slice(j * P, (j + 1) * P)
            b, bk, fr = sideb.take()
            t = mm(bk[:, :], k_("bmean"), y_, True, True, y_done[j], fr)
            yield
            t1 = V.do(lambda e: e.tensor_tensor(yc, y_, bk[:, :], ALU.subtract), t)
            give(b, t1)
            t1 = V.do(lambda e: e.tensor_tensor(q_, yc, yc, ALU.mult))
            b, b2_, fr = sideb.take()
            t = mm(b2_[:, :], k_("bmean"), q_, True, True, t1, fr)
            yield
            t1 = V.do(lambda e: e.tensor_scalar(q_, b2_[:, :], 64e-5, None, ALU.add), t)
            give(b, t1)
            t1 = A.do(lambda e: e.activation(q_, q_, ACT.Sqrt), t1)
            yield
            yield
            V.do(lambda e: e.reciprocal(q_, q_), t1)
            yield
            V.do(lambda e: e.tensor_tensor(yc, yc, q_, ALU.mult))
            V.do(lambda e: e.tensor_scalar(yc, yc, gcol("rw_gn_w_2")[:, js], gcol("rw_gn_b_2")[:, js], ALU.mult, ALU.add))
            b, b3_, fr = sideb.take()
            t = mm(b3_[:, :], gu[:, cs], Z[:, 13, :], True, True, fr)
            yield
            V.do(lambda e: e.tensor_tensor(yc, yc, BON, ALU.add))
            t1 = V.do(lambda e: e.tensor_tensor(Z[:, j, :], yc, b3_[:, :], ALU.mult), t)
            give(b, t1)
            set_free[j % 2] = [t1, t]
            y_done["yr"] = (t, t1)

        def chunks(j):
            D_ = SETS[j % 2]
            ARt, KH, BH, Wc = D_["AR"], D_["KH"], D_["BH"], D_["W"]
            v_ = Z[:, 8 + j, :]
            t_e = ready[j]
            gm = {}
            for it in range(8):
                m, hh, ps = item(it)
                b, bk, fr = mainb.take()
                ms = slice(m * P, (m + 1) * P)
                mm(bk[:, 0:256], BH[ps, ms], ARt[ps, m, :], True, True, t_e, fr, inc=False)
                t = mm(bk[:, 256:512], KH[ps, ms], ARt[ps, m, :], True, True)
                gm[it] = V.free(lambda e, it=it, bk=bk: e.tensor_tensor(GM[:, it, :], bk[:, :], k_("mgram"), ALU.mult), t,
                                chunk_done[0])
                give(b, gm[it])
                if it % 2:
                    yield
            x2 = [None, None]
            tl = {}
            for q in range(2):
                b, bk, fr = mainb.take()
                for r in range(4):
                    m, hh, ps = item(4 * q + r)
                    t = mm(bk[:, r * P:(r + 1) * P], ARt[ps, m, 0:128], BH[ps, m * P:(m + 1) * P], True, True, t_e, fr,
                           inc=(r == 3))
                tl[q] = (b, bk, t)

            def lm(n, x):
                return G.do(lambda e: e.tensor_tensor(LM[x], GM[:, :, 0:128],
                                                      k_(f"up{n}").unsqueeze(1).broadcast_to((P, 8, P)), ALU.mult),
                            gm[7], lm_used[x])

            t_lm = [lm(2, 0), lm(4, 1)]
            for q in range(2):
                b, bk, t = tl[q]
                xs = XX[:, 4 * q:4 * q + 4, 0:128]
                xt_ = XX[:, 4 * q:4 * q + 4, 128:256]
                bc = lambda n: k_(n).unsqueeze(1).broadcast_to((P, 4, P))
                t1 = V.do(lambda e, xs=xs, bk=bk: e.tensor_tensor(xs, v4(bk[:, :]), bc("low1"), ALU.mult), t)
                give(b, t1)
                V.free(lambda e, xt_=xt_, q=q: e.tensor_tensor(xt_, GM[:, 4 * q:4 * q + 4, 0:128], bc("up1"), ALU.mult))
                V.do(lambda e, xs=xs: e.tensor_tensor(xs, xs, bc("ident"), ALU.add))
                x2[q] = V.free(lambda e, xt_=xt_: e.tensor_tensor(xt_, xt_, bc("ident"), ALU.add))
            t_T = []
            for src, dst in ((lambda m: v_[:, m * P:(m + 1) * P], Vt), (lambda m: KH[:, m * P:(m + 1) * P], Kt),
                             (lambda m: BH[:, m * P:(m + 1) * P], Bt), (lambda m: ARt[:, m, 0:128], At)):
                b, bk, fr = mainb.take()
                for m in range(4):
                    t = tr(bk[:, m * P:(m + 1) * P], src(m), t_e, fr, inc=(m == 3))
                t_T.append(A.free(lambda e, dst=dst, bk=bk: e.activation(dst, v4(bk[:, :]), ACT.Copy), t, chunk_done[0]))
                give(b, t_T[-1])
            yield
            b, bk, fr = mainb.take()
            for it in range(8):
                m, hh, ps = item(it)
                t = mm(bk[:, it * 64:it * 64 + 64], GM[:, it, 256:384], Vt[:, m, ps], True, True, t_T, fr, gm[7],
                       inc=(it == 7))
            t_us = A.free(lambda e, bk=bk: e.activation(Us, bk[:, :].rearrange("p (i n) -> p i n", i=8), ACT.Copy), t)
            give(b, t_us)
            t1u = [None, None]
            for lv, n in enumerate((2, 4, 8, 16, 32)):
                x = lv % 2
                tt = [None, None]
                for q in range(2):
                    b, bk, fr = mainb.take()
                    for r in range(4):
                        it = 4 * q + r
                        t = mm(bk[:, r * P:(r + 1) * P], LM[x][:, it, :], XX[:, it, 0:128], True, True, t_lm[x], x2[q], fr,
                               inc=(r == 3))
                    tt[q] = A.free(lambda e, q=q, bk=bk: e.activation(T1b[:, 4 * q:4 * q + 4, :], v4(bk[:, :]), ACT.Copy), t,
                                   t1u[q])
                    give(b, tt[q])
                lm_used[x] = t
                if lv + 2 < 5:
                    t_lm[x] = lm((8, 16, 32)[lv], x)
                yield
                for q in range(4):
                    b, bk, fr = mainb.take()
                    for r in range(2):
                        it = 2 * q + r
                        if n < 32:
                            mm(bk[:, r * 256:r * 256 + 128], XX[:, it, 128:256], T1b[:, it, :], True, True, tt[q // 2], fr,
                               inc=False)
                        t = mm(bk[:, r * 256 + 128:r * 256 + 256], T1b[:, it, :], XX[:, it, 128:256], True, True,
                               tt[q // 2], fr, inc=(r == 1))
                    a0_ = 0 if n < 32 else 128
                    xs = XX[:, 2 * q:2 * q + 2, a0_:256]
                    x2[q // 2] = V.free(lambda e, xs=xs, bk=bk, a0_=a0_: e.tensor_tensor(
                        xs, xs, bk[:, :].rearrange("p (i n) -> p i n", i=2)[:, :, a0_:256], ALU.add), t)
                    give(b, x2[q // 2])
                    t1u[q // 2] = t
                    if q == 1:
                        yield
            t_pp = []
            for q in range(2):
                b, bk, fr = mainb.take()
                for r in range(4):
                    it = 4 * q + r
                    m, hh, ps = item(it)
                    mm(bk[:, r * P:r * P + 64], XX[:, it, 128:256], At[:, m, ps], True, True, x2[q], t_us, fr, inc=False)
                    t = mm(bk[:, r * P + 64:r * P + 128], XX[:, it, 128:256], Us[:, it, :], True, True, inc=(r == 3))
                t_pp.append(A.free(lambda e, q=q, bk=bk: e.activation(PP[:, 4 * q:4 * q + 4, :], v4(bk[:, :]), ACT.Copy), t))
                give(b, t_pp[-1])
            yield
            t_f, t_ec = [], []
            for cc in range(2):
                cr = slice(64 * cc, 64 * cc + 64)
                b, bk, fr = mainb.take()
                for it in range(8):
                    m, hh, ps = item(it)
                    t = mm(bk[ps, m * 64:m * 64 + 64], PP[cr, it, 0:64], Bt[cr, m, ps], True, True, fr, t_pp[hh],
                           inc=(it == 7))
                t_f.append(V.free(lambda e, bk=bk, cc=cc: e.tensor_tensor(
                    by_half(Fm, cc), bk[:, 0:256].rearrange("p (m n) -> p m n", m=4),
                    k_("ident64").unsqueeze(1).broadcast_to((P, 4, 64)), ALU.add), t))
                give(b, t_f[-1])
                b, bk, fr = mainb.take()
                for it in range(8):
                    m, hh, ps = item(it)
                    mm(bk[ps, m * 64:m * 64 + 64], Bt[cr, m, ps], PP[cr, it, 64:128], True, False, fr)
                    t = mm(bk[ps, m * 64:m * 64 + 64], Kt[cr, m, ps], Vt[cr, m, ps], False, True, inc=(it == 7))
                t_ec.append(V.free(lambda e, bk=bk, cc=cc: e.tensor_tensor(
                    by_half(Ec, cc), bk[:, 0:256].rearrange("p (m n) -> p m n", m=4),
                    Wc.rearrange("p (m c) -> p m c", c=2)[:, :, cc:cc + 1].broadcast_to((P, 4, 64)), ALU.mult), t))
                give(b, t_ec[-1])
                yield
            b, bq, fr = mainb.take()
            for it in range(8):
                m, hh, ps = item(it)
                t = mm(bq[ps, m * P:(m + 1) * P], PP[:, it, 0:64], GM[:, it, 128:256], True, True, fr, inc=(it == 7))
            t_q2 = V.free(lambda e, bq=bq: e.tensor_tensor(Q2, v4(bq[:, :]), ARt[:, :, 128:256], ALU.add), t)
            give(b, t_q2)
            ts_ = V.do(lambda e: e.tensor_copy(Sst[:, 64:128], Ec[:, 0:64]))
            for c in range(1, 7):
                b, bk, fr = mainb.take()
                for hh in range(2):
                    ps = slice(64 * hh, 64 * hh + 64)
                    t = mm(bk[ps, 0:64], Fm[ps, c * 64:c * 64 + 64], Sst[ps, c * 64:c * 64 + 64], True, True, t_f, ts_, fr,
                           inc=(hh == 1))
                ts_ = V.do(lambda e, bk=bk, c=c: e.scalar_tensor_tensor(
                    Sst[:, c * 64 + 64:c * 64 + 128], bk[:, 0:64], Wc[:, c:c + 1], Ec[:, c * 64:c * 64 + 64],
                    ALU.mult, ALU.add), t)
                give(b, ts_)
                yield
            b, by, fr = mainb.take()
            for it in range(8):
                m, hh, ps = item(it)
                ms = slice(m * P, (m + 1) * P)
                mm(by[ps, ms], PP[:, it, 64:128], GM[:, it, 128:256], True, False, t_pp, ts_, t_q2, fr)
                t = mm(by[ps, ms], Vt[:, m, ps], GM[:, it, 384:512], False, True, inc=False)
                for cc in range(2):
                    c = 2 * m + cc
                    if c:
                        t = mm(by[ps, c * 64:c * 64 + 64], Sst[ps, c * 64:c * 64 + 64], Q2[ps, m, cc * 64:cc * 64 + 64],
                               False, True, inc=(it == 7))
            t1 = V.do(lambda e, by=by: e.tensor_copy(y_, by[:, :]), t, t_xout)
            give(b, t1)
            y_done[j] = t1
            chunk_done[0] = [t, t1]

        chunk_done, lm_used = [None], [None, None]
        ZI = XC[:, 2560:3586].rearrange("p (b t) -> p b t", t=513)
        for b_ in range(2):
            t_zi = V.do(lambda e, b_=b_: e.memset(ZI[:, b_, 0:1], 0.0), pe.last(), t_xout)
        mu = gcol("rw_mu_2")
        zl = [None, None]
        HH = (k3_(ZH[1]), k3_(ZL[1]))
        first_rows = rows(0)
        for s4, (c0, nc_) in enumerate(((12, 2), (0, 4), (4, 4), (8, 4))):
            s, x, wv, t_w = nxt
            for q in range(nc_):
                if q == (0, 2, 2, 4)[s4]:
                    if s4 == 1:
                        s_misc, slot, t_misc = ring.take()
                        wu, au, gu = slot[0:64, 0:512], slot[64:128, 0:512], slot[:, 512:1024]
                    nxt = take_split(4096)
                c = c0 + q
                b, bk, fr = mainb.take()
                for k in range(8):
                    o_ = (k * nc_ + q) * P
                    t = mm3(bk[:, :], [a[:, o_:o_ + P] for a in wv], [a[:, k, :] for a in HH], k == 0, k == 7,
                            t_w, t_hs[k // 2], fr)
                zi = ZI[:, c % 2, :]
                t1 = A.free(lambda e, zi=zi, bk=bk: e.activation(zi[:, 1:513], bk[:, :], ACT.Copy), t, t_zi, zl[c % 2])
                give(b, t1)
                zc = Z[:, c, :]
                V.do(lambda e, zi=zi, zc=zc: e.tensor_tensor(zc, zi[:, 0:512], zi[:, 1:513], ALU.subtract), t1, pe.last())
                zl[c % 2] = V.do(lambda e, zi=zi, zc=zc, c=c: e.scalar_tensor_tensor(zc, zc, mu[:, c:c + 1], zi[:, 1:513],
                                                                                   ALU.mult, ALU.add))
                if s4 >= 2:
                    for _ in range(s4 - 1):
                        next(first_rows, None)
            done_split(s, x, t)
            if s4 == 0:
                A.do(lambda e: e.activation(Z[0:64, 12, :], Z[0:64, 12, :], ACT.Tanh), V.last())
                t1 = A.do(lambda e: e.activation(Z[:, 13, :], Z[:, 13, :], ACT.Tanh, scale=0.5))
                t_z = V.do(lambda e: e.tensor_scalar(Z[:, 13, :], Z[:, 13, :], 0.5, 0.5, ALU.mult, ALU.add), t1)
        set_free[1] = [t]
        for _ in first_rows:
            pass
        if dump("z", Z, V.last()):
            return finish()

        for j in range(4):

            def side(j=j):
                if j:
                    yield from group_norm(j - 1)
                if j < 3:
                    yield from rows(j + 1)

            other = side()
            for _ in chunks(j):
                next(other, None)
            for _ in other:
                pass
            if dump(f"ys{j}", y_, y_done[j]):
                return finish()
        for _ in group_norm(3):
            pass
        t, t_yr = y_done["yr"]
        ring.done(s_misc, t)
        t_rw = [pe.last(), V.last(), A.last(), G.last()]
        YR = Z[:, 0:4, :]
        if dump("yr", YR, t_yr):
            return finish()

        CK = at(2048, 1152).rearrange("p (i n) -> p i n", i=4)
        CQ = at(3200, 1536).rearrange("p (i n) -> p i n", i=4)
        SC = at(4736, 1536).rearrange("p (i n) -> p i n", i=4)
        KF = at(3200, 3072).rearrange("p (i h d) -> p i h d", i=4, h=8)
        QDT = at(6272, 1536).rearrange("p (k t) -> p k t", k=3)
        KDT = at(7808, 1024).rearrange("p (k t) -> p k t", k=2)
        YMT = at(6272, 2048).rearrange("p (k t) -> p k t", k=4)
        QS = at(8832, 3072).rearrange("p (i h d) -> p i h d", i=4, h=8)
        QTh = at(11904, 2048).rearrange("p (h t) -> p h t", h=4)
        KTh = at(13952, 2048).rearrange("p (h t) -> p h t", h=4)
        VV = at(22016, 2048).rearrange("p (i h d) -> p i h d", i=4, h=8)
        TMP = at(26112, 512)
        pt_at[0] = pt_at[1] = (0, at(24064, 2048).rearrange("p (k n) -> p k n", k=4))
        MT = at(8832, 4096).rearrange("p (k t) -> p k t", k=8)

        ang, nn, cosm, sinm = [TMP[:, 64 * q:64 * q + 64] for q in range(4)]
        ni = TMP[:, 256:320].bitcast(I32)
        a3 = lambda ap: ap.rearrange("p (i c) -> p i c", i=4)
        posf = small(4)
        V.do(lambda e: e.tensor_copy(posf, posi.bitcast(I32)), t_small, t_z)
        V.do(lambda e: e.tensor_tensor(a3(ang), posf.unsqueeze(2).broadcast_to((P, 4, 16)),
                                       k_("invf").unsqueeze(1).broadcast_to((P, 4, 16)), ALU.mult), A.last())
        V.do(lambda e: e.tensor_scalar(nn, ang, float(1 / (2 * np.pi)), None, ALU.mult))
        V.do(lambda e: e.tensor_copy(ni, nn))
        V.do(lambda e: e.tensor_copy(nn, ni))
        c1 = 6.28125
        c2 = float(np.float32(np.round((2 * np.pi - c1) * 2 ** 20) / 2 ** 20))
        c3 = float(2 * np.pi - c1 - c2)
        for c_ in (c1, c2, c3):
            V.do(lambda e, c_=c_: e.scalar_tensor_tensor(ang, nn, -c_, ang, ALU.mult, ALU.add))
        pi_ = 3.1415925
        V.do(lambda e: e.tensor_scalar(ang, ang, pi_, -pi_, ALU.min, ALU.max))
        V.do(lambda e: e.tensor_scalar(nn, ang, -1.0, None, ALU.mult))
        V.do(lambda e: e.tensor_tensor(nn, nn, ang, ALU.max))
        t1 = V.do(lambda e: e.tensor_scalar(nn, nn, -1.0, float(np.pi / 2), ALU.mult, ALU.add))
        A.do(lambda e: e.activation(sinm, ang, ACT.Sin), t1)
        t_cs = A.do(lambda e: e.activation(cosm, nn, ACT.Sin))

        gemm_tok(HT, 8, 384, lambda i, bk, t: evac(CQ[:, i, :], bk[:, 0:384], t, V.last()))
        gemm_tok(HT, 8, 288, lambda i, bk, t: evac(CK[:, i, :], bk[:, 0:288], t))
        t_ck = [A.last(), V.last()]
        GX = both("GX", 0, 4096)
        t_hl = pe.last()
        t_qd, _ = norm_T(lambda i: CQ[:, i, :], NT, 384, lambda i: SC[:, i, :], gcol("mla_g_qa_2"), QDT,
                         lambda i: t_ck, pe.last())
        t_kd, _ = norm_T(lambda i: CK[:, i, 0:256], NT, 256, lambda i: SC[:, i, 0:256], gcol("mla_g_kva_2"), KDT,
                         lambda i: t_ck, pe.last())
        s, slot, t_w = ring.take()
        w = slot_w(768, 0, 3)(slot)
        for i in range(NT):
            for h in range(2):
                b, bk, fr = allb.take()
                for k in range(3):
                    t = mm(bk[:, 0:384], QDT[:, k, i * P:(i + 1) * P], w[:, k, 384 * h:384 * h + 384], k == 0, k == 2,
                           t_w, t_qd, fr)
                give(b, evac(QS[:, i, 4 * h:4 * h + 4, :], bk[:, 0:384].rearrange("p (h d) -> p h d", h=4), t))
        ring.done(s, t)
        s, slot, t_w = ring.take()
        w = slot_w(1024, 0, 2)(slot)
        for i in range(NT):
            for h in range(2):
                b, bk, fr = allb.take()
                for k in range(2):
                    t = mm(bk[:, :], KDT[:, k, i * P:(i + 1) * P], w[:, k, 512 * h:512 * h + 512], k == 0, k == 1,
                           t_w, t_kd, fr)
                b4 = bk[:, :].rearrange("p (h d) -> p h d", h=4)
                A.free(lambda e, b4=b4, i=i, h=h: e.activation(KF[:, i, 4 * h:4 * h + 4, 0:64], b4[:, :, 0:64], ACT.Copy), t)
                give(b, A.free(lambda e, b4=b4, i=i, h=h: e.activation(VV[:, i, 4 * h:4 * h + 4, :], b4[:, :, 64:128], ACT.Copy), t))
        ring.done(s, t)
        t_gh = [split_r([a[:, 1024 * q:1024 * q + 1024] for a in GX], [a[:, 1024 * q:1024 * q + 1024] for a in HT2],
                        lambda ap: ap, t_rw, t_hl) for q in range(4)][-1]
        cb = lambda ap, h: a3(ap).unsqueeze(2).broadcast_to((P, 4, h, 16))
        TV4 = lambda a, h: TMP[:, a:a + 64 * h].rearrange("p (i h c) -> p i h c", i=4, h=h)
        q1, q2 = (HL[1][:, 0:512], HL[0][:, 0:512])
        qv = lambda ap: ap.rearrange("p (i h c) -> p i h c", i=4, h=8)
        t_e1 = [A.last(), V.last(), t_cs]
        rotate(QS[:, :, :, 64:80], QS[:, :, :, 80:96], QS[:, :, :, 64:80], QS[:, :, :, 80:96],
               cb(cosm, 8), cb(sinm, 8), qv(q1), qv(q2), t_e1)
        rotate(CK[:, :, 256:272], CK[:, :, 272:288], CK[:, :, 256:272], CK[:, :, 272:288],
               a3(cosm), a3(sinm), a3(TMP[:, 320:384]), a3(TMP[:, 384:448]))
        t_kf = V.do(lambda e: e.tensor_copy(KF[:, :, :, 64:96],
                                            CK[:, :, 256:288].unsqueeze(2).broadcast_to((P, 4, 8, 32))), t_e1)
        for g in range(2):
            for src, dst in ((QS, QTh), (KF, KTh)):
                for h in range(4):
                    b, bk, fr = allb.take()
                    for i in range(4):
                        t = tr(bk[0:96, i * P:(i + 1) * P], src[:, i, 4 * g + h, :], t_kf, fr, inc=(i == 3))
                    give(b, evac(dst[0:96, h, :], bk[0:96, :], t, pe.last()))
            t_T = [A.last(), V.last()]
            units = []
            for i in range(4):
                n = (i + 1) * P
                units.append(dict(n=n, scale=float(MSCALE), tok=t_T, mask=k_("causal")[:, 512 - n:512], otok=t_kf,
                                  qk=lambda h, i=i, n=n: [(QTh[0:96, h, i * P:(i + 1) * P], KTh[0:96, h, 0:n])],
                                  pv=pv_own([[VV[:, kt, 4 * g + h, :] for kt in range(i + 1)] for h in range(4)]),
                                  o=YMT[:, 2 * g:2 * g + 2, i * P:(i + 1) * P]))
            t_yt = attention(units, allb)
        if dump("yt", YMT, *t_yt):
            return finish()

        SG = at(12928, 2048).rearrange("p (b t) -> p b t", b=4)
        HH = (k3_(GX[1]), k3_(HT2[1]))
        MH, ML = both("MH", U0 + 2048, 4096), both("ML", U0 + 8832, 4096)
        t_att = pe.last()
        nb = ring.take()
        nxt = take_split(4096, t_att)
        for q in range(4):
            (sb_, slb, t_wb), (s, x, wv, t_w) = nb, nxt
            wb = [slot_w(256, 0, 4)(slb), slot_w(256, 1024, 4)(slb)]
            br_b = {}
            for c in range(2):
                for br, (src, tk) in enumerate(((YR, t_yr), (YMT, t_yt))):
                    b, bk2, fr = allb.take()
                    for k in range(4):
                        t = mm(bk2[:, :], wb[br][:, k, c * P:(c + 1) * P], src[:, k, :], k == 0, k == 3, t_wb, tk, fr)
                    br_b[(c, br)] = (b, bk2, t)
            ring.done(sb_, t)
            if q < 3:
                nb = ring.take()
            nxt = take_split(4096)
            for c in range(2):
                f = 2 * q + c
                for br in range(2):
                    b, bk, fr = allb.take()
                    for k in range(8):
                        o_ = br * 2048 + k * 256 + c * P
                        t = mm3(bk[:, :], [a[:, o_:o_ + P] for a in wv], [a[:, k, :] for a in HH], k == 0, k == 7,
                                t_w, t_gh, fr)
                    x_ = 2 * c + br
                    t1 = A.do(lambda e, x_=x_, bk=bk: e.activation(SG[:, x_, :], bk[:, :], ACT.Tanh, scale=0.5), t,
                              V.last(), t_att)
                    give(b, t1)
                    b2_, bk2, t2_ = br_b[(c, br)]
                    give(b2_, V.do(lambda e, x_=x_, bk2=bk2: e.scalar_tensor_tensor(
                        SG[:, x_, :], SG[:, x_, :], 1.0, bk2[:, :], ALU.add, ALU.mult), t1, t2_))
                V.do(lambda e, c=c: e.tensor_tensor(SG[:, 2 * c + 1, :], SG[:, 2 * c, :], SG[:, 2 * c + 1, :], ALU.add))
                V.do(lambda e, c=c, f=f: e.tensor_scalar(MT[:, f, :], SG[:, 2 * c + 1, :], 0.5, None, ALU.mult))
                t_m = split_r([a[:, 512 * f:512 * f + 512] for a in MH], [a[:, 512 * f:512 * f + 512] for a in ML],
                              lambda ap: ap)
            done_split(s, x, t)
        t_xin = x_io.start(SP, X, xs_v, pe.last())
        if dump("mt", MT, t_m):
            return finish()
        HN = [at(25600, 1024), PB2, at(6272, 1024), at(12928, 1024)]
        ms_n, rs_n = NST[nst[0] % 2]
        nst[0] += 1
        hns, fng = [], gcol("ffn_norm_g_2")

        def hn_T(i):
            for k0 in (0, 4):
                b, bk, w = allb.take()
                for k in range(4):
                    t4 = tr(bk[:, k * P:k * P + P], HN[i][:, (k0 + k) * P:(k0 + k + 1) * P], hns[i], w, inc=(k == 3))
                iv = bk[:, :].rearrange("p (k t) -> p k t", k=4)
                gb = fng[:, k0:k0 + 4].unsqueeze(2).broadcast_to((P, 4, P))
                give(b, V.do(lambda e, iv=iv, gb=gb, k0=k0: e.tensor_tensor(HT[:, k0:k0 + 4, i * P:(i + 1) * P], iv, gb,
                                                                          ALU.mult), t4))

        for h in range(2):
            s, x, wv, t_w = nxt
            if h == 0:
                nxt = take_split(4096)
            for i in range(NT):
                b, bk, fr = allb.take()
                for k in range(8):
                    t = mm3(bk[:, :], [k3_(a)[:, k, i * P:(i + 1) * P] for a in (MH[1], ML[1])],
                            [k3_(a)[:, k, :] for a in wv], k == 0, k == 7, t_w, t_m, fr)
                xt = V.do(lambda e, i=i, h=h, bk=bk: e.tensor_tensor(
                    X[:, i, 512 * h:512 * h + 512], X[:, i, 512 * h:512 * h + 512], bk[:, :], ALU.add), t, t_xin)
                give(b, xt)
                if h:
                    t1 = A.do(lambda e, i=i: e.activation(HN[i], X[:, i, :], ACT.Square, scale=1 / 32.0,
                                                          accum_out=ms_n[:, i:i + 1]), xt)
                    if i:
                        hn_T(i - 1)
                    t2 = rsqrt4(rs_n[:, i:i + 1], ms_n[:, i:i + 1], 1, eps6, t1)
                    hns.append(V.do(lambda e, i=i: e.tensor_scalar(HN[i], X[:, i, :], rs_n[:, i:i + 1], None, ALU.mult), t2))
            done_split(s, x, t)
        t_free = [pe.last(), V.last(), A.last()]
        hn_T(NT - 1)
        t_h = V.last()
        if dump("x2", X, t_h):
            return finish()

        d_hn = Dma("s_hn")
        hn_v = hn_scr.rearrange("(i p) d -> p i d", p=P)
        for i in range(NT):
            t_hn = d_hn.start(SP, hn_v[:, i, :], HN[i], hns[i])
        frow = load_row(I["final_norm_g_2"])
        RB = at(22016, 3072)
        rp = [0]

        def rbuf(n):
            rp[0] += n
            assert rp[0] <= 3072
            return RB[:, rp[0] - n:rp[0]]

        LG = rbuf(144).rearrange("p (i n) -> p i n", i=4)
        GL = rbuf(32).rearrange("p (i n) -> p i n", i=4)
        M8 = rbuf(32).rearrange("p (i n) -> p i n", i=4)
        I8 = rbuf(32).rearrange("p (i n) -> p i n", i=4)
        F8 = rbuf(32).rearrange("p (i n) -> p i n", i=4)
        OG = rbuf(16).rearrange("p (i n) -> p i n", i=4)
        OM = rbuf(16).rearrange("p (i n) -> p i n", i=4)
        EG = rbuf(16).rearrange("p (i n) -> p i n", i=4)
        N8 = rbuf(32).rearrange("p (i n) -> p i n", i=4)
        J8 = rbuf(32).rearrange("p (i n) -> p i n", i=4)
        K8 = rbuf(32).rearrange("p (i n) -> p i n", i=4)
        FMk = rbuf(128).rearrange("p (i n) -> p i n", i=4)
        OH = [rbuf(128).rearrange("p (i n) -> p i n", i=4) for _ in range(2)]
        MM_ = rbuf(128).rearrange("p (i n) -> p i n", i=4)
        POS = rbuf(128).rearrange("p (i n) -> p i n", i=4)
        TQ = rbuf(128).rearrange("p (i n) -> p i n", i=4)
        CNT, NBK, END, STA = rbuf(32), rbuf(32), rbuf(32), rbuf(32)
        OHP = [rbuf(128) for _ in range(2)]
        OHB = [rbuf(40) for _ in range(2)]
        EB = rbuf(1248)
        ng, sg, gg, e2, w1, w2, dn = [small(4) for _ in range(7)]
        pq = [[small(4) for _ in range(4)] for _ in range(2)]
        slotu = [small(4), small(4)]
        IDX = small(40)
        ebf, ebi = small(40), small(40)

        b, bk, fr = allb.take()
        for i in range(NT):
            for k in range(8):
                t = mm(bk[:, i * 36:i * 36 + 36], HT[:, k, i * P:(i + 1) * P], rw[:, k, :], k == 0, k == 7, t_h, t_small,
                       fr, inc=(i == 3 and k == 7))
        V.do(lambda e, bk=bk: e.tensor_tensor(LG, bk[:, 0:144].rearrange("p (i n) -> p i n", i=4),
                                              rb.unsqueeze(1).broadcast_to((P, 4, 36)), ALU.add), t)
        give(b, V.last())
        V.do(lambda e: e.memset(GL, 2 * NEG))
        V.do(lambda e: e.tensor_copy(GL[:, :, 0:4], LG[:, :, 0:4]))
        for i in range(NT):
            V.do(lambda e, i=i: e.max(M8[:, i, :], GL[:, i, :]))
            V.do(lambda e, i=i: e.max_index(I8[:, i, :].bitcast(U32), M8[:, i, :], GL[:, i, :]))
        V.do(lambda e: e.tensor_copy(F8, I8.bitcast(U32)))
        t1 = V.do(lambda e: e.tensor_scalar(ng, M8[:, :, 0], -1.0, None, ALU.mult))
        for i in range(NT):
            t2 = A.do(lambda e, i=i: e.activation(EG[:, i, :], LG[:, i, 0:4], ACT.Exp, bias=ng[:, i:i + 1],
                                                  accum_out=sg[:, i:i + 1]), t1)
        V.do(lambda e: e.reciprocal(gg, sg), t2)
        i4 = k_("iota")[:, 0:4].unsqueeze(1).broadcast_to((P, 4, 4))
        V.do(lambda e: e.tensor_tensor(OG, i4, F8[:, :, 0:1].broadcast_to((P, 4, 4)), ALU.is_equal))
        V.do(lambda e: e.tensor_scalar(OM, OG, 1.0, -NEG, ALU.subtract, ALU.mult))
        f4 = lambda ap: ap.rearrange("p i (g n) -> p i g n", g=4)
        gb4 = lambda ap: ap.unsqueeze(3).broadcast_to((P, 4, 4, 8))
        V.do(lambda e: e.tensor_tensor(f4(FMk), f4(LG[:, :, 4:36]), gb4(OG), ALU.mult))
        V.do(lambda e: e.tensor_tensor(f4(FMk), f4(FMk), gb4(OM), ALU.add))
        for i in range(NT):
            V.do(lambda e, i=i: e.max(N8[:, i, :], FMk[:, i, :]))
            V.do(lambda e, i=i: e.max_index(J8[:, i, :].bitcast(U32), N8[:, i, :], FMk[:, i, :]))
        V.do(lambda e: e.tensor_copy(K8, J8.bitcast(U32)))
        t1 = V.do(lambda e: e.tensor_tensor(dn, N8[:, :, 1], N8[:, :, 0], ALU.subtract))
        t1 = A.do(lambda e: e.activation(e2, dn, ACT.Exp), t1)
        V.do(lambda e: e.tensor_scalar(w1, e2, 1.0, None, ALU.add), t1)
        V.do(lambda e: e.reciprocal(w1, w1))
        V.do(lambda e: e.tensor_tensor(w1, w1, gg, ALU.mult))
        V.do(lambda e: e.tensor_tensor(w2, w1, e2, ALU.mult))
        i32_ = k_("iota")[:, 0:32].unsqueeze(1).broadcast_to((P, 4, 32))
        for q in range(2):
            V.do(lambda e, q=q: e.tensor_tensor(OH[q], i32_, K8[:, :, q:q + 1].broadcast_to((P, 4, 32)), ALU.is_equal))
        t1 = V.do(lambda e: e.tensor_tensor(MM_, OH[0], OH[1], ALU.add))
        b, bk, fr = allb.take()
        for i in range(NT):
            for i2 in range(i):
                mm(bk[:, i * 32:i * 32 + 32], k_("ones"), MM_[:, i2, :], i2 == 0, False, t1, fr)
            mm(bk[:, i * 32:i * 32 + 32], k_("triu"), MM_[:, i, :], i == 0, True, t1, fr, inc=False)
        for i in range(NT):
            t = mm(bk[:, 128:160], k_("ones"), MM_[:, i, :], i == 0, i == 3)
        V.do(lambda e, bk=bk: e.tensor_copy(POS, bk[:, 0:128].rearrange("p (i n) -> p i n", i=4)), t)
        V.do(lambda e, bk=bk: e.tensor_copy(CNT, bk[:, 128:160]))
        give(b, V.last())
        V.do(lambda e: e.tensor_scalar(NBK, CNT, 0.0, None, ALU.is_gt))
        for c_ in (128.0, 256.0, 384.0):
            V.do(lambda e, c_=c_: e.scalar_tensor_tensor(NBK, CNT, c_, NBK, ALU.is_gt, ALU.add))
        V.do(lambda e: e.tensor_tensor_scan(END, k_("ones")[:, 0:32], NBK, 0.0, ALU.mult, ALU.add))
        V.do(lambda e: e.tensor_tensor(STA, END, NBK, ALU.subtract))
        EB3 = EB[0:1, :].rearrange("p (b n) -> p b n", b=NB)
        V.do(lambda e: e.tensor_tensor(EB3, END[0:1, :].unsqueeze(1).broadcast_to((1, NB, 32)),
                                       k_("iota")[0:1, 0:NB].unsqueeze(2).broadcast_to((1, NB, 32)), ALU.is_le))
        V.do(lambda e: e.tensor_reduce(ebf[0:1, 0:NB], EB3, AX, ALU.add))
        V.do(lambda e: e.tensor_scalar(ebf[0:1, 0:NB], ebf[0:1, 0:NB], 31.0, None, ALU.min))
        V.do(lambda e: e.tensor_copy(ebi[0:1, NB:NB + 1].bitcast(I32), END[0:1, 31:32]))
        t_eb = V.do(lambda e: e.tensor_copy(ebi[0:1, 0:NB].bitcast(I32), ebf[0:1, 0:NB]))
        for q in range(2):
            ps_, sq_, gq, bq_ = pq[q]
            V.do(lambda e, q=q: e.tensor_tensor(TQ, OH[q], POS, ALU.mult))
            V.do(lambda e, ps_=ps_: e.tensor_reduce(ps_, TQ, AX, ALU.add))
            V.do(lambda e, q=q: e.tensor_tensor(TQ, OH[q], STA.unsqueeze(1).broadcast_to((P, 4, 32)), ALU.mult))
            V.do(lambda e, sq_=sq_: e.tensor_reduce(sq_, TQ, AX, ALU.add))
            V.do(lambda e, gq=gq, ps_=ps_: e.tensor_scalar(gq, ps_, 128.0, None, ALU.is_ge))
            for c_ in (256.0, 384.0):
                V.do(lambda e, c_=c_, gq=gq, ps_=ps_: e.scalar_tensor_tensor(gq, ps_, c_, gq, ALU.is_ge, ALU.add))
            V.do(lambda e, gq=gq, sq_=sq_, bq_=bq_: e.tensor_tensor(bq_, sq_, gq, ALU.add))
            V.do(lambda e, gq=gq, ps_=ps_: e.scalar_tensor_tensor(ps_, gq, -128.0, ps_, ALU.mult, ALU.add))
            V.do(lambda e, gq=gq, bq_=bq_, ps_=ps_: e.scalar_tensor_tensor(gq, bq_, 128.0, ps_, ALU.mult, ALU.add))
            t_slot = V.do(lambda e, gq=gq, q=q: e.tensor_copy(slotu[q].bitcast(U32), gq))
        oh_used = [pe.last(), pe.last()]
        b, bk, fr = allb.take()
        for q in range(2):
            for i in range(NT):
                ps_, sq_, gq, bq_ = pq[q]
                x = i % 2
                V.free(lambda e, x=x, i=i, ps_=ps_: e.tensor_scalar(OHP[x], k_("iota"), ps_[:, i:i + 1], None, ALU.is_equal),
                       t_slot, oh_used[x])
                t1 = V.free(lambda e, x=x, i=i, bq_=bq_: e.tensor_scalar(OHB[x][:, 0:NB], k_("iota")[:, 0:NB], bq_[:, i:i + 1],
                                                                       k_("tokid")[:, i:i + 1], ALU.is_equal, ALU.mult))
                t = mm(bk[:, 0:NB], OHP[x], OHB[x][:, 0:NB], q == 0 and i == 0, q == 1 and i == 3, t1, fr, inc=True)
                oh_used[x] = t
        t_idx = V.do(lambda e, bk=bk: e.tensor_copy(IDX[:, 0:NB].bitcast(U32), bk[:, 0:NB]), t)
        give(b, t_idx)
        if dump("slots", slotu[0].bitcast(F32), t_idx):
            return finish()

        ms_sem = [Dma(f"s_moe{i}") for i in range(4)]
        mslot = [RINGC[:, 0:6144], RINGC[:, 6144:12288], at(4096, 6144), at(10240, 6144)]
        XG = [at(16384 + 1024 * q, 1024) for q in range(3)]
        YB = [at(19456, 1024), at(0, 1024)]
        XTm = [at(1024 + 1024 * q, 1024).rearrange("p (k t) -> p k t", k=8) for q in range(2)]
        ACTB = [at(20480 + 256 * q, 256) for q in range(2)]
        AT_ = [at(20992 + 256 * q, 256).rearrange("p (k t) -> p k t", k=2) for q in range(2)]
        THm = [at(21504 + 256 * q, 256) for q in range(2)]
        gat_sem = [Dma(f"s_gat{i}") for i in range(3)]
        yst_sem = [Dma(f"s_yst{i}") for i in range(2)]
        fg = gcol("ffn_norm_g_2")
        Wgu, Wdn = I["moe_w_gu_2"][0], I["moe_w_down_2"][0]
        before = [pe.last(), V.last(), A.last(), t_hn]
        moe_free = [None] * 4
        down_done, gath_done, ysto = {}, {}, [None, None]
        wl, gl = {}, {}

        def load_w(n):
            x = n % 4
            SP.wait(t_eb, [t_free, t_hn] if n < 4 else None, t_idx if n else None, down_done.get(n - 4))
            ms_sem[x].n += 32
            s = mslot[x]

            def go(e, n=n, x=x, s=s):
                r = e.value_load(ebi[0:1, n:n + 1].bitcast(I32), min_val=0, max_val=31)
                gsrc = Wgu[bass.ds(r, 1), :, :].rearrange("o (k p) n -> p (o k) n", p=P)
                dsrc = Wdn[bass.ds(r, 1), :, :].rearrange("o (k p) n -> p (o k) n", p=P)
                e.dma_start(s[:, 0:4096].rearrange("p (k n) -> p k n", k=8), gsrc).then_inc(ms_sem[x].sem, 16)
                e.dma_start(s[:, 4096:6144].rearrange("p (k n) -> p k n", k=2), dsrc).then_inc(ms_sem[x].sem, 16)

            SP.items.append(go)
            wl[n] = (ms_sem[x].sem, ms_sem[x].n)

        def gather(n):
            x = n % 3
            G.wait(t_hn, t_idx, before if n < 3 else None, gath_done.get(n - 3))
            gat_sem[x].n += 16
            G.items.append(lambda e, n=n, x=x: e.indirect_dma_start(
                XG[x], None, hn_scr, bass.IndirectOffsetOnAxis(ap=IDX[:, n:n + 1].bitcast(U32), axis=0))
                .then_inc(gat_sem[x].sem, 16))
            gl[n] = (gat_sem[x].sem, gat_sem[x].n)

        def x_T(n):
            xg, x = XG[n % 3], XTm[n % 2]
            for hf in range(2):
                b, bk, fr = allb.take()
                for k in range(4):
                    t = tr(bk[:, k * P:(k + 1) * P], xg[:, (4 * hf + k) * P:(4 * hf + k + 1) * P], gl[n], fr, inc=(k == 3))
                t1 = V.free(lambda e, bk=bk, hf=hf, x=x: e.tensor_tensor(
                    x[:, 4 * hf:4 * hf + 4, :], bk[:, :].rearrange("p (k t) -> p k t", k=4),
                    fg[:, 4 * hf:4 * hf + 4].unsqueeze(2).broadcast_to((P, 4, P)), ALU.mult), t, before if n < 2 else None)
                give(b, t1)
            gath_done[n] = t
            return t1

        def up(n, t_x_):
            b, bk, fr = allb.take()
            w = mslot[n % 4][:, 0:4096].rearrange("p (k n) -> p k n", k=8)
            for k in range(8):
                t = mm(bk[:, :], XTm[n % 2][:, k, :], w[:, k, :], k == 0, k == 7, t_x_, wl[n], fr)
            a, th_ = ACTB[n % 2], THm[n % 2]
            t1 = A.free(lambda e: e.activation(th_, bk[:, 0:256], ACT.Tanh, scale=0.5), t, V.last())
            t2 = V.do(lambda e: e.scalar_tensor_tensor(th_, th_, 1.0, bk[:, 0:256], ALU.add, ALU.mult), t1)
            t3 = V.do(lambda e: e.scalar_tensor_tensor(a, th_, 0.5, bk[:, 256:512], ALU.mult, ALU.mult), pe.last())
            give(b, t3)
            return t3

        def down(n, t_a):
            b, bk, fr = allb.take()
            a, aT = ACTB[n % 2], AT_[n % 2]
            for k in range(2):
                t = tr(bk[:, k * P:(k + 1) * P], a[:, k * P:(k + 1) * P], t_a, fr, inc=(k == 1))
            t1 = A.free(lambda e: e.activation(aT, bk[:, 0:256].rearrange("p (k t) -> p k t", k=2), ACT.Copy), t)
            give(b, t1)
            w = mslot[n % 4][:, 4096:6144].rearrange("p (k n) -> p k n", k=2)
            yb = YB[n % 2]
            for h in range(2):
                b, bk2, fr = allb.take()
                for k in range(2):
                    t = mm(bk2[:, :], aT[:, k, :], w[:, k, 512 * h:512 * h + 512], k == 0, k == 1, t1, wl[n], fr)
                if h == 0:
                    t2 = A.free(lambda e, bk2=bk2: e.activation(yb[:, 0:512], bk2[:, :], ACT.Copy), t, ysto[n % 2])
                else:
                    t2 = V.free(lambda e, bk2=bk2: e.tensor_copy(yb[:, 512:1024], bk2[:, :]), t, ysto[n % 2])
                give(b, t2)
            down_done[n] = t
            ysto[n % 2] = yst_sem[n % 2].start(A, y_scr[n * P:(n + 1) * P, :], yb, A.last(), t2)

        def blocks(n0, n1):
            for n in range(n0, min(n0 + 4, n1)):
                load_w(n)
                if n < n0 + 3:
                    gather(n)
            t_a = up(n0, x_T(n0))
            t_x = x_T(n0 + 1)
            for n in range(n0, n1):
                if n + 1 < n1:
                    t_next = up(n + 1, t_x)
                    if n + 3 < n1:
                        gather(n + 3)
                if n + 2 < n1:
                    t_x = x_T(n + 2)
                down(n, t_a)
                if n + 4 < n1:
                    load_w(n + 4)
                t_a = t_next

        blocks(0, 32)
        lanes, count = (pe, V, A, G, SP), ebi[0:1, NB:NB + 1].bitcast(I32)
        y0 = [(d, d.n) for d in yst_sem]
        for q in lanes:
            q.wait(t_eb, t_fill)
            q.part()
        blocks(32, NB)
        for q in lanes:
            q.part_if(count, 32, *(y0 if q is A else ()))

        YG = [at(4096 + 1024 * q, 1024) for q in range(8)]
        y_sem = [Dma(f"s_yg{i}") for i in range(8)]
        tg = {}
        for i in range(NT):
            for q in range(2):
                x = 2 * i + q
                G.wait(ysto, pe.last())
                y_sem[x].n += 16
                G.items.append(lambda e, i=i, q=q, x=x: e.indirect_dma_start(
                    YG[x], None, y_scr, bass.IndirectOffsetOnAxis(ap=slotu[q][:, i:i + 1].bitcast(U32), axis=0))
                    .then_inc(y_sem[x].sem, 16))
                tg[x] = (y_sem[x].sem, y_sem[x].n)
        out_v = out[0].rearrange("(i p) d -> p i d", p=P)
        t_row = frow
        ms, rs = NST[nst[0] % 2]
        for i in range(NT):
            V.do(lambda e, i=i: e.scalar_tensor_tensor(X[:, i, :], YG[2 * i], w1[:, i:i + 1], X[:, i, :], ALU.mult, ALU.add),
                 tg[2 * i])
            t = V.do(lambda e, i=i: e.scalar_tensor_tensor(X[:, i, :], YG[2 * i + 1], w2[:, i:i + 1], X[:, i, :],
                                                           ALU.mult, ALU.add), tg[2 * i + 1])
            t1 = A.do(lambda e, i=i: e.activation(YG[2 * i], X[:, i, :], ACT.Square, scale=1 / 32.0,
                                                  accum_out=ms[:, i:i + 1]), t)
            t2 = rsqrt4(rs[:, i:i + 1], ms[:, i:i + 1], 1, eps6, t1)
            t3 = V.do(lambda e, i=i: e.scalar_tensor_tensor(X[:, i, :], X[:, i, :], rs[:, i:i + 1], ROW,
                                                            ALU.mult, ALU.mult), t2, t_row)
            d = Dma(f"s_out{i}")
            stores.append(d.start(SP, out_v[:, i, :], X[:, i, :], t3))
        return finish()


_INS = ["x", "mem", "mem_norm_g", "w_in", "w_mem_kv", "w_o", "g_mix_pre", "g_mix_post", "attn_sink", "qk_norm_g",
        "w_gate_up", "w_down", "g_ffn_pre", "g_ffn_post", "positions_2", "mix_norm_g_2", "w_in_2", "rw_mu_2",
        "rw_w0_2", "rw_w_up_2", "rw_a0_2", "rw_a_up_2", "rw_g_up_2", "rw_k_k_2", "rw_k_a_2", "rw_r_k_2", "rw_gn_w_2",
        "rw_gn_b_2", "mla_g_qa_2", "mla_w_q_up_2", "mla_g_kva_2", "mla_w_kv_up_2", "w_branch_rw_2",
        "w_branch_mla_2", "w_out_2", "ffn_norm_g_2", "moe_w_group_2", "moe_b_group_2", "moe_w_router_2",
        "moe_b_router_2", "moe_w_gu_2", "moe_w_down_2", "final_norm_g_2"]


def kernel(**inputs):
    import concourse.bacc as bacc
    from concourse.bass_utils import run_bass_kernel_spmd

    nc = bacc.Bacc("TRN2", target_bir_lowering=False, num_devices=1)
    arrays, aps = {}, {}
    for name in _INS:
        a = np.ascontiguousarray(inputs[name])
        arrays[f"in_{name}"] = a
        aps[name] = nc.dram_tensor(f"in_{name}", a.shape, mybir.dt.from_np(a.dtype), kind="ExternalInput").ap()
    table = const_table()
    arrays["tables"] = table
    consts = nc.dram_tensor("tables", table.shape, F32, kind="ExternalInput").ap()
    out = nc.dram_tensor("out_0", (1, S, D), F32, kind="ExternalOutput").ap()
    hn_scr = nc.dram_tensor("hn_scr", (S, D), F32).ap()
    y_scr = nc.dram_tensor("y_scr", (NB * P, D), F32).ap()
    x_scr = nc.dram_tensor("x_scr", (S, D), F32).ap()
    build(nc, aps, out, hn_scr, y_scr, x_scr, consts)
    r = run_bass_kernel_spmd(nc, [arrays], core_ids=[0])
    return r.results[0]["out_0"]
```
